# Optimizing a Trainium2 kernel written in Bass

```python
import jax, jax.numpy as jnp
from jax import lax
import numpy as np

D_MODEL = 1024
BATCH = 1
SEQ = 512
DEPTH = 2

N_MIXERS = 2
N_RET_LAYERS = (DEPTH + 1) // 2
N_GDN_LAYERS = DEPTH // 2

RET_HEADS = 4
RET_QK_DIM = D_MODEL // RET_HEADS
RET_V_DIM = 2 * D_MODEL // RET_HEADS
RET_QK_W = RET_HEADS * RET_QK_DIM
RET_V_W = RET_HEADS * RET_V_DIM
RET_IN_W = 2 * RET_QK_W + 2 * RET_V_W
RET_CHUNK = 128
ROPE_BASE = 10000.0

GDN_HEADS = 8
GDN_K_DIM = D_MODEL // GDN_HEADS
GDN_V_DIM = D_MODEL // GDN_HEADS
GDN_QK_W = GDN_HEADS * GDN_K_DIM
GDN_V_W = GDN_HEADS * GDN_V_DIM
GDN_CONV_CH = 2 * GDN_QK_W + GDN_V_W
GDN_IN_W = GDN_CONV_CH + GDN_V_W + 2 * GDN_HEADS
GDN_CHUNK = 64
CONV_WIDTH = 4

D_FF = 4 * D_MODEL
EPS = 1e-6

kernel_name = "hybrid_retention_gated_deltanet_trunk"

def rms_norm(x, gain):
    xf = x.astype(jnp.float32)
    y = xf * lax.rsqrt(jnp.mean(xf * xf, axis=-1, keepdims=True) + EPS)
    return (y * gain.astype(jnp.float32)).astype(x.dtype)

def rotary(x, pos):
    half = x.shape[-1] // 2
    inv_freq = ROPE_BASE ** (-jnp.arange(half, dtype=jnp.float32) / half)
    ang = pos.astype(jnp.float32)[:, None] * inv_freq[None, :]
    cos = jnp.cos(ang)[None, :, None, :]
    sin = jnp.sin(ang)[None, :, None, :]
    x1, x2 = x[..., :half], x[..., half:]
    return jnp.concatenate([x1 * cos - x2 * sin, x1 * sin + x2 * cos], axis=-1)

def to_chunks(t, c):
    b, T, h, d = t.shape
    return t.reshape(b, T // c, c, h, d).transpose(1, 0, 3, 2, 4)

def from_chunks(t):
    n, b, h, c, d = t.shape
    return t.transpose(1, 0, 3, 2, 4).reshape(b, n * c, h, d)

def retention(h, w_in, gn_gain, w_out):
    b, T, _ = h.shape
    proj = (h @ w_in).astype(jnp.float32)
    q, k, v, g = jnp.split(proj, [RET_QK_W, 2 * RET_QK_W, 2 * RET_QK_W + RET_V_W], axis=-1)
    pos = jnp.arange(T)
    q = rotary(q.reshape(b, T, RET_HEADS, RET_QK_DIM), pos)
    k = rotary(k.reshape(b, T, RET_HEADS, RET_QK_DIM), pos) * (RET_QK_DIM ** -0.5)
    v = v.reshape(b, T, RET_HEADS, RET_V_DIM)

    log_gamma = jnp.log1p(-(2.0 ** (-5.0 - jnp.arange(RET_HEADS, dtype=jnp.float32))))
    idx = jnp.arange(RET_CHUNK, dtype=jnp.float32)
    rel = idx[:, None] - idx[None, :]
    causal = rel >= 0
    intra = jnp.where(causal, jnp.exp(log_gamma[:, None, None] * jnp.where(causal, rel, 0.0)), 0.0)
    q_dec = jnp.exp(log_gamma[:, None] * (idx + 1.0))[..., None]
    k_dec = jnp.exp(log_gamma[:, None] * (RET_CHUNK - 1.0 - idx))[..., None]
    chunk_dec = jnp.exp(log_gamma * RET_CHUNK)[:, None, None]

    def step(S, xs):
        qc, kc, vc = xs
        scores = jnp.einsum('bhcd,bhsd->bhcs', qc, kc) * intra
        out = (jnp.einsum('bhcs,bhse->bhce', scores, vc)
               + jnp.einsum('bhcd,bhde->bhce', qc * q_dec, S))
        S = chunk_dec * S + jnp.einsum('bhsd,bhse->bhde', kc * k_dec, vc)
        return S, out

    S0 = jnp.zeros((b, RET_HEADS, RET_QK_DIM, RET_V_DIM), jnp.float32)
    _, o = lax.scan(step, S0, (to_chunks(q, RET_CHUNK), to_chunks(k, RET_CHUNK), to_chunks(v, RET_CHUNK)))
    o = from_chunks(o)
    mu = jnp.mean(o, axis=-1, keepdims=True)
    var = jnp.mean(jnp.square(o - mu), axis=-1, keepdims=True)
    o = ((o - mu) * lax.rsqrt(var + EPS)).reshape(b, T, RET_V_W) * gn_gain.astype(jnp.float32)
    y = jax.nn.silu(g) * o
    return y.astype(h.dtype) @ w_out

def causal_dwconv(x, w):
    return lax.conv_general_dilated(
        x, w[:, None, :], window_strides=(1,), padding=[(CONV_WIDTH - 1, 0)],
        dimension_numbers=('NWC', 'WIO', 'NWC'), feature_group_count=x.shape[-1])

def l2norm(x):
    return x * lax.rsqrt(jnp.sum(x * x, axis=-1, keepdims=True) + EPS)

def gated_deltanet(h, w_in, conv_w, a_log, dt_bias, norm_gain, w_out):
    b, T, _ = h.shape
    f32 = jnp.float32
    proj = h @ w_in
    qkv, z, beta_raw, a_raw = jnp.split(
        proj, [GDN_CONV_CH, GDN_CONV_CH + GDN_V_W, GDN_CONV_CH + GDN_V_W + GDN_HEADS], axis=-1)
    qkv = jax.nn.silu(causal_dwconv(qkv, conv_w.astype(qkv.dtype))).astype(f32)
    q, k, v = jnp.split(qkv, [GDN_QK_W, 2 * GDN_QK_W], axis=-1)
    q = l2norm(q.reshape(b, T, GDN_HEADS, GDN_K_DIM)) * (GDN_K_DIM ** -0.5)
    k = l2norm(k.reshape(b, T, GDN_HEADS, GDN_K_DIM))
    v = v.reshape(b, T, GDN_HEADS, GDN_V_DIM)
    beta = jax.nn.sigmoid(beta_raw.astype(f32))
    g = -jnp.exp(a_log.astype(f32)) * jax.nn.softplus(a_raw.astype(f32) + dt_bias.astype(f32))

    C = GDN_CHUNK
    qc, kc, vc = to_chunks(q, C), to_chunks(k, C), to_chunks(v, C)
    bc = to_chunks(beta[..., None], C)[..., 0]
    gc = jnp.cumsum(to_chunks(g[..., None], C)[..., 0], axis=-1)
    idx = jnp.arange(C)
    causal = idx[:, None] >= idx[None, :]
    strict = idx[:, None] > idx[None, :]
    diff = gc[..., :, None] - gc[..., None, :]
    decay = jnp.where(causal, jnp.exp(jnp.where(causal, diff, 0.0)), 0.0)

    kb = kc * bc[..., None]
    lower = jnp.where(strict, jnp.einsum('nbhcd,nbhsd->nbhcs', kb, kc) * decay, 0.0)
    a_mat = jnp.eye(C, dtype=f32) + lower
    rhs = jnp.concatenate([vc * bc[..., None], kb * jnp.exp(gc)[..., None]], axis=-1)
    sol = lax.linalg.triangular_solve(a_mat, rhs, left_side=True, lower=True, unit_diagonal=True)
    u, w = sol[..., :GDN_V_DIM], sol[..., GDN_V_DIM:]

    qk = jnp.einsum('nbhcd,nbhsd->nbhcs', qc, kc) * decay
    q_dec = qc * jnp.exp(gc)[..., None]
    g_last = gc[..., -1]
    k_dec = kc * jnp.exp(g_last[..., None] - gc)[..., None]

    def step(S, xs):
        qk_c, q_dec_c, k_dec_c, u_c, w_c, gl = xs
        v_new = u_c - jnp.einsum('bhcd,bhde->bhce', w_c, S)
        out = (jnp.einsum('bhcd,bhde->bhce', q_dec_c, S)
               + jnp.einsum('bhcs,bhse->bhce', qk_c, v_new))
        S = S * jnp.exp(gl)[..., None, None] + jnp.einsum('bhcd,bhce->bhde', k_dec_c, v_new)
        return S, out

    S0 = jnp.zeros((b, GDN_HEADS, GDN_K_DIM, GDN_V_DIM), f32)
    _, o = lax.scan(step, S0, (qk, q_dec, k_dec, u, w, g_last))
    o = from_chunks(o)
    o = o * lax.rsqrt(jnp.mean(o * o, axis=-1, keepdims=True) + EPS) * norm_gain.astype(f32)
    o = o * jax.nn.silu(z.astype(f32).reshape(b, T, GDN_HEADS, GDN_V_DIM))
    return o.reshape(b, T, GDN_V_W).astype(h.dtype) @ w_out

def sq_relu_mlp(h, w_up, w_down):
    return jnp.square(jax.nn.relu(h @ w_up)) @ w_down

def setup_inputs(seed: int = 0) -> dict:
    key = jax.random.key(seed)
    ks = jax.random.split(key, 16)
    nr, nd = N_RET_LAYERS, N_GDN_LAYERS
    nrm = jax.random.normal
    x = nrm(ks[0], (BATCH, SEQ, D_MODEL), jnp.float32)
    norm_gains = 1.0 + 0.02 * nrm(ks[1], (DEPTH, 4, D_MODEL), jnp.float32)
    ret_w_in = nrm(ks[2], (nr, D_MODEL, RET_IN_W), jnp.float32) * D_MODEL ** -0.5
    ret_gn_gain = 1.0 + 0.02 * nrm(ks[3], (nr, RET_V_W), jnp.float32)
    ret_w_out = nrm(ks[4], (nr, RET_V_W, D_MODEL), jnp.float32) * RET_V_W ** -0.5
    gdn_w_in = nrm(ks[5], (nd, D_MODEL, GDN_IN_W), jnp.float32) * D_MODEL ** -0.5
    gdn_conv_w = nrm(ks[6], (nd, CONV_WIDTH, GDN_CONV_CH), jnp.float32) * CONV_WIDTH ** -0.5
    gdn_a_log = jnp.log(jax.random.uniform(ks[7], (nd, GDN_HEADS), jnp.float32, 1.0, 16.0))
    dt = jnp.exp(jax.random.uniform(ks[8], (nd, GDN_HEADS), jnp.float32,
                                    float(np.log(1e-3)), float(np.log(1e-1))))
    gdn_dt_bias = dt + jnp.log(-jnp.expm1(-dt))
    gdn_norm_gain = 1.0 + 0.02 * nrm(ks[9], (nd, GDN_V_DIM), jnp.float32)
    gdn_w_out = nrm(ks[10], (nd, GDN_V_W, D_MODEL), jnp.float32) * GDN_V_W ** -0.5
    mlp_w_up = nrm(ks[11], (DEPTH, D_MODEL, D_FF), jnp.float32) * D_MODEL ** -0.5
    mlp_w_down = nrm(ks[12], (DEPTH, D_FF, D_MODEL), jnp.float32) * D_FF ** -0.5
    return {"x": x, "norm_gains": norm_gains,
            "ret_w_in": ret_w_in, "ret_gn_gain": ret_gn_gain, "ret_w_out": ret_w_out,
            "gdn_w_in": gdn_w_in, "gdn_conv_w": gdn_conv_w, "gdn_a_log": gdn_a_log,
            "gdn_dt_bias": gdn_dt_bias, "gdn_norm_gain": gdn_norm_gain, "gdn_w_out": gdn_w_out,
            "mlp_w_up": mlp_w_up, "mlp_w_down": mlp_w_down}

def reference(x, norm_gains, ret_w_in, ret_gn_gain, ret_w_out, gdn_w_in, gdn_conv_w, gdn_a_log,
              gdn_dt_bias, gdn_norm_gain, gdn_w_out, mlp_w_up, mlp_w_down):
    h = x
    for i in range(DEPTH):
        gains = norm_gains[i]
        j = i // N_MIXERS
        hn = rms_norm(h, gains[0])
        if i % N_MIXERS == 0:
            mix = retention(hn, ret_w_in[j], ret_gn_gain[j], ret_w_out[j])
        else:
            mix = gated_deltanet(hn, gdn_w_in[j], gdn_conv_w[j], gdn_a_log[j], gdn_dt_bias[j],
                                 gdn_norm_gain[j], gdn_w_out[j])
        h = h + rms_norm(mix, gains[1])
        ff = sq_relu_mlp(rms_norm(h, gains[2]), mlp_w_up[i], mlp_w_down[i])
        h = h + rms_norm(ff, gains[3])
    return h


_drawn_inputs = setup_inputs


def setup_inputs(seed=0):
    import zlib

    import numpy as np

    out = dict(_drawn_inputs(seed))
    spreads = {}
    factors = {}
    for name, (base, spread) in spreads.items():
        noise = np.random.default_rng([zlib.crc32(name.encode()), seed]).standard_normal(out[name].shape)
        drawn = base * np.exp(spread * noise) if base else spread * noise
        out[name] = __import__('jax').numpy.asarray(drawn.astype(out[name].dtype))
    for name, factor in factors.items():
        out[name] = (out[name] * factor).astype(out[name].dtype)
    return out
```

```python
from contextlib import ExitStack

import numpy as np

import concourse.bass as bass
from concourse import mybir

F32 = mybir.dt.float32
F32R = mybir.dt.float32r
U8 = mybir.dt.uint8
BF16 = mybir.dt.bfloat16
ALU = mybir.AluOpType
ACT = mybir.ActivationFunctionType
AX = mybir.AxisListType

P = 128
D = 1024
T = 512
KT = D // P
TT = T // P
FF = 4 * D
EPS = 1e-6
RH, RQK, RV = 4, D // 4, 2 * D // 4
RET_IN = 2 * D + 2 * 2 * D
VT = 2 * D // P
GH = 8
GDN_CONV = 3 * D
GDN_IN = 4 * D + 2 * GH
CONV = 4
UNITS = GH * TT
LEVELS = [1 << n for n in range(7)]

CK = 4
GC = 512
HALF_TILES = FF // 2 // P


def shape_constants():
    half = RQK // 2
    inv_freq = (np.float32(10000.0) ** (-np.arange(half, dtype=np.float32) / np.float32(half))).astype(np.float32)
    angle = (np.arange(T, dtype=np.float32)[None, :] * inv_freq[:, None]).astype(np.float32)
    rope = np.stack([np.cos(angle), np.sin(angle)], axis=1).astype(np.float32)
    gap = np.arange(T)[None, :] - np.arange(P)[:, None]
    log_gamma = np.log1p(-(2.0 ** (-5.0 - np.arange(RH, dtype=np.float64))))
    decay = np.where(gap[:, None, :] >= 0, np.exp(log_gamma[None, :, None] * np.maximum(gap, 0)[:, None, :]), 0.0)
    decay = (decay * RQK ** -0.5).astype(np.float32)
    row, col = np.arange(P)[:, None], np.arange(P)[None, :]
    square = np.stack([
        (row == col), (row <= col), np.ones((P, P)), np.where(row <= col, 0.0, -1e30),
    ], axis=1).astype(np.float32)
    lower = np.stack([(row // (2 * b) == col // (2 * b)) & (row // b % 2 == 1) & (col // b % 2 == 0)
                      for b in LEVELS], axis=1)
    join = np.stack([lower, lower.transpose(2, 1, 0)], axis=1).astype(np.float32)
    return {"rope": rope, "decay": decay, "square": square, "join": join}


class Plan:

    def __init__(self, nc):
        self.nc = nc
        self.at = (nc.sbuf_base + 63) // 64 * 64

    def place(self, size):
        at, self.at = self.at, self.at + (size + 31) // 32 * 32
        assert self.at <= self.nc.sbuf_usable_end, (self.at, self.nc.sbuf_usable_end)
        return at

    def tile(self, name, shape, dtype, at=None):
        size = int(np.prod(shape[1:])) * {U8: 1, BF16: 2}.get(dtype, 4)
        if at is None:
            at = self.place(size)
        return self.nc.alloc_sbuf_tensor_at(name, list(shape), dtype, offset=at)


def hybrid_trunk(nc, x, norm_gains, ret_w_in, ret_gn_gain, ret_w_out, gdn_w_in, gdn_conv_w, gdn_a_log,
                 gdn_dt_bias, gdn_norm_gain, gdn_w_out, mlp_w_up, mlp_w_down, rope_c, decay_c, square_c,
                 join_c, out):
    plan = Plan(nc)
    KB = 1024
    resid = plan.tile("resid", [P, TT, D], F32)
    act_at = plan.place(32 * KB)
    act_hi = plan.tile("act_hi", [P, KT, T], F32R, act_at)
    act_lo = plan.tile("act_lo", [P, KT, T], F32R, act_at + 16 * KB)
    w_raw = plan.tile("w_raw", [P, 2, CK, GC], F32)
    w_hi = plan.tile("w_hi", [P, 2, CK, GC], F32R)
    w_lo = plan.tile("w_lo", [P, 2, CK, GC], F32R)
    gains_at = plan.place(8 * KB)
    gains = plan.tile("gains", [P, 2, D], F32, gains_at)
    square = plan.tile("square", [P, 4, P], F32)
    ident, tri, ones, neg = (square[:, n, :] for n in range(4))
    dump_at = plan.place(2 * KB)
    dump = plan.tile("dump", [P, D], BF16, dump_at)
    stat = plan.tile("stat", [P, 10, TT], F32)
    SS_MIX, ROOT_MIX, SS_RES, ROOT_RES, NEWTON, RSTD_MIX, RSTD_RES, EPS_COL = 0, 1, 2, 3, 4, 7, 8, 9
    eps = stat[:, EPS_COL, 0:1]
    big_at = plan.place(0)

    def big(name, shape, dtype, kb):
        made = plan.tile(name, shape, dtype, big_at + int(kb * KB))
        return made

    normed = big("normed", [P, 2, D], F32, 64)
    mix = big("mix", [P, TT, D], F32, 80)
    qk_t = big("qk_t", [P, 2 * KT, T], F32, 0)
    v_tm = big("v_tm", [P, TT, 2 * D], F32, 32)
    gate = big("gate", [P, TT, 2 * D], F32, 64)
    rope_tmp = big("rope_tmp", [P, 4, T], F32, 64)
    rope = big("rope", [P, 2, T], F32, 72)
    score = plan.tile("score", [P, 2, TT, T], F32, act_at)
    decay = plan.tile("decay", [P, RH, T], F32, act_at + 16 * KB)
    bn = plan.tile("bn", [P, RH * TT, 16], F32, act_at + 24 * KB)
    BN_MEAN, BN_VAR, BN_ROOT, BN_NEWTON, BN_RSTD = 6, 7, 8, 9, 12
    y_hi = big("y_hi", [P, VT, T], F32R, 0)
    y_lo = big("y_lo", [P, VT, T], F32R, 32)
    hid_hi = big("hid_hi", [P, HALF_TILES, T], F32R, 0)
    hid_lo = big("hid_lo", [P, HALF_TILES, T], F32R, 32)
    relu = big("relu", [P, 4, T], F32, 64)
    relu_sq = big("relu_sq", [P, 4, T], F32, 72)
    mix_b = big("mix_b", [P, TT, GC], F32, 72)
    gk = big("gk", [P, GH, T], F32, 0)
    gv = big("gv", [P, GH, T], F32, 16)
    gq = big("gq", [P, GH, T], F32, 32)
    gz = big("gz", [P, TT, D], F32, 48)
    attn = big("attn", [P, UNITS, P], F32, 64)
    inv_t = big("inv_t", [P, UNITS, P], F32, 80)
    pad = big("pad", [P, 2, 4, CONV - 1 + T + 1], F32, 64)
    ba_hi = big("ba_hi", [P, KT, P], F32R, 32)
    ba_lo = big("ba_lo", [P, KT, P], F32R, 36)
    ba_raw = big("ba_raw", [P, KT, 2 * GH], F32, 98)
    ba_t = big("ba_t", [P, T], F32, 84)
    ba_cols = big("ba_cols", [P, TT, 2 * GH], F32, 86)
    conv_rows = big("conv_rows", [CONV * 3 * KT, P], F32, 87)
    conv_w = big("conv_w", [P, CONV, 3 * KT], F32, 88)
    z_gain = big("z_gain", [P, P], F32, 89)
    head_rows = big("head_rows", [P, 4, GH], F32, 90)
    ct = big("ct", [P, 16, UNITS], F32, 91)
    join_f = big("join_f", [P, 2, len(LEVELS), P], F32, 40)
    join = big("join", [P, 2, len(LEVELS), P], U8, 96)
    col = big("col", [P, 13, UNITS], F32, 97.75)
    (BETA, G, GCUM, EXP_G, EXP_TOT, EXP_REST, SS_K, SS_Q, R_K, N_K, R_Q, S_U, S_V) = range(13)
    neg_l_t = plan.tile("neg_l_t", [P, UNITS, P], F32, act_at)
    inv = plan.tile("inv", [P, UNITS // 2, P], F32, act_at + 16 * KB)
    half_prod = plan.tile("half_prod", [P, UNITS // 2, P], F32, act_at + 24 * KB)
    k_grown = plan.tile("k_grown", [P, UNITS // 2, P], F32, act_at + 24 * KB)
    w_t = plan.tile("w_t", [P, UNITS, P], F32, act_at)
    state = plan.tile("state", [P, GH, P], F32, act_at + 16 * KB)
    o_sq = plan.tile("o_sq", [P, GH, P], F32, act_at + 20 * KB)
    v_new = plan.tile("v_new", [P, GH, P], F32, act_at + 24 * KB)
    tmp = plan.tile("tmp", [P, 4, T], F32, gains_at)
    on = plan.tile("on", [P, TT, 6, GH], F32, dump_at)
    tall = lambda b: b[:, :].rearrange("p (k t) -> p k t", k=4)

    count = [0, 0, 0]

    def take(groups, chunks):
        was = tuple(count)
        for n, more in enumerate((groups, groups * chunks, groups * (chunks - 1))):
            count[n] += more
        return was

    def take_mlp():
        return [(take(4, 2), take(2, 4)) for _ in range(2)]

    RET_QK, RET_V, RET_G, RET_OUT = take(4, 2), take(4, 2), take(4, 2), take(2, 4)
    MLP = [take_mlp()]
    GDN_K, GDN_V, GDN_Q, GDN_Z, GDN_OUT = (take(2, 2) for _ in range(5))
    MLP.append(take_mlp())
    CHUNKS = count[1]
    NEXT_GROUP = [0, MLP[0][0][0][0], GDN_K[0], MLP[1][0][0][0], count[0]]
    GAIN_ROWS = [(None, (0, 0)), ((0, 1), (0, 2)), ((0, 3), (1, 0)), ((1, 1), (1, 2)), ((1, 3), None)]
    GAINS_LANDED = [16, 48, 80, 112, 128]

    with ExitStack() as ctx:
        bank = [ctx.enter_context(nc.psum_tensor(f"bank{n}", [P, T], F32)) for n in range(8)]
        sems = {}

        def sem(name):
            if name not in sems:
                sems[name] = ctx.enter_context(nc.semaphore(name))
            return sems[name]

        class Chain:

            def __init__(self, eng, name):
                self.eng, self.sem, self.n = eng, sem(name), 0

            def link(self, ins):
                self.n += 1
                ins.then_inc(self.sem, 1)
                self.eng.wait_ge(self.sem, self.n)

        w_landed = [sem("w_landed0"), sem("w_landed1")]
        w_high = sem("w_high")
        w_ready = sem("w_ready")
        chunk_used = sem("chunk_used")
        bank_full = sem("bank_full")
        emptied = sem("emptied")

        block = ctx.enter_context(nc.Block())

        @block.sync
        def _(sp):
            def stream(start, groups, w, chunks, col0=0):
                c0 = start[1]
                rows = w.rearrange("(k p) n -> p k n", p=P)

                def load(g, j, cols):
                    if c0 or not isinstance(g, int):
                        sp.wait_ge(w_ready, g * chunks + (c0 + j - 1))
                    sp.dma_start(w_raw[:, j % 2, :, :], rows[:, j * CK:(j + 1) * CK, cols])\
                        .then_inc(w_landed[j % 2], 16)

                if c0 == 0:
                    for j in range(2):
                        load(0, j, slice(col0, col0 + GC))
                with sp.Fori(0 if c0 else 1, groups) as g:
                    cols = bass.ds(sp.snap(g * GC + col0), GC)
                    for j in range(chunks):
                        load(g, j, cols)

            def stream_mlp(layer):
                for half, (up, down) in enumerate(MLP[layer]):
                    stream(up, 4, mlp_w_up[layer], 2, half * FF // 2)
                    stream(down, 2, mlp_w_down[layer, half * FF // 2:(half + 1) * FF // 2, :], 4)

            stream(RET_QK, 12, ret_w_in[0], 2)
            stream(RET_OUT, 2, ret_w_out[0], 4)
            sp.dma_start(ba_raw[:, :, :], gdn_w_in[0].rearrange("(k p) n -> p k n", p=P)[:, :, 4 * D:GDN_IN])\
                .then_inc(sem("ba_landed"), 16)
            stream_mlp(0)
            for start, first in ((GDN_K, D), (GDN_V, 2 * D), (GDN_Q, 0), (GDN_Z, 3 * D)):
                stream(start, 2, gdn_w_in[0], 2, first)
            stream(GDN_OUT, 2, gdn_w_out[0], 2)
            stream_mlp(1)

        @block.gpsimd
        def _(pool):
            def low_parts(first, last):
                with pool.Fori(first // 2, last // 2) as i:
                    for s in range(2):
                        pool.wait_ge(w_high, i * 2 + (s + 1))
                        nc.gpsimd.tensor_tensor(w_lo[:, s, :, :], w_raw[:, s, :, :], w_hi[:, s, :, :].bitcast(F32),
                                                ALU.subtract).then_inc(w_ready, 1)

            low_parts(0, GDN_OUT[1])
            pool.wait_ge(w_high, GDN_OUT[1] + 1)
            nc.gpsimd.tensor_tensor(w_lo[:, 0, :, :], w_raw[:, 0, :, :], w_hi[:, 0, :, :].bitcast(F32),
                                    ALU.subtract).then_inc(w_ready, 1)
            for h in range(GH):
                pool.wait_ge(sem("row_exped"), h + 1)
                pool.wait_ge(sem("unit_prods"), h + 1)
                nc.gpsimd.tensor_tensor(gq[:, h, :], gq[:, h, :], tmp[:, 2 + h % 2, :], ALU.mult)\
                    .then_inc(sem("q_grown"), 1)
            units = gv[:, :, :].rearrange("p h (n e) -> p h n e", n=TT)
            for n in range(TT):
                pool.wait_ge(sem("o_scaled"), n + 1)
                nc.gpsimd.tensor_tensor(units[:, :, n, :], units[:, :, n, :],
                                        gz[:, n, :].rearrange("p (h e) -> p h e", h=GH), ALU.mult)\
                    .then_inc(sem("o_gated"), 1)
            pool.wait_ge(w_high, GDN_OUT[1] + 2)
            nc.gpsimd.tensor_tensor(w_lo[:, 1, :, :], w_raw[:, 1, :, :], w_hi[:, 1, :, :].bitcast(F32),
                                    ALU.subtract).then_inc(w_ready, 1)
            low_parts(GDN_OUT[1] + 2, CHUNKS)

        @block.tensor
        def _(pe):
            def three(dst, sta_hi, sta_lo, mov_hi, mov_lo, first, last):
                pe.matmul(dst, sta_hi, mov_hi, start=first, stop=False)
                pe.matmul(dst, sta_hi, mov_lo, start=False, stop=False)
                return pe.matmul(dst, sta_lo, mov_hi, start=False, stop=last)

            def group(c, parity, chunks, features_out, a_hi, a_lo):
                for j in range(chunks):
                    pe.wait_ge(w_ready, c + (j + 1))
                    s = j % 2
                    for m in range(4):
                        dst, mm = bank[4 * parity + m][:, :], slice(m * P, (m + 1) * P)
                        for kt in range(CK):
                            k = j * CK + kt
                            ends = (k == 0, k == chunks * CK - 1)
                            if features_out:
                                done = three(dst, w_hi[:, s, kt, mm], w_lo[:, s, kt, mm],
                                             a_hi[:, k, :], a_lo[:, k, :], *ends)
                            else:
                                done = three(dst, a_hi[:, k, mm], a_lo[:, k, mm],
                                             w_hi[:, s, kt, :], w_lo[:, s, kt, :], *ends)
                        if j == chunks - 1:
                            done.then_inc(bank_full, 1)
                    if j < chunks - 1:
                        done.then_inc(chunk_used, 1)

            def groups(start, n, chunks, features_out, a_hi, a_lo):
                g0, c0, _ = start
                if g0:
                    pe.wait_ge(emptied, 4 * (g0 - 1))

                def pair(i):
                    group(i * (2 * chunks) + c0, 0, chunks, features_out, a_hi, a_lo)
                    if g0 or i:
                        pe.wait_ge(emptied, i * 8 + 4 * g0)
                    group(i * (2 * chunks) + (c0 + chunks), 1, chunks, features_out, a_hi, a_lo)

                if n == 2 or not g0:
                    for i in range(n // 2):
                        if i:
                            pe.wait_ge(emptied, i * 8 + 4 * (g0 - 1))
                        pair(i)
                    return
                with pe.Fori(0, n // 2) as i:
                    pair(i)
                    pe.wait_ge(emptied, i * 8 + 4 * (g0 + 1))

            def transpose_acts(b):
                if b:
                    pe.wait_ge(emptied, 4 * (NEXT_GROUP[b] - 1))
                for m in range(TT):
                    pe.wait_ge(sem("normed"), TT * b + m + 1)
                    if m >= 2:
                        pe.wait_ge(sem("act_low"), 2 * (TT * b + m - 1))
                    for k in range(KT):
                        done = pe.transpose(bank[2 * (m % 2) + k // 4][:, k % 4 * P:(k % 4 + 1) * P],
                                            normed[:, m % 2, k * P:(k + 1) * P], ident)
                    done.then_inc(sem("acts_transposed"), 1)
                pe.wait_ge(sem("act_low"), 2 * TT * (b + 1))

            def retention():
                pe.wait_ge(emptied, 4 * RET_OUT[0])
                pe.wait_ge(sem("roped"), KT)

                def scores(h):
                    if h:
                        pe.wait_ge(sem("decayed"), TT * h)
                    for i in range(TT):
                        for d in range(2):
                            done = pe.matmul(bank[i][:, 0:T - i * P], qk_t[:, KT + 2 * h + d, i * P:(i + 1) * P],
                                             qk_t[:, 2 * h + d, i * P:T], start=d == 0, stop=d == 1)
                        done.then_inc(sem("scored"), 1)

                scores(0)
                for h in range(RH):
                    if h + 1 < RH:
                        scores(h + 1)
                    else:
                        pe.wait_ge(sem("decayed"), TT * RH)
                    for j in range(TT):
                        if h:
                            pe.wait_ge(sem("y_gated"), TT * (h - 1) + j + 1)
                        for i in range(j + 1):
                            done = pe.matmul(bank[4 + j][:, :], score[:, h % 2, i, j * P:(j + 1) * P],
                                             v_tm[:, i, h * RV:(h + 1) * RV], start=i == 0, stop=i == j)
                        done.then_inc(sem("attended"), 1)
                for n in range(RH * TT):
                    h, m = n // TT, n % TT
                    pe.wait_ge(sem("y_scaled"), n + 1)
                    pe.wait_ge(sem("y_gated"), min(n + 9, RH * TT) if n < 8 else RH * TT)
                    if n >= 8:
                        pe.wait_ge(sem("y_low"), n - 7)
                    for f in range(4):
                        done = pe.transpose(bank[n % 8][:, f * P:(f + 1) * P],
                                            gate[:, m, h * RV + f * P:h * RV + (f + 1) * P], ident)
                    done.then_inc(sem("y_transposed"), 1)
                pe.wait_ge(sem("y_low"), RH * TT)

            def mlp(layer):
                for half, (up, down) in enumerate(MLP[layer]):
                    groups(up, 4, 2, True, act_hi, act_lo)
                    pe.wait_ge(sem("hid_low"), HALF_TILES * (2 * layer + half + 1))
                    groups(down, 2, 4, False, hid_hi, hid_lo)

            def delta_projections():
                g0, c0, _ = GDN_K
                pe.wait_ge(emptied, 4 * g0)
                pe.wait_ge(sem("ba_low"), 1)
                for k in range(KT):
                    done = three(bank[4][:, :], ba_hi[:, k, :], ba_lo[:, k, :], act_hi[:, k, :], act_lo[:, k, :],
                                 k == 0, k == KT - 1)
                done.then_inc(sem("ba_full"), 1)
                group(c0, 0, 2, True, act_hi, act_lo)
                pe.wait_ge(sem("ba_out"), 1)
                pe.wait_ge(sem("conv_rows_landed"), 16)
                for n in range(TT):
                    pe.transpose(bank[5][:, n * P:(n + 1) * P], ba_t[:, n * P:(n + 1) * P], ident)
                rows = CONV * 3 * KT
                pe.transpose(bank[6][:, 0:rows], conv_rows[:, :], ident[0:rows, 0:rows]).then_inc(sem("small_turned"), 1)
                pe.wait_ge(sem("small_out"), 2)
                group(c0 + 2, 1, 2, True, act_hi, act_lo)
                groups(GDN_V, 2, 2, True, act_hi, act_lo)
                groups(GDN_Q, 2, 2, True, act_hi, act_lo)
                groups(GDN_Z, 2, 2, False, act_hi, act_lo)

            def unit(t, u):
                return t[:, u // TT, u % TT * P:(u % TT + 1) * P]

            def delta_rule():
                pe.wait_ge(emptied, 4 * GDN_OUT[0])
                pe.wait_ge(sem("silued"), 3 * GH)
                pe.wait_ge(sem("g_made"), 1)
                pe.matmul(bank[7][:, 0:UNITS], tri, col[:, G, :], start=True, stop=True)
                pe.matmul(bank[7][:, UNITS:2 * UNITS], ones, col[:, G, :], start=True, stop=True)\
                    .then_inc(sem("g_summed"), 1)
                for i in range(2 * GH):
                    src, h = (gk, gq)[i // GH], i % GH
                    if i == 7:
                        pe.wait_ge(sem("g_sums_read"), 2)
                    if i >= 8:
                        pe.wait_ge(sem("kq_squared"), i - 7)
                    for n in range(TT):
                        done = pe.transpose(bank[i % 8][:, n * P:(n + 1) * P], src[:, h, n * P:(n + 1) * P], ident)
                    done.then_inc(sem("kq_turned"), 1)
                pe.wait_ge(sem("kq_squared"), 2 * GH)
                for h in range(GH):
                    if h >= 2:
                        pe.wait_ge(sem("row_exped"), h - 1)
                        pe.wait_ge(sem("row_shifted"), h - 1)
                    for n in range(TT):
                        g = col[:, G, h * TT + n:h * TT + n + 1].broadcast_to([P, P])
                        done = pe.matmul(bank[4 + h % 2][:, n * P:(n + 1) * P], g, tri, start=True, stop=True)
                    done.then_inc(sem("row_made"), 1)
                    if h >= 2:
                        pe.wait_ge(sem("unit_scaled"), h - 1)
                    for first, other in ((0, gk), (2, gq)):
                        for n in range(TT):
                            done = pe.matmul(bank[first + h % 2][:, n * P:(n + 1) * P], gk[:, h, n * P:(n + 1) * P],
                                             other[:, h, n * P:(n + 1) * P], start=True, stop=True)
                    done.then_inc(sem("unit_prods"), 1)
                    if h:
                        pe.wait_ge(sem("k_turned_out"), h)
                        pe.wait_ge(sem("v_turned_out"), h)
                    for b, src in ((6, gk), (7, gv)):
                        for n in range(TT):
                            done = pe.transpose(bank[b][:, n * P:(n + 1) * P], src[:, h, n * P:(n + 1) * P], ident)
                    done.then_inc(sem("kv_turned"), 1)
                pe.wait_ge(sem("unit_scaled"), GH)
                pe.wait_ge(sem("v_turned_out"), GH)
                pe.wait_ge(sem("k_turned_out"), GH)
                n_p = n_second = 0
                for batch in range(2):
                    heads = range(4 * batch, 4 * batch + 4)
                    for r, h in enumerate(heads):
                        pe.wait_ge(sem("inv_seeded"), h + 1)
                        for n in range(TT):
                            done = pe.transpose(bank[r][:, n * P:(n + 1) * P], inv_t[:, h * TT + n, :], ident)
                        done.then_inc(sem("inv_turned"), 1)
                    for level in range(1, len(LEVELS)):
                        for r, h in enumerate(heads):
                            if level == 1:
                                pe.wait_ge(sem("inv_placed"), h + 1)
                            else:
                                pe.wait_ge(sem("joined"), n_second - 4 + r + 1)
                            for n in range(TT):
                                u = h * TT + n
                                done = pe.matmul(bank[r][:, n * P:(n + 1) * P], neg_l_t[:, u, :],
                                                 inv[:, u - batch * UNITS // 2, :], start=True, stop=True)
                            done.then_inc(sem("prod_made"), 1)
                        for r, h in enumerate(heads):
                            n_p += 1
                            pe.wait_ge(sem("prod_out"), n_p)
                            if n_second >= 2:
                                pe.wait_ge(sem("joined"), n_second - 1)
                            for n in range(TT):
                                u = h * TT + n
                                v = u - batch * UNITS // 2
                                cols = slice(n * P, (n + 1) * P)
                                if level < len(LEVELS) - 1:
                                    pe.matmul(bank[4 + r % 2 * 2][:, cols], inv_t[:, u, :], half_prod[:, v, :],
                                              start=True, stop=True)
                                done = pe.matmul(bank[5 + r % 2 * 2][:, cols], half_prod[:, v, :], inv_t[:, u, :],
                                                 start=True, stop=True)
                            done.then_inc(sem("seconds_made"), 1)
                            n_second += 1
                    for r, h in enumerate(heads):
                        pe.wait_ge(sem("k_grown"), h + 1)
                        pe.wait_ge(sem("joined"), n_second - 4 + r + 1)
                        for n in range(TT):
                            u = h * TT + n
                            done = pe.matmul(bank[r][:, n * P:(n + 1) * P], k_grown[:, u - batch * UNITS // 2, :],
                                             inv_t[:, u, :], start=True, stop=True)
                        done.then_inc(sem("w_made"), 1)
                    for r, h in enumerate(heads):
                        pe.wait_ge(sem("w_out"), h + 1)
                for n in range(TT):
                    for q in range(2):
                        if n:
                            pe.wait_ge(sem("state_made"), 2 * (n - 1) + q + 1)
                            pe.wait_ge(sem("v_new_made"), 2 * (n - 1) + q + 1)
                        for r in range(4):
                            h = 4 * q + r
                            u = h * TT + n
                            cols = slice(r * P, (r + 1) * P)
                            done = pe.matmul(bank[q][:, cols], inv_t[:, u, :], unit(gv, u), start=True, stop=n == 0)
                            if n:
                                done = pe.matmul(bank[q][:, cols], w_t[:, u, :], state[:, h, :], start=False, stop=True)
                        done.then_inc(sem("v_new_full"), 1)
                    for q in range(2):
                        pe.wait_ge(sem("v_new_made"), 2 * n + q + 1)
                        if n:
                            pe.wait_ge(sem("o_out"), 2 * (n - 1) + q + 1)
                        else:
                            pe.wait_ge(sem("q_grown"), GH)
                        for r in range(4):
                            h = 4 * q + r
                            u = h * TT + n
                            cols = slice(r * P, (r + 1) * P)
                            if n:
                                pe.matmul(bank[2 + q][:, cols], unit(gq, u), state[:, h, :], start=True, stop=False)
                            done = pe.matmul(bank[2 + q][:, cols], attn[:, u, :], v_new[:, h, :],
                                             start=n == 0, stop=True)
                        done.then_inc(sem("o_full"), 1)
                        if n == TT - 1:
                            continue
                        pe.wait_ge(sem("k_faded"), 4 * q + 4)
                        for r in range(4):
                            h = 4 * q + r
                            done = pe.matmul(bank[4 + q][:, r * P:(r + 1) * P], unit(gk, h * TT + n), v_new[:, h, :],
                                             start=True, stop=True)
                        done.then_inc(sem("state_full"), 1)
                pe.wait_ge(sem("o_gated"), TT)
                for n in range(TT):
                    for h in range(GH):
                        done = pe.transpose(bank[2 * n + h // 4][:, h % 4 * P:(h % 4 + 1) * P],
                                            unit(gv, h * TT + n), ident)
                    done.then_inc(sem("o_turned"), 1)
                pe.wait_ge(sem("o_low"), 2 * TT)

            pe.wait_ge(sem("const_landed"), 16)
            transpose_acts(0)
            groups(RET_QK, 4, 2, True, act_hi, act_lo)
            groups(RET_V, 8, 2, False, act_hi, act_lo)
            retention()
            groups(RET_OUT, 2, 4, False, y_hi, y_lo)
            transpose_acts(1)
            mlp(0)
            transpose_acts(2)
            delta_projections()
            delta_rule()
            groups(GDN_OUT, 2, 2, False, act_hi, act_lo)
            transpose_acts(3)
            mlp(1)

        @block.scalar
        def _(act):
            chain = Chain(act, "act_step")

            def high(slot):
                act.activation(w_hi[:, slot, :, :], w_raw[:, slot, :, :], ACT.Copy).then_inc(w_high, 1)

            def splits(start, i, chunks, first=1, last=None):
                g0, c0, u0 = start
                for j in range(first, (last or chunks) + 1):
                    act.wait_ge(w_landed[j % 2], i * (8 * chunks) + 16 * ((c0 + j) // 2 + 1))
                    if j == 1:
                        if g0 or not isinstance(i, int) or i:
                            act.wait_ge(bank_full, i * 4 + 4 * g0)
                    else:
                        act.wait_ge(chunk_used, i * (chunks - 1) + (u0 + j - 1))
                    high(j % 2)

            def empty(start, i, p, m, dst, func=ACT.Copy):
                act.wait_ge(bank_full, i * 4 + (4 * start[0] + m + 1))
                act.activation(dst, bank[4 * p + m][:, :], func).then_inc(emptied, 1)

            def load_gains(b):
                for n, row in enumerate(GAIN_ROWS[b]):
                    if row is not None:
                        act.dma_start(gains[:, n, :], norm_gains[row[0], row[1], :].partition_broadcast(P))\
                            .then_inc(sem("gains_landed"), 16)

            def sum_squares(src, m, where):
                chain.link(act.activation(dump[:, :], src, ACT.Square, accum_out=stat[:, where, m:m + 1]))

            def root(m, ss, to, done):
                act.activation(stat[:, to, m:m + 1], stat[:, ss, m:m + 1], ACT.Sqrt, scale=1.0 / D, bias=eps)\
                    .then_inc(sem(done), 1)

            def high_acts(b, m):
                act.wait_ge(sem("acts_transposed"), TT * b + m + 1)
                for half in range(2):
                    act.activation(act_hi[:, 4 * half:4 * half + 4, m * P:(m + 1) * P],
                                   tall(bank[2 * (m % 2) + half]), ACT.Copy).then_inc(sem("act_high"), 1)

            def norms(b, before):
                for m in range(TT + 2):
                    if m < TT:
                        before(m)
                        if b:
                            sum_squares(mix[:, m, :], m, SS_MIX)
                            root(m, SS_MIX, ROOT_MIX, "mix_rooted")
                    if 1 <= m <= TT and b < 4:
                        if b:
                            act.wait_ge(sem("residual_done"), TT * (b - 1) + m)
                        sum_squares(resid[:, m - 1, :], m - 1, SS_RES)
                        root(m - 1, SS_RES, ROOT_RES, "resid_rooted")
                    if m >= 2 and b < 4:
                        high_acts(b, m - 2)

            for m in range(TT):
                act.dma_start(resid[:, m, :], x[0, m * P:(m + 1) * P, :]).then_inc(sem(f"x_landed{m}"), 16)
            act.dma_start(square[:, :, :], square_c).then_inc(sem("const_landed"), 16)
            load_gains(0)
            act.dma_start(rope[:, :, :], rope_c).then_inc(sem("rope_landed"), 16)
            act.wait_ge(sem("eps_set"), 1)

            def before_input(m):
                act.wait_ge(sem(f"x_landed{m}"), 16)

            norms(0, before_input)
            act.wait_ge(w_landed[0], 16)
            high(0)
            act.wait_ge(sem("normed"), TT)
            act.dma_start(gains[:, :, :].rearrange("p a n -> p (a n)"), ret_gn_gain[0].partition_broadcast(P))\
                .then_inc(sem("gn_gain_landed"), 16)

            for i in range(4):
                splits(RET_QK, i, 2)
                for m in range(4):
                    empty(RET_QK, i, i % 2, m, qk_t[:, 4 * i + m, :])
            with act.Fori(0, 2) as i2:
                for p in range(2):
                    i = i2 * 2 + p
                    splits(RET_V, i, 2)
                    for m in range(4):
                        empty(RET_V, i, p, m, v_tm[:, m, bass.ds(i * GC, GC)])
            act.wait_ge(sem("roped"), KT)
            with act.Fori(0, 2) as i2:
                for p in range(2):
                    i = i2 * 2 + p
                    splits(RET_G, i, 2)
                    for m in range(4):
                        empty(RET_G, i, p, m, gate[:, m, bass.ds(i * GC, GC)], ACT.Silu)
            act.dma_start(decay[:, :, :], decay_c).then_inc(sem("decay_landed"), 16)
            act.wait_ge(sem("gate_gained"), 4 * TT)
            load_gains(1)
            for n in range(RH * TT + 1):
                if n < RH * TT:
                    act.wait_ge(sem("varied"), n + 1)
                    act.activation(bn[:, n, BN_ROOT:BN_ROOT + 1], bn[:, n, BN_VAR:BN_VAR + 1], ACT.Sqrt, bias=eps)\
                        .then_inc(sem("gn_rooted"), 1)
                if n:
                    h, m = (n - 1) // TT, (n - 1) % TT
                    act.wait_ge(sem("gn_inverted"), n)
                    y = gate[:, m, h * RV:(h + 1) * RV]
                    act.activation(y, y, ACT.Copy, scale=bn[:, n - 1, BN_RSTD:BN_RSTD + 1])\
                        .then_inc(sem("y_scaled"), 1)
            for n in range(RH * TT):
                h, m = n // TT, n % TT
                act.wait_ge(sem("y_transposed"), n + 1)
                act.activation(y_hi[:, 4 * h:4 * h + 4, m * P:(m + 1) * P], tall(bank[n % 8]), ACT.Copy)\
                    .then_inc(sem("y_high"), 1)
            splits(RET_OUT, 0, 4)
            for m in range(TT):
                empty(RET_OUT, 0, 0, m, mix[:, m, 0:GC])
            splits(RET_OUT, 1, 4)

            def empty_last(start, m):
                empty(start, 1, 1, m, mix[:, m, GC:2 * GC])
                act.wait_ge(emptied, 4 * (start[0] + 1) + m + 1)

            norms(1, lambda m: empty_last(RET_OUT, m))

            def mlp(layer):
                b = 2 * layer + 2
                for half, (up, down) in enumerate(MLP[layer]):
                    with act.Fori(0, 2) as i2:
                        for p in range(2):
                            i = i2 * 2 + p
                            splits(up, i, 2)
                            for m in range(4):
                                empty(up, i, p, m, relu[:, m, :], ACT.Relu)
                            act.wait_ge(sem("squared"), i * 4 + (HALF_TILES * (2 * layer + half) + 4))
                    splits(down, 0, 4)
                    for m in range(TT):
                        empty(down, 0, 0, m, mix_b[:, m, :] if half else mix[:, m, 0:GC])
                    splits(down, 1, 4, last=3 if layer and half else None)
                    if half == 0:
                        for m in range(TT):
                            empty(down, 1, 1, m, mix[:, m, GC:2 * GC])

                def before(m):
                    act.wait_ge(sem("mix_summed"), 8 * layer + m + 1)
                    empty(MLP[layer][1][1], 1, 1, m, mix_b[:, m, :])
                    act.wait_ge(sem("mix_summed"), 8 * layer + 4 + m + 1)
                norms(b, before)

            act.wait_ge(sem("normed"), 2 * TT)
            load_gains(2)
            mlp(0)

            act.dma_start(conv_rows[:, :], gdn_conv_w[0].rearrange("j (k p) -> (j k) p", p=P))\
                .then_inc(sem("conv_rows_landed"), 16)
            act.dma_start(join_f[:, :, :, :], join_c).then_inc(sem("join_landed"), 16)
            act.dma_start(z_gain[:, :], gdn_norm_gain[0].partition_broadcast(P)).then_inc(sem("rows_landed"), 16)
            act.dma_start(head_rows[:, 0, :], gdn_dt_bias[0].partition_broadcast(P)).then_inc(sem("rows_landed"), 16)
            act.dma_start(head_rows[:, 1, :], gdn_a_log[0].partition_broadcast(P)).then_inc(sem("rows_landed"), 16)
            act.wait_ge(sem("ba_cleared"), 1)
            act.wait_ge(sem("ba_landed"), 16)
            act.activation(ba_hi[:, :, 0:2 * GH], ba_raw[:, :, :], ACT.Copy).then_inc(sem("ba_high"), 1)
            act.wait_ge(sem("ba_full"), 1)
            act.activation(ba_t[:, :], bank[4][:, :], ACT.Copy).then_inc(sem("ba_out"), 1)
            order = [(GDN_K, gk), (GDN_V, gv), (GDN_Q, gq)]

            def silu(gi):
                for m in range(4):
                    act.wait_ge(sem("convolved"), 4 * gi + m + 1)
                    t = order[gi // 2][1][:, gi % 2 * 4 + m, :]
                    act.activation(t, t, ACT.Silu).then_inc(sem("silued"), 1)

            for gi in range(8):
                start, p = (order + [(GDN_Z, None)])[gi // 2][0], gi % 2
                splits(start, p, 2)
                if gi == 0:
                    act.wait_ge(sem("small_turned"), 1)
                    act.activation(ba_cols[:, :, :], tall(bank[5])[:, :, 0:2 * GH], ACT.Copy)\
                        .then_inc(sem("small_out"), 1)
                    rows = CONV * 3 * KT
                    act.activation(conv_w[:, :, :].rearrange("p j k -> p (j k)"), bank[6][:, 0:rows], ACT.Copy)\
                        .then_inc(sem("small_out"), 1)
                if gi == 1:
                    act.wait_ge(sem("cols_a"), 1)
                    act.activation(ct[:, 2:4, :], ct[:, 0:2, :], ACT.Exp).then_inc(sem("cols_b"), 1)
                    act.wait_ge(sem("rows_landed"), 48)
                    act.activation(head_rows[:, 2, :], head_rows[:, 1, :], ACT.Exp).then_inc(sem("cols_b"), 1)
                    act.wait_ge(sem("cols_c"), 1)
                    act.activation(ct[:, 6, :], ct[:, 5, :], ACT.Ln).then_inc(sem("cols_d"), 1)
                if 1 <= gi <= 6:
                    silu(gi - 1)
                for m in range(4):
                    if gi < 6:
                        if gi >= 2:
                            act.wait_ge(sem("convolved"), 4 * (gi - 2) + m + 1)
                        if gi < 2:
                            act.wait_ge(sem("pad_cleared"), 1)
                        empty(start, p, p, m, pad[:, p, m, CONV - 1:CONV - 1 + T])
                    else:
                        empty(start, p, p, m, gz[:, m, p * GC:(p + 1) * GC], ACT.Silu)
            act.wait_ge(sem("g_summed"), 1)
            act.activation(col[:, EXP_G, :], bank[7][:, 0:UNITS], ACT.Exp)
            act.activation(col[:, EXP_TOT, :], bank[7][:, UNITS:2 * UNITS], ACT.Exp).then_inc(sem("g_sums_read"), 1)
            act.wait_ge(sem("rest_made"), 1)
            act.activation(ct[:, 8, :], ct[:, 7, :], ACT.Exp).then_inc(sem("rest_exped"), 1)
            for i in range(2 * GH):
                act.wait_ge(sem("kq_turned"), i + 1)
                if i >= 4:
                    act.wait_ge(sem("kq_summed"), i - 3)
                act.activation(tmp[:, i % 4, :], bank[i % 8][:, :], ACT.Square).then_inc(sem("kq_squared"), 1)
            act.wait_ge(sem("kq_x_made"), 1)
            act.activation(ct[:, 2:4, :], ct[:, 0:2, :], ACT.Sqrt).then_inc(sem("kq_rooted"), 1)
            act.wait_ge(sem("kq_summed"), 2 * GH)
            for h in range(GH):
                act.wait_ge(sem("row_shifted"), h + 1)
                if h >= 2:
                    act.wait_ge(sem("q_grown"), h - 1)
                act.activation(tmp[:, 2 + h % 2, :], bank[4 + h % 2][:, :], ACT.Exp).then_inc(sem("row_exped"), 1)
                act.activation(tmp[:, h % 2, :], tmp[:, h % 2, :], ACT.Exp).then_inc(sem("decay_made"), 1)
                act.wait_ge(sem("kv_turned"), h + 1)
                act.activation(gk[:, h, :], bank[6][:, :], ACT.Copy).then_inc(sem("k_turned_out"), 1)
            act.wait_ge(sem("q_grown"), GH)
            act.wait_ge(sem("unit_scaled"), GH)
            load_gains(3)
            n_p = 0
            for batch in range(2):
                heads = range(4 * batch, 4 * batch + 4)
                for r, h in enumerate(heads):
                    act.wait_ge(sem("inv_turned"), h + 1)
                    act.activation(inv[:, 4 * r:4 * r + 4, :], tall(bank[r]), ACT.Copy).then_inc(sem("inv_placed"), 1)
                for level in range(1, len(LEVELS)):
                    for r in range(4):
                        n_p += 1
                        act.wait_ge(sem("prod_made"), n_p)
                        act.activation(half_prod[:, 4 * r:4 * r + 4, :], tall(bank[r]), ACT.Copy)\
                            .then_inc(sem("prod_out"), 1)
                for r, h in enumerate(heads):
                    act.wait_ge(sem("w_made"), h + 1)
                    act.activation(w_t[:, h * TT:(h + 1) * TT, :], tall(bank[r]), ACT.Copy, scale=-1.0)\
                        .then_inc(sem("w_out"), 1)
            outs = gv[:, :, :].rearrange("p h (n e) -> p h n e", n=TT)
            for n in range(TT):
                act.wait_ge(sem("o_out"), 2 * n + 2)
                if n:
                    act.wait_ge(sem("o_summed"), n)
                act.activation(o_sq[:, :, :], outs[:, :, n, :], ACT.Square).then_inc(sem("o_squared"), 1)
                act.wait_ge(sem("o_summed"), n + 1)
                act.activation(on[:, n, 1, :], on[:, n, 0, :], ACT.Sqrt, scale=1.0 / P, bias=eps)\
                    .then_inc(sem("o_rooted"), 1)
            for n in range(TT):
                act.wait_ge(sem("o_turned"), n + 1)
                for half in range(2):
                    act.activation(act_hi[:, 4 * half:4 * half + 4, n * P:(n + 1) * P], tall(bank[2 * n + half]),
                                   ACT.Copy).then_inc(sem("o_high"), 1)
            splits(GDN_OUT, 0, 2)
            for m in range(TT):
                empty(GDN_OUT, 0, 0, m, mix[:, m, 0:GC])
            splits(GDN_OUT, 1, 2)
            norms(3, lambda m: empty_last(GDN_OUT, m))
            act.wait_ge(sem("normed"), 4 * TT)
            load_gains(4)
            mlp(1)
            for m in range(TT):
                act.wait_ge(sem("residual_done"), 3 * TT + m + 1)
                act.dma_start(out[0, m * P:(m + 1) * P, :], resid[:, m, :]).then_inc(sem("stored"), 16)
            act.wait_ge(sem("stored"), 16 * TT)

        @block.vector
        def _(dve):
            chain = Chain(dve, "dve_step")
            link = chain.link

            def inv_root(x, root, temp, out_, scale=1.0, add=EPS):
                t = [temp(n) for n in range(3)]
                link(dve.tensor_scalar(t[0], x, scale, add, ALU.mult, ALU.add))
                link(dve.reciprocal(t[1], root))
                link(dve.tensor_tensor(t[2], t[0], t[1], ALU.mult))
                link(dve.tensor_tensor(t[2], t[2], t[1], ALU.mult))
                link(dve.tensor_scalar(t[2], t[2], -0.5, 1.5, ALU.mult, ALU.add))
                return dve.tensor_tensor(out_, t[1], t[2], ALU.mult)

            def norms(b, before=None):
                def col_of(n, m):
                    return stat[:, n, m:m + 1]
                if b:
                    dve.wait_ge(sem("gains_landed"), GAINS_LANDED[b])
                for m in range(TT + 2):
                    if m < TT and b:
                        if before:
                            before(m)
                        dve.wait_ge(sem("mix_rooted"), TT * (b - 1) + m + 1)
                        link(inv_root(col_of(SS_MIX, m), col_of(ROOT_MIX, m), lambda n: col_of(NEWTON + n, m),
                                      col_of(RSTD_MIX, m), 1.0 / D))
                        link(dve.scalar_tensor_tensor(mix[:, m, :], mix[:, m, :], col_of(RSTD_MIX, m), gains[:, 0, :],
                                                      ALU.mult, ALU.mult))
                        dve.tensor_tensor(resid[:, m, :], resid[:, m, :], mix[:, m, :], ALU.add)\
                            .then_inc(sem("residual_done"), 1)
                    if 1 <= m <= TT and b < 4:
                        if b == 0 and m == 1:
                            dve.wait_ge(sem("gains_landed"), GAINS_LANDED[0])
                        if b:
                            dve.wait_ge(sem("residual_done"), TT * (b - 1) + m)
                        dve.wait_ge(sem("resid_rooted"), TT * b + m)
                        link(inv_root(col_of(SS_RES, m - 1), col_of(ROOT_RES, m - 1),
                                      lambda n: col_of(NEWTON + n, m - 1), col_of(RSTD_RES, m - 1), 1.0 / D))
                        if TT * b + m > 2:
                            dve.wait_ge(sem("acts_transposed"), TT * b + m - 2)
                        dve.scalar_tensor_tensor(normed[:, (m - 1) % 2, :], resid[:, m - 1, :], col_of(RSTD_RES, m - 1),
                                                 gains[:, 1, :], ALU.mult, ALU.mult).then_inc(sem("normed"), 1)
                    if m >= 2 and b < 4:
                        t = m - 2
                        for half in range(2):
                            dve.wait_ge(sem("act_high"), 2 * (TT * b + t) + half + 1)
                            where = (slice(None), slice(4 * half, 4 * half + 4), slice(t * P, (t + 1) * P))
                            dve.tensor_tensor(act_lo[where], tall(bank[2 * (t % 2) + half]), act_hi[where].bitcast(F32),
                                              ALU.subtract).then_inc(sem("act_low"), 1)

            dve.memset(stat[:, :, :], EPS).then_inc(sem("eps_set"), 1)
            dve.wait_ge(sem("eps_set"), 1)
            norms(0)

            dve.wait_ge(sem("rope_landed"), 16)
            cos, sin = rope[:, 0, :], rope[:, 1, :]
            for n in range(KT):
                dve.wait_ge(emptied, 2 * n + 2)
                x1, x2 = qk_t[:, 2 * n, :], qk_t[:, 2 * n + 1, :]
                dve.tensor_tensor(rope_tmp[:, 0, :], x1, cos, ALU.mult)
                dve.tensor_tensor(rope_tmp[:, 1, :], x2, sin, ALU.mult)
                dve.tensor_tensor(rope_tmp[:, 2, :], x1, sin, ALU.mult)
                link(dve.tensor_tensor(rope_tmp[:, 3, :], x2, cos, ALU.mult))
                dve.tensor_tensor(x1, rope_tmp[:, 0, :], rope_tmp[:, 1, :], ALU.subtract)
                dve.tensor_tensor(x2, rope_tmp[:, 2, :], rope_tmp[:, 3, :], ALU.add).then_inc(sem("roped"), 1)
                dve.wait_ge(sem("roped"), n + 1)
            dve.wait_ge(sem("gn_gain_landed"), 16)
            with dve.Fori(0, 4) as i:
                for m in range(TT):
                    dve.wait_ge(emptied, i * 4 + (4 * RET_G[0] + m + 1))
                    g = gate[:, m, bass.ds(i * GC, GC)]
                    dve.tensor_tensor(g, g, gains[:, :, :].rearrange("p a n -> p (a n)")[:, bass.ds(i * GC, GC)],
                                      ALU.mult).then_inc(sem("gate_gained"), 1)
            dve.wait_ge(sem("gate_gained"), 4 * TT)
            dve.wait_ge(sem("decay_landed"), 16)

            def decayed(h):
                for i in range(TT):
                    dve.wait_ge(sem("scored"), TT * h + i + 1)
                    if h >= 2:
                        dve.wait_ge(sem("attended"), TT * (h - 1))
                    dve.tensor_tensor(score[:, h % 2, i, i * P:T], bank[i][:, 0:T - i * P],
                                      decay[:, h, 0:T - i * P], ALU.mult).then_inc(sem("decayed"), 1)

            def inverted(n):
                dve.wait_ge(sem("gn_rooted"), n + 1)
                inv_root(bn[:, n, BN_VAR:BN_VAR + 1], bn[:, n, BN_ROOT:BN_ROOT + 1],
                         lambda t: bn[:, n, BN_NEWTON + t:BN_NEWTON + t + 1], bn[:, n, BN_RSTD:BN_RSTD + 1])\
                    .then_inc(sem("gn_inverted"), 1)

            decayed(0)
            for h in range(RH):
                if h + 1 < RH:
                    decayed(h + 1)
                for m in range(TT):
                    n = TT * h + m
                    dve.wait_ge(sem("attended"), n + 1)
                    link(dve.bn_stats(bn[:, n, 0:6], bank[4 + m][:, :]))
                    dve.bn_aggr(bn[:, n, BN_MEAN:BN_VAR + 1], bn[:, n, 0:6]).then_inc(sem("varied"), 1)
                    dve.wait_ge(sem("varied"), n + 1)
                    y = gate[:, m, h * RV:(h + 1) * RV]
                    dve.scalar_tensor_tensor(y, bank[4 + m][:, :], bn[:, n, BN_MEAN:BN_MEAN + 1], y,
                                             ALU.subtract, ALU.mult).then_inc(sem("y_gated"), 1)
                    inverted(n)
            for n in range(RH * TT):
                h, m = n // TT, n % TT
                dve.wait_ge(sem("y_high"), n + 1)
                where = (slice(None), slice(4 * h, 4 * h + 4), slice(m * P, (m + 1) * P))
                dve.tensor_tensor(y_lo[where], tall(bank[n % 8]), y_hi[where].bitcast(F32), ALU.subtract)\
                    .then_inc(sem("y_low"), 1)
            norms(1)

            def mlp(layer):
                for half, (up, down) in enumerate(MLP[layer]):
                    base = HALF_TILES * (2 * layer + half)
                    with dve.Fori(0, 4) as i:
                        for m in range(4):
                            dve.wait_ge(emptied, i * 4 + (4 * up[0] + m + 1))
                            dve.tensor_tensor(relu_sq[:, m, :], relu[:, m, :], relu[:, m, :], ALU.mult)\
                                .then_inc(sem("squared"), 1)
                            dve.wait_ge(sem("squared"), i * 4 + (base + m + 1))
                            dve.tensor_copy(hid_hi[:, bass.ds(i * 4 + m, 1), :], relu_sq[:, m:m + 1, :])\
                                .then_inc(sem("hid_high"), 1)
                            dve.wait_ge(sem("hid_high"), i * 4 + (base + m + 1))
                            dve.tensor_tensor(hid_lo[:, bass.ds(i * 4 + m, 1), :], relu_sq[:, m:m + 1, :],
                                              hid_hi[:, bass.ds(i * 4 + m, 1), :].bitcast(F32), ALU.subtract)\
                                .then_inc(sem("hid_low"), 1)

                def add_part(i, m):
                    dve.wait_ge(emptied, 4 * (MLP[layer][1][1][0] + i) + m + 1)
                    part = mix[:, m, i * GC:(i + 1) * GC]
                    dve.tensor_tensor(part, part, mix_b[:, m, :], ALU.add).then_inc(sem("mix_summed"), 1)
                    dve.wait_ge(sem("mix_summed"), 8 * layer + 4 * i + m + 1)

                for m in range(TT):
                    add_part(0, m)
                norms(2 * layer + 2, lambda m: add_part(1, m))

            mlp(0)

            dve.wait_ge(bank_full, 4 * GDN_K[0])
            dve.memset(ba_hi[:, :, :].bitcast(F32), 0.0)
            dve.memset(ba_lo[:, :, :].bitcast(F32), 0.0).then_inc(sem("ba_cleared"), 1)
            dve.wait_ge(sem("ba_high"), 1)
            dve.tensor_tensor(ba_lo[:, :, 0:2 * GH], ba_raw[:, :, :], ba_hi[:, :, 0:2 * GH].bitcast(F32), ALU.subtract)\
                .then_inc(sem("ba_low"), 1)
            dve.memset(pad[:, :, :, 0:CONV - 1], 0.0).then_inc(sem("pad_cleared"), 1)
            dve.wait_ge(sem("join_landed"), 16)
            dve.tensor_copy(join[:, :, :, :], join_f[:, :, :, :]).then_inc(sem("join_cast"), 1)

            def by_unit(t, first):
                return t[:, :, first:first + GH].rearrange("p n h -> p h n")

            def units_of(c):
                return c.rearrange("p (h n) -> p h n", n=TT)

            def spread(row):
                return row.rearrange("p (h o) -> p h o", o=1).broadcast_to([P, GH, TT])

            def columns_before():
                dve.wait_ge(sem("small_out"), 1)
                dve.wait_ge(sem("rows_landed"), 48)
                link(dve.tensor_scalar(units_of(ct[:, 0, :]), by_unit(ba_cols, 0), -1.0, None, ALU.mult))
                link(dve.tensor_tensor(units_of(ct[:, 4, :]), by_unit(ba_cols, GH), spread(head_rows[:, 0, :]), ALU.add))
                link(dve.tensor_scalar(ct[:, 9, :], ct[:, 4, :], -1.0, None, ALU.mult))
                dve.tensor_tensor(ct[:, 1, :], ct[:, 9, :], ct[:, 4, :], ALU.min).then_inc(sem("cols_a"), 1)
                dve.wait_ge(sem("cols_b"), 2)
                dve.tensor_scalar(ct[:, 5, :], ct[:, 3, :], 1.0, None, ALU.add).then_inc(sem("cols_c"), 1)
                dve.wait_ge(sem("cols_c"), 1)

            def columns_after():
                link(dve.tensor_scalar(ct[:, 10, :], ct[:, 2, :], 1.0, None, ALU.add))
                link(dve.reciprocal(col[:, BETA, :], ct[:, 10, :]))
                link(dve.tensor_scalar(ct[:, 11, :], ct[:, 5, :], -1.0, 1e-30, ALU.add, ALU.max))
                link(dve.reciprocal(ct[:, 12, :], ct[:, 11, :]))
                dve.wait_ge(sem("cols_d"), 1)
                link(dve.tensor_tensor(ct[:, 13, :], ct[:, 6, :], ct[:, 3, :], ALU.mult))
                link(dve.tensor_tensor(ct[:, 13, :], ct[:, 13, :], ct[:, 12, :], ALU.mult))
                link(dve.scalar_tensor_tensor(ct[:, 14, :], ct[:, 5, :], 1.0, ct[:, 3, :], ALU.is_equal, ALU.mult))
                link(dve.scalar_tensor_tensor(ct[:, 13, :], ct[:, 4, :], 0.0, ct[:, 13, :], ALU.max, ALU.add))
                link(dve.tensor_tensor(ct[:, 13, :], ct[:, 13, :], ct[:, 14, :], ALU.add))
                dve.scalar_tensor_tensor(units_of(col[:, G, :]), units_of(ct[:, 13, :]), -1.0,
                                         spread(head_rows[:, 2, :]), ALU.mult, ALU.mult).then_inc(sem("g_made"), 1)

            order = [(GDN_K, gk, KT), (GDN_V, gv, 2 * KT), (GDN_Q, gq, 0)]
            dve.wait_ge(sem("pad_cleared"), 1)
            columns_before()
            dve.wait_ge(sem("small_out"), 2)
            for gi in range(6):
                start, dest, tile0 = order[gi // 2]
                p = gi % 2
                for m in range(4):
                    dve.wait_ge(emptied, 4 * (start[0] + p) + m + 1)
                    t = dest[:, 4 * p + m, :]
                    w = [conv_w[:, j, tile0 + 4 * p + m:tile0 + 4 * p + m + 1] for j in range(CONV)]
                    link(dve.tensor_scalar(t, pad[:, p, m, 0:T], w[0], None, ALU.mult))
                    for j in range(1, CONV):
                        step = dve.scalar_tensor_tensor(t, pad[:, p, m, j:j + T], w[j], t, ALU.mult, ALU.add)
                        if j < CONV - 1:
                            link(step)
                    step.then_inc(sem("convolved"), 1)
                if gi == 0:
                    columns_after()
            for p in range(2):
                for m in range(TT):
                    dve.wait_ge(emptied, 4 * (GDN_Z[0] + p) + m + 1)
                    z = gz[:, m, p * GC:(p + 1) * GC].rearrange("p (h e) -> p h e", h=4)
                    dve.tensor_tensor(z, z, z_gain[:, :].rearrange("p (o e) -> p o e", o=1).broadcast_to([P, 4, P]),
                                      ALU.mult).then_inc(sem("z_gained"), 1)

            def over(c, n=P):
                return c.rearrange("p (k o) -> p k o", o=1).broadcast_to([P, c.shape[-1], n])

            dve.wait_ge(sem("g_sums_read"), 1)
            link(dve.tensor_copy(col[:, GCUM, :], bank[7][:, 0:UNITS]))
            link(dve.tensor_tensor(ct[:, 7, :], bank[7][:, UNITS:2 * UNITS], col[:, GCUM, :], ALU.subtract))
            dve.sem_inc(sem("rest_made"), 1)
            dve.sem_inc(sem("g_sums_read"), 1)
            for i in range(2 * GH):
                dve.wait_ge(sem("kq_squared"), i + 1)
                dve.tensor_reduce(col[:, (SS_K, SS_Q)[i // GH], i % GH * TT:(i % GH + 1) * TT],
                                  tmp[:, i % 4, :].rearrange("p (n e) -> p n e", n=TT), AX.X, ALU.add)\
                    .then_inc(sem("kq_summed"), 1)
            dve.wait_ge(sem("kq_summed"), 2 * GH)
            both = col[:, SS_K:SS_Q + 1, :]
            link(dve.tensor_scalar(ct[:, 0:2, :], both, EPS, None, ALU.add))
            dve.sem_inc(sem("kq_x_made"), 1)
            dve.wait_ge(sem("kq_rooted"), 1)
            link(inv_root(both, ct[:, 2:4, :], lambda n: ct[:, 9 + 2 * n:11 + 2 * n, :], ct[:, 2:4, :]))
            link(dve.tensor_copy(col[:, R_K, :], ct[:, 2, :]))
            link(dve.tensor_scalar(col[:, R_Q, :], ct[:, 3, :], float(P) ** -0.5, None, ALU.mult))
            link(dve.tensor_tensor(col[:, N_K, :], ct[:, 0, :], ct[:, 2, :], ALU.mult))
            link(dve.tensor_tensor(col[:, S_V, :], col[:, BETA, :], ct[:, 2, :], ALU.mult))
            link(dve.scalar_tensor_tensor(col[:, S_U, :], ct[:, 2, :], -1.0, col[:, S_V, :], ALU.mult, ALU.mult))
            dve.wait_ge(sem("rest_exped"), 1)
            link(dve.tensor_tensor(col[:, EXP_REST, :], ct[:, 8, :], ct[:, 2, :], ALU.mult))

            def column(c, u):
                return col[:, c, u:u + 1]

            for h in range(GH):
                dve.wait_ge(sem("row_made"), h + 1)
                for n in range(TT):
                    u = h * TT + n
                    cols = slice(n * P, (n + 1) * P)
                    step = dve.scalar_tensor_tensor(tmp[:, h % 2, cols], bank[4 + h % 2][:, cols], column(GCUM, u), neg,
                                                    ALU.subtract, ALU.add)
                step.then_inc(sem("row_shifted"), 1)
                dve.wait_ge(sem("unit_prods"), h + 1)
                dve.wait_ge(sem("decay_made"), h + 1)
                for n in range(TT):
                    u = h * TT + n
                    cols = slice(n * P, (n + 1) * P)
                    dve.scalar_tensor_tensor(neg_l_t[:, u, :], bank[h % 2][:, cols], column(S_U, u), tmp[:, h % 2, cols],
                                             ALU.mult, ALU.mult)
                    step = dve.scalar_tensor_tensor(attn[:, u, :], bank[2 + h % 2][:, cols], column(R_K, u),
                                                    tmp[:, h % 2, cols], ALU.mult, ALU.mult)
                step.then_inc(sem("unit_scaled"), 1)
                dve.wait_ge(sem("kv_turned"), h + 1)
                dve.tensor_tensor(gv[:, h, :].rearrange("p (n e) -> p n e", n=TT), tall(bank[7]),
                                  over(col[:, N_K, h * TT:(h + 1) * TT]), ALU.mult).then_inc(sem("v_turned_out"), 1)
            dve.wait_ge(sem("unit_scaled"), GH)
            dve.wait_ge(sem("join_cast"), 1)

            def mask(side, level):
                return join[:, side, level:level + 1, :].broadcast_to([P, TT, P])

            def seed(h):
                us = slice(h * TT, (h + 1) * TT)
                link(dve.tensor_copy(inv_t[:, us, :],
                                     ident.rearrange("p (o e) -> p o e", o=1).broadcast_to([P, TT, P])))
                dve.copy_predicated(inv_t[:, us, :], mask(1, 0), neg_l_t[:, us, :]).then_inc(sem("inv_seeded"), 1)

            n_second = 0
            for h in range(GH):
                seed(h)
            dve.wait_ge(sem("inv_seeded"), GH)
            for batch in range(2):
                heads = range(4 * batch, 4 * batch + 4)
                for level in range(1, len(LEVELS)):
                    for r, h in enumerate(heads):
                        n_second += 1
                        dve.wait_ge(sem("seconds_made"), n_second)
                        if level < len(LEVELS) - 1:
                            dve.copy_predicated(inv[:, 4 * r:4 * r + 4, :], mask(0, level), tall(bank[4 + r % 2 * 2]))
                        dve.copy_predicated(inv_t[:, h * TT:(h + 1) * TT, :], mask(1, level),
                                            tall(bank[5 + r % 2 * 2])).then_inc(sem("joined"), 1)
                        if level == len(LEVELS) - 1:
                            k = gk[:, h, :].rearrange("p (n e) -> p n e", n=TT)
                            cs = slice(h * TT, (h + 1) * TT)
                            dve.wait_ge(sem("k_turned_out"), GH)
                            dve.tensor_tensor(k_grown[:, 4 * r:4 * r + 4, :], k, over(col[:, EXP_G, cs]), ALU.mult)\
                                .then_inc(sem("k_grown"), 1)
                            dve.tensor_tensor(k, k, over(col[:, EXP_REST, cs]), ALU.mult).then_inc(sem("k_faded"), 1)
            outs = gv[:, :, :].rearrange("p h (n e) -> p h n e", n=TT)
            per_unit = [col[:, c, :].rearrange("p (h n) -> p h n", n=TT) for c in range(13)]

            def some(c, q, n):
                return per_unit[c][:, 4 * q:4 * q + 4, n:n + 1].broadcast_to([P, 4, P])

            def outputs(n):
                dve.wait_ge(sem("o_squared"), n + 1)
                dve.tensor_reduce(on[:, n, 0, :], o_sq[:, :, :], AX.X, ALU.add).then_inc(sem("o_summed"), 1)
                dve.wait_ge(sem("o_rooted"), n + 1)
                link(inv_root(on[:, n, 0, :], on[:, n, 1, :], lambda t: on[:, n, 2 + t, :], on[:, n, 5, :], 1.0 / P))
                dve.tensor_tensor(outs[:, :, n, :], outs[:, :, n, :], over(on[:, n, 5, :]), ALU.mult)\
                    .then_inc(sem("o_scaled"), 1)

            for n in range(TT):
                for q in range(2):
                    hs = slice(4 * q, 4 * q + 4)
                    dve.wait_ge(sem("v_new_full"), 2 * n + q + 1)
                    if n:
                        dve.wait_ge(sem("state_full"), 2 * (n - 1) + q + 1)
                    dve.tensor_tensor(v_new[:, hs, :], tall(bank[q]), some(S_V, q, n), ALU.mult)\
                        .then_inc(sem("v_new_made"), 1)
                for q in range(2):
                    hs = slice(4 * q, 4 * q + 4)
                    dve.wait_ge(sem("o_full"), 2 * n + q + 1)
                    dve.tensor_tensor(outs[:, hs, n, :], tall(bank[2 + q]), some(R_Q, q, n), ALU.mult)\
                        .then_inc(sem("o_out"), 1)
                    if n == TT - 1:
                        continue
                    dve.wait_ge(sem("state_full"), 2 * n + q + 1)
                    if n == 0:
                        dve.tensor_copy(state[:, hs, :], tall(bank[4 + q])).then_inc(sem("state_made"), 1)
                        continue
                    dve.wait_ge(sem("state_made"), 2 * (n - 1) + q + 1)
                    for r in range(4):
                        h = 4 * q + r
                        step = dve.scalar_tensor_tensor(state[:, h, :], state[:, h, :], column(EXP_TOT, h * TT + n),
                                                        bank[4 + q][:, r * P:(r + 1) * P], ALU.mult, ALU.add)
                    step.then_inc(sem("state_made"), 1)
                if n:
                    outputs(n - 1)
            outputs(TT - 1)
            for n in range(TT):
                for half in range(2):
                    dve.wait_ge(sem("o_high"), 2 * n + half + 1)
                    where = (slice(None), slice(4 * half, 4 * half + 4), slice(n * P, (n + 1) * P))
                    dve.tensor_tensor(act_lo[where], tall(bank[2 * n + half]), act_hi[where].bitcast(F32), ALU.subtract)\
                        .then_inc(sem("o_low"), 1)
            norms(3)
            mlp(1)


_INS = ["x", "norm_gains", "ret_w_in", "ret_gn_gain", "ret_w_out", "gdn_w_in", "gdn_conv_w", "gdn_a_log",
        "gdn_dt_bias", "gdn_norm_gain", "gdn_w_out", "mlp_w_up", "mlp_w_down"]


def kernel(**inputs):
    import concourse.bacc as bacc
    from concourse.bass_utils import run_bass_kernel_spmd

    nc = bacc.Bacc("TRN2", target_bir_lowering=False, num_devices=1)
    arrays, args = {}, []
    given = {name: np.ascontiguousarray(inputs[name]) for name in _INS}
    for name, a in {**given, **shape_constants()}.items():
        arrays[f"in_{name}_dram"] = a
        args.append(nc.dram_tensor(f"in_{name}_dram", a.shape, mybir.dt.from_np(a.dtype), kind="ExternalInput").ap())
    out = nc.dram_tensor("out_dram", (1, T, D), F32, kind="ExternalOutput").ap()
    hybrid_trunk(nc, *args, out)
    result = run_bass_kernel_spmd(nc, [arrays], core_ids=[0])
    return result.results[0]["out_dram"]
```

```python
from contextlib import ExitStack

import numpy as np

import concourse.bass as bass
from concourse import mybir

F32 = mybir.dt.float32
F32R = mybir.dt.float32r
U8 = mybir.dt.uint8
BF16 = mybir.dt.bfloat16
ALU = mybir.AluOpType
ACT = mybir.ActivationFunctionType
AX = mybir.AxisListType

P = 128
D = 1024
T = 512
KT = D // P
TT = T // P
FF = 4 * D
EPS = 1e-6
RH, RQK, RV = 4, D // 4, 2 * D // 4
RET_IN = 2 * D + 2 * 2 * D
VT = 2 * D // P
GH = 8
GDN_CONV = 3 * D
GDN_IN = 4 * D + 2 * GH
CONV = 4
UNITS = GH * TT
BLOCK = 32
LEVELS = [32, 64]

CK = 4
GC = 512
HALF_TILES = FF // 2 // P


def shape_constants():
    half = RQK // 2
    inv_freq = (np.float32(10000.0) ** (-np.arange(half, dtype=np.float32) / np.float32(half))).astype(np.float32)
    angle = (np.arange(T, dtype=np.float32)[None, :] * inv_freq[:, None]).astype(np.float32)
    rope = np.stack([np.cos(angle), np.sin(angle)], axis=1).astype(np.float32)
    gap = np.arange(T)[None, :] - np.arange(P)[:, None]
    log_gamma = np.log1p(-(2.0 ** (-5.0 - np.arange(RH, dtype=np.float64))))
    decay = np.where(gap[:, None, :] >= 0, np.exp(log_gamma[None, :, None] * np.maximum(gap, 0)[:, None, :]), 0.0)
    decay = (decay * RQK ** -0.5).astype(np.float32)
    row, col = np.arange(P)[:, None], np.arange(P)[None, :]
    square = np.stack([
        (row == col), (row <= col), np.ones((P, P)), np.where(row <= col, 0.0, -1e30),
    ], axis=1).astype(np.float32)
    lower = np.stack([(row // (2 * b) == col // (2 * b)) & (row // b % 2 == 1) & (col // b % 2 == 0)
                      for b in LEVELS], axis=1)
    join = np.stack([lower, lower.transpose(2, 1, 0)], axis=1).astype(np.float32)
    return {"rope": rope, "decay": decay, "square": square, "join": join}


class Plan:

    def __init__(self, nc):
        self.nc = nc
        self.at = (nc.sbuf_base + 63) // 64 * 64

    def place(self, size):
        at, self.at = self.at, self.at + (size + 31) // 32 * 32
        assert self.at <= self.nc.sbuf_usable_end, (self.at, self.nc.sbuf_usable_end)
        return at

    def tile(self, name, shape, dtype, at=None):
        size = int(np.prod(shape[1:])) * {U8: 1, BF16: 2}.get(dtype, 4)
        if at is None:
            at = self.place(size)
        return self.nc.alloc_sbuf_tensor_at(name, list(shape), dtype, offset=at)


def hybrid_trunk(nc, x, norm_gains, ret_w_in, ret_gn_gain, ret_w_out, gdn_w_in, gdn_conv_w, gdn_a_log,
                 gdn_dt_bias, gdn_norm_gain, gdn_w_out, mlp_w_up, mlp_w_down, rope_c, decay_c, square_c,
                 join_c, out):
    plan = Plan(nc)
    KB = 1024
    resid = plan.tile("resid", [P, TT, D], F32)
    act_at = plan.place(32 * KB)
    act_hi = plan.tile("act_hi", [P, KT, T], F32R, act_at)
    act_lo = plan.tile("act_lo", [P, KT, T], F32R, act_at + 16 * KB)
    w_raw = plan.tile("w_raw", [P, 2, CK, GC], F32)
    w_hi = plan.tile("w_hi", [P, 2, CK, GC], F32R)
    w_lo = plan.tile("w_lo", [P, 2, CK, GC], F32R)
    gains_at = plan.place(8 * KB)
    gains = plan.tile("gains", [P, 2, D], F32, gains_at)
    square = plan.tile("square", [P, 4, P], F32)
    ident, tri, ones, neg = (square[:, n, :] for n in range(4))
    dump_at = plan.place(2 * KB)
    dump = plan.tile("dump", [P, D], BF16, dump_at)
    stat = plan.tile("stat", [P, 10, TT], F32)
    SS_MIX, ROOT_MIX, SS_RES, ROOT_RES, NEWTON, RSTD_MIX, RSTD_RES, EPS_COL = 0, 1, 2, 3, 4, 7, 8, 9
    eps = stat[:, EPS_COL, 0:1]
    big_at = plan.place(0)

    def big(name, shape, dtype, kb):
        made = plan.tile(name, shape, dtype, big_at + int(kb * KB))
        return made

    normed = big("normed", [P, 2, D], F32, 64)
    mix = big("mix", [P, TT, D], F32, 80)
    qk_t = big("qk_t", [P, 2 * KT, T], F32, 0)
    v_tm = big("v_tm", [P, TT, 2 * D], F32, 32)
    gate = big("gate", [P, TT, 2 * D], F32, 64)
    rope_tmp = big("rope_tmp", [P, 4, T], F32, 64)
    rope = big("rope", [P, 2, T], F32, 72)
    score = plan.tile("score", [P, 2, TT, T], F32, act_at)
    decay = plan.tile("decay", [P, RH, T], F32, act_at + 16 * KB)
    bn = plan.tile("bn", [P, RH * TT, 16], F32, act_at + 24 * KB)
    BN_MEAN, BN_VAR, BN_ROOT, BN_NEWTON, BN_RSTD = 6, 7, 8, 9, 12
    y_hi = big("y_hi", [P, VT, T], F32R, 0)
    y_lo = big("y_lo", [P, VT, T], F32R, 32)
    hid_hi = big("hid_hi", [P, HALF_TILES, T], F32R, 0)
    hid_lo = big("hid_lo", [P, HALF_TILES, T], F32R, 32)
    relu = big("relu", [P, 4, T], F32, 64)
    relu_sq = big("relu_sq", [P, 4, T], F32, 72)
    mix_b = big("mix_b", [P, TT, GC], F32, 72)
    gk = big("gk", [P, GH, T], F32, 0)
    gv = big("gv", [P, GH, T], F32, 16)
    gq = big("gq", [P, GH, T], F32, 32)
    gz = big("gz", [P, TT, D], F32, 48)
    neg_l_t = big("neg_l_t", [P, UNITS, P], F32, 64)
    w_t = big("w_t", [P, UNITS, P], F32, 64)
    pad = big("pad", [P, 4, CONV - 1 + T + 1], F32, 80)
    block_l = big("block_l", [P, BLOCK, BLOCK], F32, 88.25)
    block_x = big("block_x", [P, BLOCK, BLOCK], F32, 92.25)
    attn = big("attn", [P, UNITS, P], F32, 80)
    ba_hi = big("ba_hi", [P, KT, P], F32R, 32)
    ba_lo = big("ba_lo", [P, KT, P], F32R, 36)
    ba_t = big("ba_t", [P, T], F32, 40)
    ba_cols = big("ba_cols", [P, TT, 2 * GH], F32, 42)
    conv_rows = big("conv_rows", [CONV * 3 * KT, P], F32, 43)
    join_f = big("join_f", [P, 2, len(LEVELS), P], F32, 44)
    ba_raw = big("ba_raw", [P, KT, 2 * GH], F32, 96.25)
    col = big("col", [P, 13, UNITS], F32, 96.25)
    (BETA, G, GCUM, EXP_G, EXP_TOT, EXP_REST, SS_K, SS_Q, R_K, N_K, R_Q, S_U, S_V) = range(13)
    z_gain = big("z_gain", [P, P], F32, 97.875)
    join = big("join", [P, 2, len(LEVELS), P], U8, 98.375)
    conv_w = big("conv_w", [P, CONV, 3 * KT], F32, 98.875)
    head_rows = big("head_rows", [P, 4, GH], F32, 99.25)
    ct = plan.tile("ct", [P, 16, UNITS], F32, dump_at)
    inv_t = plan.tile("inv_t", [P, UNITS, P], F32, act_at)
    inv = plan.tile("inv", [P, UNITS // 2, P], F32, act_at + 16 * KB)
    half_prod = plan.tile("half_prod", [P, UNITS // 2, P], F32, act_at + 24 * KB)
    k_grown = plan.tile("k_grown", [P, UNITS // 2, P], F32, act_at + 24 * KB)
    state = plan.tile("state", [P, GH, P], F32, act_at + 16 * KB)
    o_sq = plan.tile("o_sq", [P, GH, P], F32, act_at + 20 * KB)
    v_new = plan.tile("v_new", [P, GH, P], F32, act_at + 24 * KB)
    tmp = plan.tile("tmp", [P, 4, T], F32, gains_at)
    on = plan.tile("on", [P, TT, 6, GH], F32, dump_at)
    tall = lambda b: b[:, :].rearrange("p (k t) -> p k t", k=4)

    count = [0, 0, 0]

    def take(groups, chunks):
        was = tuple(count)
        for n, more in enumerate((groups, groups * chunks, groups * (chunks - 1))):
            count[n] += more
        return was

    def take_mlp():
        return [(take(4, 2), take(2, 4)) for _ in range(2)]

    RET_QK, RET_V, RET_G, RET_OUT = take(4, 2), take(4, 2), take(4, 2), take(2, 4)
    MLP = [take_mlp()]
    GDN_K, GDN_V, GDN_Q, GDN_Z, GDN_OUT = (take(2, 2) for _ in range(5))
    MLP.append(take_mlp())
    CHUNKS = count[1]
    NEXT_GROUP = [0, MLP[0][0][0][0], GDN_K[0], MLP[1][0][0][0], count[0]]
    GAIN_ROWS = [(None, (0, 0)), ((0, 1), (0, 2)), ((0, 3), (1, 0)), ((1, 1), (1, 2)), ((1, 3), None)]
    GAINS_LANDED = [16, 48, 80, 112, 128]

    with ExitStack() as ctx:
        bank = [ctx.enter_context(nc.psum_tensor(f"bank{n}", [P, T], F32)) for n in range(8)]
        sems = {}

        def sem(name):
            if name not in sems:
                sems[name] = ctx.enter_context(nc.semaphore(name))
            return sems[name]

        class Chain:

            def __init__(self, eng, name):
                self.eng, self.sem, self.n = eng, sem(name), 0

            def link(self, ins):
                self.n += 1
                ins.then_inc(self.sem, 1)
                self.eng.wait_ge(self.sem, self.n)

        w_landed = [sem("w_landed0"), sem("w_landed1")]
        w_high = sem("w_high")
        w_ready = sem("w_ready")
        chunk_used = sem("chunk_used")
        bank_full = sem("bank_full")
        emptied = sem("emptied")

        block = ctx.enter_context(nc.Block())

        @block.sync
        def _(sp):
            def stream(start, groups, w, chunks, col0=0):
                c0 = start[1]
                rows = w.rearrange("(k p) n -> p k n", p=P)

                def load(g, j, cols):
                    if c0 or not isinstance(g, int):
                        sp.wait_ge(w_ready, g * chunks + (c0 + j - 1))
                    sp.dma_start(w_raw[:, j % 2, :, :], rows[:, j * CK:(j + 1) * CK, cols])\
                        .then_inc(w_landed[j % 2], 16)

                if c0 == 0:
                    for j in range(2):
                        load(0, j, slice(col0, col0 + GC))
                with sp.Fori(0 if c0 else 1, groups) as g:
                    cols = bass.ds(sp.snap(g * GC + col0), GC)
                    for j in range(chunks):
                        load(g, j, cols)

            def stream_mlp(layer):
                for half, (up, down) in enumerate(MLP[layer]):
                    stream(up, 4, mlp_w_up[layer], 2, half * FF // 2)
                    stream(down, 2, mlp_w_down[layer, half * FF // 2:(half + 1) * FF // 2, :], 4)

            for m in range(TT):
                sp.dma_start(resid[:, m, :], x[0, m * P:(m + 1) * P, :]).then_inc(sem(f"x_landed{m}"), 16)
            stream(RET_QK, 12, ret_w_in[0], 2)
            stream(RET_OUT, 2, ret_w_out[0], 4)
            sp.dma_start(ba_raw[:, :, :], gdn_w_in[0].rearrange("(k p) n -> p k n", p=P)[:, :, 4 * D:GDN_IN])\
                .then_inc(sem("ba_landed"), 16)
            stream_mlp(0)
            for start, first in ((GDN_K, D), (GDN_V, 2 * D), (GDN_Q, 0), (GDN_Z, 3 * D)):
                stream(start, 2, gdn_w_in[0], 2, first)
            stream(GDN_OUT, 2, gdn_w_out[0], 2)
            stream_mlp(1)

        @block.gpsimd
        def _(pool):
            def low_parts(first, last):
                with pool.Fori(first // 2, last // 2) as i:
                    for s in range(2):
                        pool.wait_ge(w_high, i * 2 + (s + 1))
                        nc.gpsimd.tensor_tensor(w_lo[:, s, :, :], w_raw[:, s, :, :], w_hi[:, s, :, :].bitcast(F32),
                                                ALU.subtract).then_inc(w_ready, 1)

            low_parts(0, GDN_OUT[1])
            pool.wait_ge(w_high, GDN_OUT[1] + 1)
            nc.gpsimd.tensor_tensor(w_lo[:, 0, :, :], w_raw[:, 0, :, :], w_hi[:, 0, :, :].bitcast(F32),
                                    ALU.subtract).then_inc(w_ready, 1)
            pool.wait_ge(emptied, 4 * GDN_OUT[0])
            pool.memset(inv_t[:, :, :], 0.0).then_inc(sem("inv_cleared"), 1)
            for h in range(GH):
                pool.wait_ge(sem("row_exped"), h + 1)
                pool.wait_ge(sem("unit_prods"), h + 1)
                nc.gpsimd.tensor_tensor(gq[:, h, :], gq[:, h, :], tmp[:, 2 + h % 2, :], ALU.mult)\
                    .then_inc(sem("q_grown"), 1)
            for p in range(2):
                for m in range(TT):
                    z = gz[:, m, p * GC:(p + 1) * GC].rearrange("p (h e) -> p h e", h=4)
                    nc.gpsimd.tensor_tensor(z, z, z_gain[:, :].rearrange("p (o e) -> p o e", o=1)
                                            .broadcast_to([P, 4, P]), ALU.mult).then_inc(sem("z_gained"), 1)
            pool.wait_ge(sem("z_gained"), 2 * TT)
            units = gv[:, :, :].rearrange("p h (n e) -> p h n e", n=TT)
            for n in range(TT):
                pool.wait_ge(sem("o_scaled"), n + 1)
                nc.gpsimd.tensor_tensor(units[:, :, n, :], units[:, :, n, :],
                                        gz[:, n, :].rearrange("p (h e) -> p h e", h=GH), ALU.mult)\
                    .then_inc(sem("o_gated"), 1)
            pool.wait_ge(w_high, GDN_OUT[1] + 2)
            nc.gpsimd.tensor_tensor(w_lo[:, 1, :, :], w_raw[:, 1, :, :], w_hi[:, 1, :, :].bitcast(F32),
                                    ALU.subtract).then_inc(w_ready, 1)
            low_parts(GDN_OUT[1] + 2, CHUNKS)

        @block.tensor
        def _(pe):
            def three(dst, sta_hi, sta_lo, mov_hi, mov_lo, first, last):
                pe.matmul(dst, sta_hi, mov_hi, start=first, stop=False)
                pe.matmul(dst, sta_hi, mov_lo, start=False, stop=False)
                return pe.matmul(dst, sta_lo, mov_hi, start=False, stop=last)

            def group(c, parity, chunks, features_out, a_hi, a_lo, aside={}, tiles=None):
                for j in range(chunks):
                    if tiles is not None:
                        pe.wait_ge(sem("hid_low"), tiles + CK * (j + 1))
                    pe.wait_ge(w_ready, c + (j + 1))
                    s = j % 2
                    for m in range(4):
                        dst, mm = bank[4 * parity + m][:, :], slice(m * P, (m + 1) * P)
                        for kt in range(CK):
                            k = j * CK + kt
                            ends = (k == 0, k == chunks * CK - 1)
                            if features_out:
                                done = three(dst, w_hi[:, s, kt, mm], w_lo[:, s, kt, mm],
                                             a_hi[:, k, :], a_lo[:, k, :], *ends)
                            else:
                                done = three(dst, a_hi[:, k, mm], a_lo[:, k, mm],
                                             w_hi[:, s, kt, :], w_lo[:, s, kt, :], *ends)
                        if j == chunks - 1:
                            done.then_inc(bank_full, 1)
                        elif m == 3:
                            done.then_inc(chunk_used, 1)
                        if (j, m) in aside:
                            aside[j, m]()

            def groups(start, n, chunks, features_out, a_hi, a_lo):
                g0, c0, _ = start
                if g0:
                    pe.wait_ge(emptied, 4 * (g0 - 1))

                def pair(i):
                    group(i * (2 * chunks) + c0, 0, chunks, features_out, a_hi, a_lo)
                    if g0 or i:
                        pe.wait_ge(emptied, i * 8 + 4 * g0)
                    group(i * (2 * chunks) + (c0 + chunks), 1, chunks, features_out, a_hi, a_lo)

                if n == 2 or not g0:
                    for i in range(n // 2):
                        if i:
                            pe.wait_ge(emptied, i * 8 + 4 * (g0 - 1))
                        pair(i)
                    return
                with pe.Fori(0, n // 2) as i:
                    pair(i)
                    pe.wait_ge(emptied, i * 8 + 4 * (g0 + 1))

            def transpose_acts(b):
                if b:
                    pe.wait_ge(emptied, 4 * (NEXT_GROUP[b] - 1))
                for m in range(TT):
                    pe.wait_ge(sem("normed"), TT * b + m + 1)
                    if m >= 2:
                        pe.wait_ge(sem("act_low"), 2 * (TT * b + m - 1))
                    for k in range(KT):
                        done = pe.transpose(bank[2 * (m % 2) + k // 4][:, k % 4 * P:(k % 4 + 1) * P],
                                            normed[:, m % 2, k * P:(k + 1) * P], ident)
                    done.then_inc(sem("acts_transposed"), 1)
                pe.wait_ge(sem("act_low"), 2 * TT * (b + 1))

            def retention():
                pe.wait_ge(emptied, 4 * RET_OUT[0])
                pe.wait_ge(sem("roped"), KT)

                def scores(h):
                    if h:
                        pe.wait_ge(sem("decayed"), TT * h)
                    for i in range(TT):
                        for d in range(2):
                            done = pe.matmul(bank[i][:, 0:T - i * P], qk_t[:, KT + 2 * h + d, i * P:(i + 1) * P],
                                             qk_t[:, 2 * h + d, i * P:T], start=d == 0, stop=d == 1)
                        done.then_inc(sem("scored"), 1)

                scores(0)
                for h in range(RH):
                    if h + 1 < RH:
                        scores(h + 1)
                    else:
                        pe.wait_ge(sem("decayed"), TT * RH)
                    for j in range(TT):
                        if h:
                            pe.wait_ge(sem("y_gated"), TT * (h - 1) + j + 1)
                        for i in range(j + 1):
                            done = pe.matmul(bank[4 + j][:, :], score[:, h % 2, i, j * P:(j + 1) * P],
                                             v_tm[:, i, h * RV:(h + 1) * RV], start=i == 0, stop=i == j)
                        done.then_inc(sem("attended"), 1)
                for n in range(RH * TT):
                    h, m = n // TT, n % TT
                    pe.wait_ge(sem("y_scaled"), n + 1)
                    pe.wait_ge(sem("y_gated"), min(n + 9, RH * TT) if n < 8 else RH * TT)
                    if n >= 8:
                        pe.wait_ge(sem("y_low"), n - 7)
                    for f in range(4):
                        done = pe.transpose(bank[n % 8][:, f * P:(f + 1) * P],
                                            gate[:, m, h * RV + f * P:h * RV + (f + 1) * P], ident)
                    done.then_inc(sem("y_transposed"), 1)
                pe.wait_ge(sem("y_low"), RH * TT)

            def mlp(layer):
                for half, (up, down) in enumerate(MLP[layer]):
                    groups(up, 4, 2, True, act_hi, act_lo)
                    g0, c0, _ = down
                    for p in range(2):
                        pe.wait_ge(emptied, 4 * (g0 + p - 1))
                        group(c0 + 4 * p, p, 4, False, hid_hi, hid_lo,
                              tiles=HALF_TILES * (2 * layer + half) if p == 0 else None)

            def unit(t, u):
                return t[:, u // TT, u % TT * P:(u % TT + 1) * P]

            def drained(gi):
                if gi == 1:
                    pe.wait_ge(sem("kq_squared"), GH)
                    pe.wait_ge(sem("g_sums_read"), 2)
                if gi in (2, 3):
                    pe.wait_ge(sem("triangled"), 4 * (gi - 1))
                if gi == 4:
                    pe.wait_ge(sem("v_turned_out"), GH)
                if gi == 5:
                    pe.wait_ge(sem("kq_squared"), 2 * GH)

            def turn(src, h, b, done):
                for n in range(TT):
                    last = pe.transpose(bank[b][:, n * P:(n + 1) * P], src[:, h, n * P:(n + 1) * P], ident)
                last.then_inc(sem(done), 1)

            def turn_k(first):
                pe.wait_ge(emptied, 4 * GDN_V[0])
                pe.wait_ge(sem("silued"), first + 4)
                for i in range(4):
                    if first:
                        pe.wait_ge(sem("kq_squared"), i + 1)
                        if i == 3:
                            pe.wait_ge(sem("g_sums_read"), 2)
                    turn(gk, first + i, 4 + i, "kq_turned")

            def turn_q(first):
                pe.wait_ge(emptied, 4 * GDN_Z[0])
                pe.wait_ge(sem("silued"), 2 * GH + first + 4)
                for i in range(4):
                    if first:
                        pe.wait_ge(sem("kq_squared"), GH + i + 1)
                    turn(gq, first + i, 4 + i, "kq_turned")

            def turn_v(first):
                pe.wait_ge(emptied, 4 * (GDN_Q[0] + 1))
                pe.wait_ge(sem("silued"), GH + first + 4)
                for i in range(4):
                    if first:
                        pe.wait_ge(sem("v_turned_out"), i + 1)
                    turn(gv, first + i, i, "v_turned")

            def sum_g():
                pe.wait_ge(sem("g_made"), 1)
                pe.wait_ge(sem("kq_squared"), 4)
                pe.matmul(bank[7][:, 0:UNITS], tri, col[:, G, :], start=True, stop=True)
                pe.matmul(bank[7][:, UNITS:2 * UNITS], ones, col[:, G, :], start=True, stop=True)\
                    .then_inc(sem("g_summed"), 1)

            def row_sums(h, b):
                for n in range(TT):
                    g = col[:, G, h * TT + n:h * TT + n + 1].broadcast_to([P, P])
                    done = pe.matmul(bank[b][:, n * P:(n + 1) * P], g, tri, start=True, stop=True)
                return done

            def products(h, b, other):
                for n in range(TT):
                    done = pe.matmul(bank[b][:, n * P:(n + 1) * P], gk[:, h, n * P:(n + 1) * P],
                                     other[:, h, n * P:(n + 1) * P], start=True, stop=True)
                return done

            def triangles(first):
                g = GDN_V[0] + 1 + first // 4
                pe.wait_ge(emptied, 4 * g)
                if first % 4:
                    pe.wait_ge(sem("triangled"), first)
                for i in range(2):
                    b = (0 if first < 4 else 4) + 2 * i
                    row_sums(first + i, b).then_inc(sem("tri_rows"), 1)
                    products(first + i, b + 1, gk).then_inc(sem("tri_prods"), 1)

            def delta_projections():
                g0, c0, _ = GDN_K
                pe.wait_ge(emptied, 4 * g0)
                pe.wait_ge(sem("ba_low"), 1)
                for k in range(KT):
                    done = three(bank[4][:, :], ba_hi[:, k, :], ba_lo[:, k, :], act_hi[:, k, :], act_lo[:, k, :],
                                 k == 0, k == KT - 1)
                done.then_inc(sem("ba_full"), 1)
                group(c0, 0, 2, True, act_hi, act_lo)
                pe.wait_ge(sem("ba_out"), 1)
                pe.wait_ge(sem("conv_rows_landed"), 16)
                for n in range(TT):
                    pe.transpose(bank[5][:, n * P:(n + 1) * P], ba_t[:, n * P:(n + 1) * P], ident)
                rows = CONV * 3 * KT
                pe.transpose(bank[6][:, 0:rows], conv_rows[:, :], ident[0:rows, 0:rows]).then_inc(sem("small_turned"), 1)
                pe.wait_ge(sem("small_out"), 2)
                group(c0 + 2, 1, 2, True, act_hi, act_lo)
                for gi, (start, features_out, aside) in enumerate((
                        (GDN_V, True, {(0, 1): lambda: turn_k(0), (0, 3): sum_g, (1, 1): lambda: turn_k(4)}),
                        (GDN_V, True, {(0, 1): lambda: triangles(0), (1, 1): lambda: triangles(2)}),
                        (GDN_Q, True, {(0, 1): lambda: triangles(4), (1, 1): lambda: triangles(6)}),
                        (GDN_Q, True, {(0, 1): lambda: turn_v(0), (1, 1): lambda: turn_v(4)}),
                        (GDN_Z, False, {(0, 1): lambda: turn_q(0), (1, 1): lambda: turn_q(4)}),
                        (GDN_Z, False, {}))):
                    p = gi % 2
                    pe.wait_ge(emptied, 4 * (start[0] + p - 1))
                    drained(gi)
                    group(start[1] + 2 * p, p, 2, features_out, act_hi, act_lo, aside)

            def delta_rule():
                pe.wait_ge(emptied, 4 * GDN_OUT[0])
                for h in range(GH):
                    if h >= 2:
                        pe.wait_ge(sem("row_exped"), h - 1)
                    row_sums(h, 4 + h % 2).then_inc(sem("row_made"), 1)
                    if h >= 2:
                        pe.wait_ge(sem("unit_scaled"), h - 1)
                        pe.wait_ge(sem("k_turned_out"), h - 1)
                    products(h, 2 + h % 2, gq).then_inc(sem("unit_prods"), 1)
                    turn(gk, h, 6 + h % 2, "k_turned")
                pe.wait_ge(sem("row_exped"), GH)
                pe.wait_ge(sem("unit_scaled"), GH)
                pe.wait_ge(sem("k_turned_out"), GH)
                n_p = n_second = 0
                pe.wait_ge(sem("inv_seeded"), P // BLOCK)
                for batch in range(2):
                    heads = range(4 * batch, 4 * batch + 4)
                    for r, h in enumerate(heads):
                        for n in range(TT):
                            done = pe.transpose(bank[r][:, n * P:(n + 1) * P], inv_t[:, h * TT + n, :], ident)
                        done.then_inc(sem("inv_turned"), 1)
                    for level in range(len(LEVELS)):
                        for r, h in enumerate(heads):
                            if level == 0:
                                pe.wait_ge(sem("inv_placed"), h + 1)
                            else:
                                pe.wait_ge(sem("joined"), n_second - 4 + r + 1)
                            for n in range(TT):
                                u = h * TT + n
                                done = pe.matmul(bank[r][:, n * P:(n + 1) * P], neg_l_t[:, u, :],
                                                 inv[:, u - batch * UNITS // 2, :], start=True, stop=True)
                            done.then_inc(sem("prod_made"), 1)
                        for r, h in enumerate(heads):
                            n_p += 1
                            pe.wait_ge(sem("prod_out"), n_p)
                            if n_second >= 2:
                                pe.wait_ge(sem("joined"), n_second - 1)
                            for n in range(TT):
                                u = h * TT + n
                                v = u - batch * UNITS // 2
                                cols = slice(n * P, (n + 1) * P)
                                if level < len(LEVELS) - 1:
                                    pe.matmul(bank[4 + r % 2 * 2][:, cols], inv_t[:, u, :], half_prod[:, v, :],
                                              start=True, stop=True)
                                done = pe.matmul(bank[5 + r % 2 * 2][:, cols], half_prod[:, v, :], inv_t[:, u, :],
                                                 start=True, stop=True)
                            done.then_inc(sem("seconds_made"), 1)
                            n_second += 1
                    for r, h in enumerate(heads):
                        pe.wait_ge(sem("k_grown"), h + 1)
                        pe.wait_ge(sem("joined"), n_second - 4 + r + 1)
                        for n in range(TT):
                            u = h * TT + n
                            done = pe.matmul(bank[r][:, n * P:(n + 1) * P], k_grown[:, u - batch * UNITS // 2, :],
                                             inv_t[:, u, :], start=True, stop=True)
                        done.then_inc(sem("w_made"), 1)
                    for r, h in enumerate(heads):
                        pe.wait_ge(sem("w_out"), h + 1)
                for n in range(TT):
                    for q in range(2):
                        if n:
                            pe.wait_ge(sem("state_made"), 2 * (n - 1) + q + 1)
                            pe.wait_ge(sem("v_new_made"), 2 * (n - 1) + q + 1)
                        for r in range(4):
                            h = 4 * q + r
                            u = h * TT + n
                            cols = slice(r * P, (r + 1) * P)
                            done = pe.matmul(bank[q][:, cols], inv_t[:, u, :], unit(gv, u), start=True, stop=n == 0)
                            if n:
                                done = pe.matmul(bank[q][:, cols], w_t[:, u, :], state[:, h, :], start=False, stop=True)
                        done.then_inc(sem("v_new_full"), 1)
                    for q in range(2):
                        pe.wait_ge(sem("v_new_made"), 2 * n + q + 1)
                        if n:
                            pe.wait_ge(sem("o_out"), 2 * (n - 1) + q + 1)
                        else:
                            pe.wait_ge(sem("q_grown"), GH)
                        for r in range(4):
                            h = 4 * q + r
                            u = h * TT + n
                            cols = slice(r * P, (r + 1) * P)
                            if n:
                                pe.matmul(bank[2 + q][:, cols], unit(gq, u), state[:, h, :], start=True, stop=False)
                            done = pe.matmul(bank[2 + q][:, cols], attn[:, u, :], v_new[:, h, :],
                                             start=n == 0, stop=True)
                        done.then_inc(sem("o_full"), 1)
                        if n == TT - 1:
                            continue
                        pe.wait_ge(sem("k_faded"), 4 * q + 4)
                        for r in range(4):
                            h = 4 * q + r
                            done = pe.matmul(bank[4 + q][:, r * P:(r + 1) * P], unit(gk, h * TT + n), v_new[:, h, :],
                                             start=True, stop=True)
                        done.then_inc(sem("state_full"), 1)
                pe.wait_ge(sem("o_gated"), TT)
                for n in range(TT):
                    for h in range(GH):
                        done = pe.transpose(bank[2 * n + h // 4][:, h % 4 * P:(h % 4 + 1) * P],
                                            unit(gv, h * TT + n), ident)
                    done.then_inc(sem("o_turned"), 1)
                pe.wait_ge(sem("o_low"), 2 * TT)

            pe.wait_ge(sem("const_landed"), 16)
            transpose_acts(0)
            groups(RET_QK, 4, 2, True, act_hi, act_lo)
            groups(RET_V, 8, 2, False, act_hi, act_lo)
            retention()
            groups(RET_OUT, 2, 4, False, y_hi, y_lo)
            transpose_acts(1)
            mlp(0)
            transpose_acts(2)
            delta_projections()
            delta_rule()
            groups(GDN_OUT, 2, 2, False, act_hi, act_lo)
            transpose_acts(3)
            mlp(1)

        @block.scalar
        def _(act):
            chain = Chain(act, "act_step")

            def high(slot):
                act.activation(w_hi[:, slot, :, :], w_raw[:, slot, :, :], ACT.Copy).then_inc(w_high, 1)

            def splits(start, i, chunks, first=1, last=None):
                g0, c0, u0 = start
                for j in range(first, (last or chunks) + 1):
                    act.wait_ge(w_landed[j % 2], i * (8 * chunks) + 16 * ((c0 + j) // 2 + 1))
                    if j == 1:
                        if g0 or not isinstance(i, int) or i:
                            act.wait_ge(bank_full, i * 4 + 4 * g0)
                    else:
                        act.wait_ge(chunk_used, i * (chunks - 1) + (u0 + j - 1))
                    high(j % 2)

            def empty(start, i, p, m, dst, func=ACT.Copy):
                act.wait_ge(bank_full, i * 4 + (4 * start[0] + m + 1))
                act.activation(dst, bank[4 * p + m][:, :], func).then_inc(emptied, 1)

            def load_gains(b):
                for n, row in enumerate(GAIN_ROWS[b]):
                    if row is not None:
                        act.dma_start(gains[:, n, :], norm_gains[row[0], row[1], :].partition_broadcast(P))\
                            .then_inc(sem("gains_landed"), 16)

            def sum_squares(src, m, where):
                chain.link(act.activation(dump[:, :], src, ACT.Square, accum_out=stat[:, where, m:m + 1]))

            def root(m, ss, to, done):
                act.activation(stat[:, to, m:m + 1], stat[:, ss, m:m + 1], ACT.Sqrt, scale=1.0 / D, bias=eps)\
                    .then_inc(sem(done), 1)

            def high_acts(b, m):
                act.wait_ge(sem("acts_transposed"), TT * b + m + 1)
                for half in range(2):
                    act.activation(act_hi[:, 4 * half:4 * half + 4, m * P:(m + 1) * P],
                                   tall(bank[2 * (m % 2) + half]), ACT.Copy).then_inc(sem("act_high"), 1)

            def norms(b, before):
                for m in range(TT + 2):
                    if m < TT:
                        before(m)
                        if b:
                            sum_squares(mix[:, m, :], m, SS_MIX)
                            root(m, SS_MIX, ROOT_MIX, "mix_rooted")
                    if 1 <= m <= TT and b < 4:
                        if b:
                            act.wait_ge(sem("residual_done"), TT * (b - 1) + m)
                        sum_squares(resid[:, m - 1, :], m - 1, SS_RES)
                        root(m - 1, SS_RES, ROOT_RES, "resid_rooted")
                    if m >= 2 and b < 4:
                        high_acts(b, m - 2)

            act.dma_start(square[:, :, :], square_c).then_inc(sem("const_landed"), 16)
            load_gains(0)
            act.dma_start(rope[:, :, :], rope_c).then_inc(sem("rope_landed"), 16)
            act.wait_ge(sem("eps_set"), 1)

            def before_input(m):
                act.wait_ge(sem(f"x_landed{m}"), 16)

            norms(0, before_input)
            act.wait_ge(w_landed[0], 16)
            high(0)
            act.wait_ge(sem("normed"), TT)
            act.dma_start(gains[:, :, :].rearrange("p a n -> p (a n)"), ret_gn_gain[0].partition_broadcast(P))\
                .then_inc(sem("gn_gain_landed"), 16)

            for i in range(4):
                splits(RET_QK, i, 2)
                for m in range(4):
                    empty(RET_QK, i, i % 2, m, qk_t[:, 4 * i + m, :])
            with act.Fori(0, 2) as i2:
                for p in range(2):
                    i = i2 * 2 + p
                    splits(RET_V, i, 2)
                    for m in range(4):
                        empty(RET_V, i, p, m, v_tm[:, m, bass.ds(i * GC, GC)])
            act.wait_ge(sem("roped"), KT)
            with act.Fori(0, 2) as i2:
                for p in range(2):
                    i = i2 * 2 + p
                    splits(RET_G, i, 2)
                    for m in range(4):
                        empty(RET_G, i, p, m, gate[:, m, bass.ds(i * GC, GC)], ACT.Silu)
            act.dma_start(decay[:, :, :], decay_c).then_inc(sem("decay_landed"), 16)
            act.wait_ge(sem("gate_gained"), 4 * TT)
            load_gains(1)
            for n in range(RH * TT + 1):
                if n < RH * TT:
                    act.wait_ge(sem("varied"), n + 1)
                    act.activation(bn[:, n, BN_ROOT:BN_ROOT + 1], bn[:, n, BN_VAR:BN_VAR + 1], ACT.Sqrt, bias=eps)\
                        .then_inc(sem("gn_rooted"), 1)
                if n:
                    h, m = (n - 1) // TT, (n - 1) % TT
                    act.wait_ge(sem("gn_inverted"), n)
                    y = gate[:, m, h * RV:(h + 1) * RV]
                    act.activation(y, y, ACT.Copy, scale=bn[:, n - 1, BN_RSTD:BN_RSTD + 1])\
                        .then_inc(sem("y_scaled"), 1)
            for n in range(RH * TT):
                h, m = n // TT, n % TT
                act.wait_ge(sem("y_transposed"), n + 1)
                act.activation(y_hi[:, 4 * h:4 * h + 4, m * P:(m + 1) * P], tall(bank[n % 8]), ACT.Copy)\
                    .then_inc(sem("y_high"), 1)
            splits(RET_OUT, 0, 4)
            for m in range(TT):
                empty(RET_OUT, 0, 0, m, mix[:, m, 0:GC])
            splits(RET_OUT, 1, 4)

            def empty_last(start, m):
                empty(start, 1, 1, m, mix[:, m, GC:2 * GC])
                act.wait_ge(emptied, 4 * (start[0] + 1) + m + 1)

            norms(1, lambda m: empty_last(RET_OUT, m))

            def mlp(layer):
                b = 2 * layer + 2
                for half, (up, down) in enumerate(MLP[layer]):
                    with act.Fori(0, 2) as i2:
                        for p in range(2):
                            i = i2 * 2 + p
                            splits(up, i, 2)
                            for m in range(4):
                                empty(up, i, p, m, relu[:, m, :], ACT.Relu)
                            act.wait_ge(sem("squared"), i * 4 + (HALF_TILES * (2 * layer + half) + 4))
                    splits(down, 0, 4)
                    for m in range(TT):
                        empty(down, 0, 0, m, mix_b[:, m, :] if half else mix[:, m, 0:GC])
                    splits(down, 1, 4, last=3 if layer and half else None)
                    if half == 0:
                        for m in range(TT):
                            empty(down, 1, 1, m, mix[:, m, GC:2 * GC])

                def before(m):
                    act.wait_ge(sem("mix_summed"), 8 * layer + m + 1)
                    empty(MLP[layer][1][1], 1, 1, m, mix_b[:, m, :])
                    act.wait_ge(sem("mix_summed"), 8 * layer + 4 + m + 1)
                norms(b, before)

            act.wait_ge(sem("normed"), 2 * TT)
            load_gains(2)
            mlp(0)

            act.dma_start(conv_rows[:, :], gdn_conv_w[0].rearrange("j (k p) -> (j k) p", p=P))\
                .then_inc(sem("conv_rows_landed"), 16)
            act.dma_start(join_f[:, :, :, :], join_c).then_inc(sem("join_landed"), 16)
            act.dma_start(z_gain[:, :], gdn_norm_gain[0].partition_broadcast(P)).then_inc(sem("rows_landed"), 16)
            act.dma_start(head_rows[:, 0, :], gdn_dt_bias[0].partition_broadcast(P)).then_inc(sem("rows_landed"), 16)
            act.dma_start(head_rows[:, 1, :], gdn_a_log[0].partition_broadcast(P)).then_inc(sem("rows_landed"), 16)
            act.wait_ge(sem("ba_cleared"), 1)
            act.wait_ge(sem("ba_landed"), 16)
            act.activation(ba_hi[:, :, 0:2 * GH], ba_raw[:, :, :], ACT.Copy).then_inc(sem("ba_high"), 1)
            act.wait_ge(sem("ba_full"), 1)
            act.activation(ba_t[:, :], bank[4][:, :], ACT.Copy).then_inc(sem("ba_out"), 1)
            order = [(GDN_K, gk), (GDN_V, gv), (GDN_Q, gq)]

            def silu(gi):
                for m in range(4):
                    act.wait_ge(sem("convolved"), 4 * gi + m + 1)
                    t = order[gi // 2][1][:, gi % 2 * 4 + m, :]
                    act.activation(t, t, ACT.Silu).then_inc(sem("silued"), 1)

            def square_heads(first, last):
                for i in range(first, last):
                    act.wait_ge(sem("kq_turned"), i + 1)
                    slot = i % 4 if i < GH else i % 2
                    if 4 <= i < GH:
                        act.wait_ge(sem("kq_summed"), i - 3)
                    if i >= GH + 2:
                        act.wait_ge(sem("kq_summed"), i - 1)
                    act.activation(tmp[:, slot, :], bank[4 + i % 4][:, :], ACT.Square).then_inc(sem("kq_squared"), 1)

            def tri_exps(first):
                for h in (first, first + 1):
                    act.wait_ge(sem("tri_shifted"), h + 1)
                    act.activation(tmp[:, h % 2, :], tmp[:, h % 2, :], ACT.Exp).then_inc(sem("tri_exped"), 1)

            def v_out(first):
                for h in range(first, first + 4):
                    act.wait_ge(sem("v_turned"), h + 1)
                    act.wait_ge(sem("cols_k"), 1)
                    for n in range(TT):
                        u = h * TT + n
                        done = act.activation(gv[:, h, n * P:(n + 1) * P], bank[h % 4][:, n * P:(n + 1) * P],
                                              ACT.Copy, scale=col[:, N_K, u:u + 1])
                    done.then_inc(sem("v_turned_out"), 1)

            for gi in range(8):
                start, p = (order + [(GDN_Z, None)])[gi // 2][0], gi % 2
                splits(start, p, 2, last=1)
                if gi == 0:
                    act.wait_ge(sem("small_turned"), 1)
                    act.activation(ba_cols[:, :, :], tall(bank[5])[:, :, 0:2 * GH], ACT.Copy)\
                        .then_inc(sem("small_out"), 1)
                    rows = CONV * 3 * KT
                    act.activation(conv_w[:, :, :].rearrange("p j k -> p (j k)"), bank[6][:, 0:rows], ACT.Copy)\
                        .then_inc(sem("small_out"), 1)
                if gi == 1:
                    act.wait_ge(sem("cols_a"), 1)
                    act.activation(ct[:, 2:4, :], ct[:, 0:2, :], ACT.Exp).then_inc(sem("cols_b"), 1)
                    act.wait_ge(sem("rows_landed"), 48)
                    act.activation(head_rows[:, 2, :], head_rows[:, 1, :], ACT.Exp).then_inc(sem("cols_b"), 1)
                    act.wait_ge(sem("cols_c"), 1)
                    act.activation(ct[:, 6, :], ct[:, 5, :], ACT.Ln).then_inc(sem("cols_d"), 1)
                if gi == 2:
                    square_heads(0, 4)
                if gi == 5:
                    v_out(0)
                splits(start, p, 2, first=2)
                if gi == 2:
                    act.wait_ge(sem("g_summed"), 1)
                    act.activation(col[:, EXP_G, :], bank[7][:, 0:UNITS], ACT.Exp)
                    act.activation(col[:, EXP_TOT, :], bank[7][:, UNITS:2 * UNITS], ACT.Exp)\
                        .then_inc(sem("g_sums_read"), 1)
                    act.wait_ge(sem("rest_made"), 1)
                    act.activation(ct[:, 8, :], ct[:, 7, :], ACT.Exp).then_inc(sem("rest_exped"), 1)
                if gi in (3, 4):
                    tri_exps(4 * (gi - 3))
                if gi == 6:
                    square_heads(GH, GH + 4)
                if 1 <= gi <= 6:
                    silu(gi - 1)
                if gi == 2:
                    square_heads(4, GH)
                    act.wait_ge(sem("kq_x_made"), 1)
                    act.activation(ct[:, 2, :], ct[:, 0, :], ACT.Sqrt).then_inc(sem("kq_rooted"), 1)
                if gi in (3, 4):
                    tri_exps(4 * (gi - 3) + 2)
                if gi == 5:
                    v_out(4)
                if gi == 6:
                    square_heads(GH + 4, 2 * GH)
                for m in range(4):
                    if gi < 6:
                        if gi:
                            act.wait_ge(sem("convolved"), 4 * (gi - 1) + m + 1)
                        else:
                            act.wait_ge(sem("pad_cleared"), 1)
                        empty(start, p, p, m, pad[:, m, CONV - 1:CONV - 1 + T])
                    else:
                        empty(start, p, p, m, gz[:, m, p * GC:(p + 1) * GC], ACT.Silu)
                if gi == 7:
                    act.wait_ge(sem("kq_x_made"), 2)
                    act.activation(ct[:, 3, :], ct[:, 1, :], ACT.Sqrt).then_inc(sem("kq_rooted"), 1)
            act.wait_ge(sem("blocks_done"), 1)
            for h in range(GH):
                act.wait_ge(sem("row_shifted"), h + 1)
                if h >= 2:
                    act.wait_ge(sem("q_grown"), h - 1)
                act.activation(tmp[:, 2 + h % 2, :], bank[4 + h % 2][:, :], ACT.Exp).then_inc(sem("row_exped"), 1)
                act.activation(tmp[:, h % 2, :], tmp[:, h % 2, :], ACT.Exp).then_inc(sem("decay_made"), 1)
                act.wait_ge(sem("k_turned"), h + 1)
                act.activation(gk[:, h, :], bank[6 + h % 2][:, :], ACT.Copy).then_inc(sem("k_turned_out"), 1)
            act.wait_ge(sem("q_grown"), GH)
            act.wait_ge(sem("unit_scaled"), GH)
            load_gains(3)
            n_p = 0
            for batch in range(2):
                heads = range(4 * batch, 4 * batch + 4)
                for r, h in enumerate(heads):
                    act.wait_ge(sem("inv_turned"), h + 1)
                    act.activation(inv[:, 4 * r:4 * r + 4, :], tall(bank[r]), ACT.Copy).then_inc(sem("inv_placed"), 1)
                for level in range(len(LEVELS)):
                    for r in range(4):
                        n_p += 1
                        act.wait_ge(sem("prod_made"), n_p)
                        act.activation(half_prod[:, 4 * r:4 * r + 4, :], tall(bank[r]), ACT.Copy)\
                            .then_inc(sem("prod_out"), 1)
                for r, h in enumerate(heads):
                    act.wait_ge(sem("w_made"), h + 1)
                    act.activation(w_t[:, h * TT:(h + 1) * TT, :], tall(bank[r]), ACT.Copy, scale=-1.0)\
                        .then_inc(sem("w_out"), 1)
            outs = gv[:, :, :].rearrange("p h (n e) -> p h n e", n=TT)
            for n in range(TT):
                act.wait_ge(sem("o_out"), 2 * n + 2)
                if n:
                    act.wait_ge(sem("o_summed"), n)
                act.activation(o_sq[:, :, :], outs[:, :, n, :], ACT.Square).then_inc(sem("o_squared"), 1)
                act.wait_ge(sem("o_summed"), n + 1)
                act.activation(on[:, n, 1, :], on[:, n, 0, :], ACT.Sqrt, scale=1.0 / P, bias=eps)\
                    .then_inc(sem("o_rooted"), 1)
            for n in range(TT):
                act.wait_ge(sem("o_turned"), n + 1)
                for half in range(2):
                    act.activation(act_hi[:, 4 * half:4 * half + 4, n * P:(n + 1) * P], tall(bank[2 * n + half]),
                                   ACT.Copy).then_inc(sem("o_high"), 1)
            splits(GDN_OUT, 0, 2)
            for m in range(TT):
                empty(GDN_OUT, 0, 0, m, mix[:, m, 0:GC])
            splits(GDN_OUT, 1, 2)
            norms(3, lambda m: empty_last(GDN_OUT, m))
            act.wait_ge(sem("normed"), 4 * TT)
            load_gains(4)
            mlp(1)
            for m in range(TT):
                act.wait_ge(sem("residual_done"), 3 * TT + m + 1)
                act.dma_start(out[0, m * P:(m + 1) * P, :], resid[:, m, :]).then_inc(sem("stored"), 16)
            act.wait_ge(sem("stored"), 16 * TT)

        @block.vector
        def _(dve):
            chain = Chain(dve, "dve_step")
            link = chain.link

            def inv_root(x, root, temp, out_, scale=1.0, add=EPS):
                t = [temp(n) for n in range(3)]
                dve.tensor_scalar(t[0], x, scale, add, ALU.mult, ALU.add)
                link(dve.reciprocal(t[1], root))
                link(dve.tensor_tensor(t[2], t[0], t[1], ALU.mult))
                link(dve.tensor_tensor(t[2], t[2], t[1], ALU.mult))
                link(dve.tensor_scalar(t[2], t[2], -0.5, 1.5, ALU.mult, ALU.add))
                return dve.tensor_tensor(out_, t[1], t[2], ALU.mult)

            def norms(b, before=None):
                def col_of(n, m):
                    return stat[:, n, m:m + 1]
                if b:
                    dve.wait_ge(sem("gains_landed"), GAINS_LANDED[b])
                for m in range(TT + 2):
                    if m < TT and b:
                        if before:
                            before(m)
                        dve.wait_ge(sem("mix_rooted"), TT * (b - 1) + m + 1)
                        link(inv_root(col_of(SS_MIX, m), col_of(ROOT_MIX, m), lambda n: col_of(NEWTON + n, m),
                                      col_of(RSTD_MIX, m), 1.0 / D))
                        link(dve.scalar_tensor_tensor(mix[:, m, :], mix[:, m, :], col_of(RSTD_MIX, m), gains[:, 0, :],
                                                      ALU.mult, ALU.mult))
                        dve.tensor_tensor(resid[:, m, :], resid[:, m, :], mix[:, m, :], ALU.add)\
                            .then_inc(sem("residual_done"), 1)
                    if 1 <= m <= TT and b < 4:
                        if b == 0 and m == 1:
                            dve.wait_ge(sem("gains_landed"), GAINS_LANDED[0])
                        if b:
                            dve.wait_ge(sem("residual_done"), TT * (b - 1) + m)
                        dve.wait_ge(sem("resid_rooted"), TT * b + m)
                        link(inv_root(col_of(SS_RES, m - 1), col_of(ROOT_RES, m - 1),
                                      lambda n: col_of(NEWTON + n, m - 1), col_of(RSTD_RES, m - 1), 1.0 / D))
                        if TT * b + m > 2:
                            dve.wait_ge(sem("acts_transposed"), TT * b + m - 2)
                        dve.scalar_tensor_tensor(normed[:, (m - 1) % 2, :], resid[:, m - 1, :], col_of(RSTD_RES, m - 1),
                                                 gains[:, 1, :], ALU.mult, ALU.mult).then_inc(sem("normed"), 1)
                    if m >= 2 and b < 4:
                        t = m - 2
                        for half in range(2):
                            dve.wait_ge(sem("act_high"), 2 * (TT * b + t) + half + 1)
                            where = (slice(None), slice(4 * half, 4 * half + 4), slice(t * P, (t + 1) * P))
                            dve.tensor_tensor(act_lo[where], tall(bank[2 * (t % 2) + half]), act_hi[where].bitcast(F32),
                                              ALU.subtract).then_inc(sem("act_low"), 1)

            dve.memset(stat[:, :, :], EPS).then_inc(sem("eps_set"), 1)
            dve.wait_ge(sem("eps_set"), 1)
            norms(0)

            dve.wait_ge(sem("rope_landed"), 16)
            cos, sin = rope[:, 0, :], rope[:, 1, :]
            for n in range(KT):
                dve.wait_ge(emptied, 2 * n + 2)
                x1, x2 = qk_t[:, 2 * n, :], qk_t[:, 2 * n + 1, :]
                dve.tensor_tensor(rope_tmp[:, 0, :], x1, cos, ALU.mult)
                dve.tensor_tensor(rope_tmp[:, 1, :], x2, sin, ALU.mult)
                dve.tensor_tensor(rope_tmp[:, 2, :], x1, sin, ALU.mult)
                link(dve.tensor_tensor(rope_tmp[:, 3, :], x2, cos, ALU.mult))
                dve.tensor_tensor(x1, rope_tmp[:, 0, :], rope_tmp[:, 1, :], ALU.subtract)
                dve.tensor_tensor(x2, rope_tmp[:, 2, :], rope_tmp[:, 3, :], ALU.add).then_inc(sem("roped"), 1)
                dve.wait_ge(sem("roped"), n + 1)
            dve.wait_ge(sem("gn_gain_landed"), 16)
            with dve.Fori(0, 4) as i:
                for m in range(TT):
                    dve.wait_ge(emptied, i * 4 + (4 * RET_G[0] + m + 1))
                    g = gate[:, m, bass.ds(i * GC, GC)]
                    dve.tensor_tensor(g, g, gains[:, :, :].rearrange("p a n -> p (a n)")[:, bass.ds(i * GC, GC)],
                                      ALU.mult).then_inc(sem("gate_gained"), 1)
            dve.wait_ge(sem("gate_gained"), 4 * TT)
            dve.wait_ge(sem("decay_landed"), 16)

            def decayed(h):
                for i in range(TT):
                    dve.wait_ge(sem("scored"), TT * h + i + 1)
                    if h >= 2:
                        dve.wait_ge(sem("attended"), TT * (h - 1))
                    dve.tensor_tensor(score[:, h % 2, i, i * P:T], bank[i][:, 0:T - i * P],
                                      decay[:, h, 0:T - i * P], ALU.mult).then_inc(sem("decayed"), 1)

            def inverted(n):
                dve.wait_ge(sem("gn_rooted"), n + 1)
                inv_root(bn[:, n, BN_VAR:BN_VAR + 1], bn[:, n, BN_ROOT:BN_ROOT + 1],
                         lambda t: bn[:, n, BN_NEWTON + t:BN_NEWTON + t + 1], bn[:, n, BN_RSTD:BN_RSTD + 1])\
                    .then_inc(sem("gn_inverted"), 1)

            decayed(0)
            for h in range(RH):
                if h + 1 < RH:
                    decayed(h + 1)
                for m in range(TT):
                    n = TT * h + m
                    dve.wait_ge(sem("attended"), n + 1)
                    link(dve.bn_stats(bn[:, n, 0:6], bank[4 + m][:, :]))
                    dve.bn_aggr(bn[:, n, BN_MEAN:BN_VAR + 1], bn[:, n, 0:6]).then_inc(sem("varied"), 1)
                    dve.wait_ge(sem("varied"), n + 1)
                    y = gate[:, m, h * RV:(h + 1) * RV]
                    dve.scalar_tensor_tensor(y, bank[4 + m][:, :], bn[:, n, BN_MEAN:BN_MEAN + 1], y,
                                             ALU.subtract, ALU.mult).then_inc(sem("y_gated"), 1)
                    inverted(n)
            for n in range(RH * TT):
                h, m = n // TT, n % TT
                dve.wait_ge(sem("y_high"), n + 1)
                where = (slice(None), slice(4 * h, 4 * h + 4), slice(m * P, (m + 1) * P))
                dve.tensor_tensor(y_lo[where], tall(bank[n % 8]), y_hi[where].bitcast(F32), ALU.subtract)\
                    .then_inc(sem("y_low"), 1)
            norms(1)

            def mlp(layer):
                for half, (up, down) in enumerate(MLP[layer]):
                    base = HALF_TILES * (2 * layer + half)
                    with dve.Fori(0, 4) as i:
                        for m in range(4):
                            dve.wait_ge(emptied, i * 4 + (4 * up[0] + m + 1))
                            dve.tensor_tensor(relu_sq[:, m, :], relu[:, m, :], relu[:, m, :], ALU.mult)\
                                .then_inc(sem("squared"), 1)
                            dve.wait_ge(sem("squared"), i * 4 + (base + m + 1))
                            dve.tensor_copy(hid_hi[:, bass.ds(i * 4 + m, 1), :], relu_sq[:, m:m + 1, :])\
                                .then_inc(sem("hid_high"), 1)
                            dve.wait_ge(sem("hid_high"), i * 4 + (base + m + 1))
                            dve.tensor_tensor(hid_lo[:, bass.ds(i * 4 + m, 1), :], relu_sq[:, m:m + 1, :],
                                              hid_hi[:, bass.ds(i * 4 + m, 1), :].bitcast(F32), ALU.subtract)\
                                .then_inc(sem("hid_low"), 1)

                def add_part(i, m):
                    dve.wait_ge(emptied, 4 * (MLP[layer][1][1][0] + i) + m + 1)
                    part = mix[:, m, i * GC:(i + 1) * GC]
                    dve.tensor_tensor(part, part, mix_b[:, m, :], ALU.add).then_inc(sem("mix_summed"), 1)
                    dve.wait_ge(sem("mix_summed"), 8 * layer + 4 * i + m + 1)

                for m in range(TT):
                    add_part(0, m)
                norms(2 * layer + 2, lambda m: add_part(1, m))

            mlp(0)

            dve.wait_ge(bank_full, 4 * GDN_K[0])
            dve.memset(ba_hi[:, :, :].bitcast(F32), 0.0)
            dve.memset(ba_lo[:, :, :].bitcast(F32), 0.0).then_inc(sem("ba_cleared"), 1)
            dve.wait_ge(sem("ba_high"), 1)
            dve.tensor_tensor(ba_lo[:, :, 0:2 * GH], ba_raw[:, :, :], ba_hi[:, :, 0:2 * GH].bitcast(F32), ALU.subtract)\
                .then_inc(sem("ba_low"), 1)
            dve.memset(pad[:, :, 0:CONV - 1], 0.0).then_inc(sem("pad_cleared"), 1)
            dve.wait_ge(sem("join_landed"), 16)
            dve.tensor_copy(join[:, :, :, :], join_f[:, :, :, :]).then_inc(sem("join_cast"), 1)

            def by_unit(t, first):
                return t[:, :, first:first + GH].rearrange("p n h -> p h n")

            def units_of(c):
                return c.rearrange("p (h n) -> p h n", n=TT)

            def spread(row):
                return row.rearrange("p (h o) -> p h o", o=1).broadcast_to([P, GH, TT])

            def columns_before():
                dve.wait_ge(sem("small_out"), 1)
                dve.wait_ge(sem("rows_landed"), 48)
                link(dve.tensor_scalar(units_of(ct[:, 0, :]), by_unit(ba_cols, 0), -1.0, None, ALU.mult))
                link(dve.tensor_tensor(units_of(ct[:, 4, :]), by_unit(ba_cols, GH), spread(head_rows[:, 0, :]), ALU.add))
                link(dve.tensor_scalar(ct[:, 9, :], ct[:, 4, :], -1.0, None, ALU.mult))
                dve.tensor_tensor(ct[:, 1, :], ct[:, 9, :], ct[:, 4, :], ALU.min).then_inc(sem("cols_a"), 1)
                dve.wait_ge(sem("cols_b"), 2)
                dve.tensor_scalar(ct[:, 5, :], ct[:, 3, :], 1.0, None, ALU.add).then_inc(sem("cols_c"), 1)
                dve.wait_ge(sem("cols_c"), 1)

            def columns_after():
                link(dve.tensor_scalar(ct[:, 10, :], ct[:, 2, :], 1.0, None, ALU.add))
                link(dve.reciprocal(col[:, BETA, :], ct[:, 10, :]))
                link(dve.tensor_scalar(ct[:, 11, :], ct[:, 5, :], -1.0, 1e-30, ALU.add, ALU.max))
                link(dve.reciprocal(ct[:, 12, :], ct[:, 11, :]))
                dve.wait_ge(sem("cols_d"), 1)
                link(dve.tensor_tensor(ct[:, 13, :], ct[:, 6, :], ct[:, 3, :], ALU.mult))
                link(dve.tensor_tensor(ct[:, 13, :], ct[:, 13, :], ct[:, 12, :], ALU.mult))
                link(dve.scalar_tensor_tensor(ct[:, 14, :], ct[:, 5, :], 1.0, ct[:, 3, :], ALU.is_equal, ALU.mult))
                link(dve.scalar_tensor_tensor(ct[:, 13, :], ct[:, 4, :], 0.0, ct[:, 13, :], ALU.max, ALU.add))
                link(dve.tensor_tensor(ct[:, 13, :], ct[:, 13, :], ct[:, 14, :], ALU.add))
                dve.scalar_tensor_tensor(units_of(col[:, G, :]), units_of(ct[:, 13, :]), -1.0,
                                         spread(head_rows[:, 2, :]), ALU.mult, ALU.mult).then_inc(sem("g_made"), 1)

            order = [(GDN_K, gk, KT), (GDN_V, gv, 2 * KT), (GDN_Q, gq, 0)]
            dve.wait_ge(sem("pad_cleared"), 1)
            columns_before()
            dve.wait_ge(sem("small_out"), 2)
            def over(c, n=P):
                return c.rearrange("p (k o) -> p k o", o=1).broadcast_to([P, c.shape[-1], n])

            def column(c, u):
                return col[:, c, u:u + 1]

            def convolve(gi):
                start, dest, tile0 = order[gi // 2]
                p = gi % 2
                for m in range(4):
                    dve.wait_ge(emptied, 4 * (start[0] + p) + m + 1)
                    t = dest[:, 4 * p + m, :]
                    w = [conv_w[:, j, tile0 + 4 * p + m:tile0 + 4 * p + m + 1] for j in range(CONV)]
                    link(dve.tensor_scalar(t, pad[:, m, 0:T], w[0], None, ALU.mult))
                    for j in range(1, CONV):
                        step = dve.scalar_tensor_tensor(t, pad[:, m, j:j + T], w[j], t, ALU.mult, ALU.add)
                        if j < CONV - 1:
                            link(step)
                    step.then_inc(sem("convolved"), 1)

            def g_sums():
                dve.wait_ge(sem("g_sums_read"), 1)
                link(dve.tensor_copy(col[:, GCUM, :], bank[7][:, 0:UNITS]))
                link(dve.tensor_tensor(ct[:, 7, :], bank[7][:, UNITS:2 * UNITS], col[:, GCUM, :], ALU.subtract))
                dve.sem_inc(sem("rest_made"), 1)
                dve.sem_inc(sem("g_sums_read"), 1)

            def reduce_squares(first, last):
                for i in range(first, last):
                    dve.wait_ge(sem("kq_squared"), i + 1)
                    slot = i % 4 if i < GH else i % 2
                    dve.tensor_reduce(col[:, (SS_K, SS_Q)[i // GH], i % GH * TT:(i % GH + 1) * TT],
                                      tmp[:, slot, :].rearrange("p (n e) -> p n e", n=TT), AX.X, ALU.add)\
                        .then_inc(sem("kq_summed"), 1)

            def k_columns():
                dve.wait_ge(sem("kq_summed"), GH)
                link(dve.tensor_scalar(ct[:, 0, :], col[:, SS_K, :], EPS, None, ALU.add))
                dve.sem_inc(sem("kq_x_made"), 1)
                dve.wait_ge(sem("kq_rooted"), 1)
                link(inv_root(col[:, SS_K, :], ct[:, 2, :], lambda n: ct[:, 9 + n, :], col[:, R_K, :]))
                rk = col[:, R_K, :]
                link(dve.tensor_tensor(col[:, S_V, :], col[:, BETA, :], rk, ALU.mult))
                link(dve.scalar_tensor_tensor(col[:, S_U, :], rk, -1.0, col[:, S_V, :], ALU.mult, ALU.mult))
                dve.wait_ge(sem("rest_exped"), 1)
                link(dve.tensor_tensor(col[:, EXP_REST, :], ct[:, 8, :], rk, ALU.mult))
                dve.tensor_tensor(col[:, N_K, :], ct[:, 0, :], rk, ALU.mult).then_inc(sem("cols_k"), 1)

            def q_columns():
                dve.wait_ge(sem("kq_summed"), 2 * GH)
                link(dve.tensor_scalar(ct[:, 1, :], col[:, SS_Q, :], EPS, None, ALU.add))
                dve.sem_inc(sem("kq_x_made"), 1)
                dve.wait_ge(sem("kq_rooted"), 2)
                link(inv_root(col[:, SS_Q, :], ct[:, 3, :], lambda n: ct[:, 9 + n, :], ct[:, 12, :]))
                link(dve.tensor_scalar(col[:, R_Q, :], ct[:, 12, :], float(P) ** -0.5, None, ALU.mult))

            def shifted(h, b):
                for n in range(TT):
                    cols = slice(n * P, (n + 1) * P)
                    step = dve.scalar_tensor_tensor(tmp[:, h % 2, cols], bank[b][:, cols], column(GCUM, h * TT + n),
                                                    neg, ALU.subtract, ALU.add)
                return step

            def triangle(h):
                b = (0 if h < 4 else 4) + 2 * (h % 2)
                dve.wait_ge(sem("tri_prods"), h + 1)
                dve.wait_ge(sem("tri_exped"), h + 1)
                for n in range(TT):
                    u = h * TT + n
                    cols = slice(n * P, (n + 1) * P)
                    step = dve.scalar_tensor_tensor(neg_l_t[:, u, :], bank[b + 1][:, cols], column(S_U, u),
                                                    tmp[:, h % 2, cols], ALU.mult, ALU.mult)
                step.then_inc(sem("triangled"), 1)

            def triangles(first):
                for h0 in (first, first + 2):
                    for h in (h0, h0 + 1):
                        b = (0 if h < 4 else 4) + 2 * (h % 2)
                        dve.wait_ge(sem("tri_rows"), h + 1)
                        shifted(h, b).then_inc(sem("tri_shifted"), 1)
                    for h in (h0, h0 + 1):
                        triangle(h)

            def quarter(i):
                return slice(i * BLOCK, (i + 1) * BLOCK)

            def take_blocks():
                dve.wait_ge(sem("triangled"), GH)
                dve.memset(block_x[:, :, :], 0.0)
                for i in range(P // BLOCK):
                    step = dve.transpose(block_l[quarter(i), :, :],
                                         neg_l_t[quarter(i), :, quarter(i)].rearrange("s u c -> s c u"))
                link(step)
                flat = block_x[:, :, :].rearrange("p r c -> p (r c)")
                link(dve.memset(flat[:, 0:BLOCK * BLOCK:BLOCK + 1], 1.0))

            def block_rows(first, last):
                for r in range(first, last):
                    prod = tmp[:, 2:4, :].rearrange("p a n -> p (a n)")[:, 0:r * r].rearrange("p (c s) -> p c s", c=r)
                    link(dve.tensor_tensor(prod, block_x[:, 0:r, 0:r].rearrange("p s c -> p c s"),
                                           block_l[:, r:r + 1, 0:r].broadcast_to([P, r, r]), ALU.mult))
                    link(dve.tensor_reduce(block_x[:, r, 0:r], prod, AX.X, ALU.add))

            dve.wait_ge(sem("small_out"), 2)
            convolve(0)
            columns_after()
            convolve(1)
            reduce_squares(0, 4)
            g_sums()
            reduce_squares(4, GH)
            k_columns()
            convolve(2)
            triangles(0)
            convolve(3)
            triangles(4)
            convolve(4)
            take_blocks()
            block_rows(1, 14)
            convolve(5)
            block_rows(14, 23)
            reduce_squares(GH, 2 * GH)
            block_rows(23, BLOCK)
            dve.sem_inc(sem("blocks_done"), 1)
            q_columns()
            dve.wait_ge(sem("inv_cleared"), 1)
            for i in range(P // BLOCK):
                dve.transpose(inv_t[quarter(i), :, quarter(i)].rearrange("b u c -> b c u"), block_x[quarter(i), :, :])\
                    .then_inc(sem("inv_seeded"), 1)
            dve.wait_ge(sem("inv_seeded"), P // BLOCK)
            for h in range(GH):
                dve.wait_ge(sem("row_made"), h + 1)
                shifted(h, 4 + h % 2).then_inc(sem("row_shifted"), 1)
                dve.wait_ge(sem("unit_prods"), h + 1)
                dve.wait_ge(sem("decay_made"), h + 1)
                for n in range(TT):
                    u = h * TT + n
                    cols = slice(n * P, (n + 1) * P)
                    step = dve.scalar_tensor_tensor(attn[:, u, :], bank[2 + h % 2][:, cols], column(R_K, u),
                                                    tmp[:, h % 2, cols], ALU.mult, ALU.mult)
                step.then_inc(sem("unit_scaled"), 1)
            dve.wait_ge(sem("join_cast"), 1)

            def mask(side, level):
                return join[:, side, level:level + 1, :].broadcast_to([P, TT, P])

            n_second = 0
            for batch in range(2):
                heads = range(4 * batch, 4 * batch + 4)
                for level in range(len(LEVELS)):
                    for r, h in enumerate(heads):
                        n_second += 1
                        dve.wait_ge(sem("seconds_made"), n_second)
                        if level < len(LEVELS) - 1:
                            dve.copy_predicated(inv[:, 4 * r:4 * r + 4, :], mask(0, level), tall(bank[4 + r % 2 * 2]))
                        dve.copy_predicated(inv_t[:, h * TT:(h + 1) * TT, :], mask(1, level),
                                            tall(bank[5 + r % 2 * 2])).then_inc(sem("joined"), 1)
                        if level == len(LEVELS) - 1:
                            k = gk[:, h, :].rearrange("p (n e) -> p n e", n=TT)
                            cs = slice(h * TT, (h + 1) * TT)
                            dve.wait_ge(sem("k_turned_out"), GH)
                            dve.tensor_tensor(k_grown[:, 4 * r:4 * r + 4, :], k, over(col[:, EXP_G, cs]), ALU.mult)\
                                .then_inc(sem("k_grown"), 1)
                            dve.tensor_tensor(k, k, over(col[:, EXP_REST, cs]), ALU.mult).then_inc(sem("k_faded"), 1)
            outs = gv[:, :, :].rearrange("p h (n e) -> p h n e", n=TT)
            per_unit = [col[:, c, :].rearrange("p (h n) -> p h n", n=TT) for c in range(13)]

            def some(c, q, n):
                return per_unit[c][:, 4 * q:4 * q + 4, n:n + 1].broadcast_to([P, 4, P])

            def outputs(n):
                dve.wait_ge(sem("o_squared"), n + 1)
                dve.tensor_reduce(on[:, n, 0, :], o_sq[:, :, :], AX.X, ALU.add).then_inc(sem("o_summed"), 1)
                dve.wait_ge(sem("o_rooted"), n + 1)
                link(inv_root(on[:, n, 0, :], on[:, n, 1, :], lambda t: on[:, n, 2 + t, :], on[:, n, 5, :], 1.0 / P))
                dve.tensor_tensor(outs[:, :, n, :], outs[:, :, n, :], over(on[:, n, 5, :]), ALU.mult)\
                    .then_inc(sem("o_scaled"), 1)

            for n in range(TT):
                for q in range(2):
                    hs = slice(4 * q, 4 * q + 4)
                    dve.wait_ge(sem("v_new_full"), 2 * n + q + 1)
                    if n:
                        dve.wait_ge(sem("state_full"), 2 * (n - 1) + q + 1)
                    dve.tensor_tensor(v_new[:, hs, :], tall(bank[q]), some(S_V, q, n), ALU.mult)\
                        .then_inc(sem("v_new_made"), 1)
                for q in range(2):
                    hs = slice(4 * q, 4 * q + 4)
                    dve.wait_ge(sem("o_full"), 2 * n + q + 1)
                    dve.tensor_tensor(outs[:, hs, n, :], tall(bank[2 + q]), some(R_Q, q, n), ALU.mult)\
                        .then_inc(sem("o_out"), 1)
                    if n == TT - 1:
                        continue
                    dve.wait_ge(sem("state_full"), 2 * n + q + 1)
                    if n == 0:
                        dve.tensor_copy(state[:, hs, :], tall(bank[4 + q])).then_inc(sem("state_made"), 1)
                        continue
                    dve.wait_ge(sem("state_made"), 2 * (n - 1) + q + 1)
                    for r in range(4):
                        h = 4 * q + r
                        step = dve.scalar_tensor_tensor(state[:, h, :], state[:, h, :], column(EXP_TOT, h * TT + n),
                                                        bank[4 + q][:, r * P:(r + 1) * P], ALU.mult, ALU.add)
                    step.then_inc(sem("state_made"), 1)
                if n:
                    outputs(n - 1)
            outputs(TT - 1)
            for n in range(TT):
                for half in range(2):
                    dve.wait_ge(sem("o_high"), 2 * n + half + 1)
                    where = (slice(None), slice(4 * half, 4 * half + 4), slice(n * P, (n + 1) * P))
                    dve.tensor_tensor(act_lo[where], tall(bank[2 * n + half]), act_hi[where].bitcast(F32), ALU.subtract)\
                        .then_inc(sem("o_low"), 1)
            norms(3)
            mlp(1)


_INS = ["x", "norm_gains", "ret_w_in", "ret_gn_gain", "ret_w_out", "gdn_w_in", "gdn_conv_w", "gdn_a_log",
        "gdn_dt_bias", "gdn_norm_gain", "gdn_w_out", "mlp_w_up", "mlp_w_down"]


def kernel(**inputs):
    import concourse.bacc as bacc
    from concourse.bass_utils import run_bass_kernel_spmd

    nc = bacc.Bacc("TRN2", target_bir_lowering=False, num_devices=1)
    arrays, args = {}, []
    given = {name: np.ascontiguousarray(inputs[name]) for name in _INS}
    for name, a in {**given, **shape_constants()}.items():
        arrays[f"in_{name}_dram"] = a
        args.append(nc.dram_tensor(f"in_{name}_dram", a.shape, mybir.dt.from_np(a.dtype), kind="ExternalInput").ap())
    out = nc.dram_tensor("out_dram", (1, T, D), F32, kind="ExternalOutput").ap()
    hybrid_trunk(nc, *args, out)
    result = run_bass_kernel_spmd(nc, [arrays], core_ids=[0])
    return result.results[0]["out_dram"]
```

```python
from contextlib import ExitStack

import numpy as np

import concourse.bass as bass
from concourse import mybir

F32 = mybir.dt.float32
F32R = mybir.dt.float32r
U8 = mybir.dt.uint8
BF16 = mybir.dt.bfloat16
ALU = mybir.AluOpType
ACT = mybir.ActivationFunctionType
AX = mybir.AxisListType

P = 128
D = 1024
T = 512
KT = D // P
TT = T // P
FF = 4 * D
EPS = 1e-6
RH, RQK, RV = 4, D // 4, 2 * D // 4
VT = 2 * D // P
GH = 8
GDN_IN = 4 * D + 2 * GH
CONV = 4
UNITS = GH * TT
BLOCK = 32
LEVELS = [32, 64]

CK = 4
GC = 512
HALF_TILES = FF // 2 // P


def shape_constants():
    half = RQK // 2
    inv_freq = (np.float32(10000.0) ** (-np.arange(half, dtype=np.float32) / np.float32(half))).astype(np.float32)
    angle = (np.arange(T, dtype=np.float32)[None, :] * inv_freq[:, None]).astype(np.float32)
    rope = np.stack([np.cos(angle), np.sin(angle)], axis=1).astype(np.float32)
    gap = np.arange(T)[None, :] - np.arange(P)[:, None]
    log_gamma = np.log1p(-(2.0 ** (-5.0 - np.arange(RH, dtype=np.float64))))
    decay = np.where(gap[:, None, :] >= 0, np.exp(log_gamma[None, :, None] * np.maximum(gap, 0)[:, None, :]), 0.0)
    decay = (decay * RQK ** -0.5).astype(np.float32)
    row, col = np.arange(P)[:, None], np.arange(P)[None, :]
    square = np.stack([
        (row == col), (row <= col), np.ones((P, P)), np.where(row <= col, 0.0, -1e30),
    ], axis=1).astype(np.float32)
    join = np.stack([(row // (2 * b) == col // (2 * b)) & (row // b % 2 == 0) & (col // b % 2 == 1)
                     for b in LEVELS], axis=1).astype(np.float32)
    return {"rope": rope, "decay": decay, "square": square, "join": join}


class Plan:

    def __init__(self, nc):
        self.nc = nc
        self.at = (nc.sbuf_base + 63) // 64 * 64

    def place(self, size):
        at, self.at = self.at, self.at + (size + 31) // 32 * 32
        assert self.at <= self.nc.sbuf_usable_end, (self.at, self.nc.sbuf_usable_end)
        return at

    def tile(self, name, shape, dtype, at=None):
        size = int(np.prod(shape[1:])) * {U8: 1, BF16: 2}.get(dtype, 4)
        if at is None:
            at = self.place(size)
        return self.nc.alloc_sbuf_tensor_at(name, list(shape), dtype, offset=at)


def hybrid_trunk(nc, x, norm_gains, ret_w_in, ret_gn_gain, ret_w_out, gdn_w_in, gdn_conv_w, gdn_a_log,
                 gdn_dt_bias, gdn_norm_gain, gdn_w_out, mlp_w_up, mlp_w_down, rope_c, decay_c, square_c,
                 join_c, out):
    plan = Plan(nc)
    KB = 1024
    resid = plan.tile("resid", [P, TT, D], F32)
    act_at = plan.place(32 * KB)
    act_hi = plan.tile("act_hi", [P, KT, T], F32R, act_at)
    act_lo = plan.tile("act_lo", [P, KT, T], F32R, act_at + 16 * KB)
    w_raw = plan.tile("w_raw", [P, 2, CK, GC], F32)
    w_hi = plan.tile("w_hi", [P, 2, CK, GC], F32R)
    w_lo = plan.tile("w_lo", [P, 2, CK, GC], F32R)
    gains_at = plan.place(8 * KB)
    gains = plan.tile("gains", [P, 2, D], F32, gains_at)
    square = plan.tile("square", [P, 4, P], F32)
    ident, tri, ones, neg = (square[:, n, :] for n in range(4))
    dump_at = plan.place(2 * KB)
    dump = plan.tile("dump", [P, D], BF16, dump_at)
    stat = plan.tile("stat", [P, 12, TT], F32)
    SS_MIX, ROOT_MIX, SS_RES, ROOT_RES, NEWTON, RSTD_MIX, RSTD_RES, EPS_COL, SS_HALF, HALF_EPS = \
        0, 1, 2, 3, 4, 7, 8, 9, 10, 11
    eps = stat[:, EPS_COL, 0:1]
    big_at = plan.place(0)

    def big(name, shape, dtype, kb):
        made = plan.tile(name, shape, dtype, big_at + int(kb * KB))
        size = int(np.prod(shape[1:])) * {U8: 1, BF16: 2}.get(dtype, 4)
        assert big_at + int(kb * KB) + size <= nc.sbuf_usable_end
        return made

    normed = big("normed", [P, 2, D], F32, 64)
    mix = big("mix", [P, TT, D], F32, 80)
    qk_t = big("qk_t", [P, 2 * KT, T], F32, 0)
    v_tm = big("v_tm", [P, TT, 2 * D], F32, 32)
    gate = big("gate", [P, TT, 2 * D], F32, 64)
    rope_tmp = big("rope_tmp", [P, 4, T], F32, 64)
    rope = big("rope", [P, 2, T], F32, 72)
    score = plan.tile("score", [P, 2, TT, T], F32, act_at)
    decay = plan.tile("decay", [P, RH, T], F32, act_at + 16 * KB)
    bn = plan.tile("bn", [P, RH * TT, 16], F32, act_at + 24 * KB)
    BN_MEAN, BN_VAR, BN_ROOT, BN_NEWTON, BN_RSTD = 6, 7, 8, 9, 12
    y_hi = big("y_hi", [P, VT, T], F32R, 0)
    y_lo = big("y_lo", [P, VT, T], F32R, 32)
    hid_hi = big("hid_hi", [P, HALF_TILES, T], F32R, 0)
    hid_lo = big("hid_lo", [P, HALF_TILES, T], F32R, 32)
    relu = big("relu", [P, 4, T], F32, 64)
    relu_sq = big("relu_sq", [P, 4, T], F32, 72)
    gk = big("gk", [P, GH, T], F32, 0)
    gv = big("gv", [P, GH, T], F32, 16)
    gq = big("gq", [P, GH, T], F32, 32)
    gz = big("gz", [P, TT, D], F32, 48)
    neg_l_t = big("neg_l_t", [P, UNITS, P], F32, 64)
    w_t = big("w_t", [P, UNITS, P], F32, 64)
    pad = big("pad", [P, 4, CONV - 1 + T + 1], F32, 80)
    block_l = big("block_l", [P, BLOCK, BLOCK], F32, 88.25)
    block_x = big("block_x", [P, BLOCK, BLOCK], F32, 92.25)
    attn = big("attn", [P, UNITS, P], F32, 80)
    go_hi = big("go_hi", [P, KT, T], F32R, 0)
    go_lo = big("go_lo", [P, KT, T], F32R, 32)
    ba_hi = big("ba_hi", [P, KT, P], F32R, 32)
    ba_lo = big("ba_lo", [P, KT, P], F32R, 36)
    ba_t = big("ba_t", [P, T], F32, 40)
    ba_cols = big("ba_cols", [P, TT, 2 * GH], F32, 42)
    conv_rows = big("conv_rows", [CONV * 3 * KT, P], F32, 43)
    join_f = big("join_f", [P, len(LEVELS), P], F32, 44)
    ba_raw = big("ba_raw", [P, KT, 2 * GH], F32, 96.25)
    col = big("col", [P, 13, UNITS], F32, 96.25)
    (BETA, G, GCUM, EXP_G, EXP_TOT, EXP_REST, SS_K, SS_Q, R_K, N_K, R_Q, S_U, S_V) = range(13)
    z_gain = big("z_gain", [P, P], F32, 97.875)
    join = big("join", [P, len(LEVELS), P], U8, 98.375)
    conv_w = big("conv_w", [P, CONV, 3 * KT], F32, 98.875)
    head_rows = big("head_rows", [P, 4, GH], F32, 99.25)
    ct = plan.tile("ct", [P, 16, UNITS], F32, dump_at)
    inv_t = plan.tile("inv_t", [P, UNITS, P], F32, act_at)
    inv = plan.tile("inv", [P, UNITS // 2, P], F32, act_at + 16 * KB)
    half_prod = plan.tile("half_prod", [P, UNITS // 2, P], F32, act_at + 24 * KB)
    k_grown = plan.tile("k_grown", [P, UNITS // 2, P], F32, act_at + 24 * KB)
    states = [plan.tile(f"state{n}", [P, GH, P], F32, act_at + (16 + 12 * n) * KB) for n in range(2)]
    o_sq = plan.tile("o_sq", [P, GH, P], F32, act_at + 20 * KB)
    v_new = plan.tile("v_new", [P, GH, P], F32, act_at + 24 * KB)
    tmp = plan.tile("tmp", [P, 4, T], F32, gains_at)
    squares = plan.tile("squares", [P, 2, TT, P], BF16, gains_at)
    on = plan.tile("on", [P, TT, 6, GH], F32, dump_at)
    tall = lambda b: b[:, :].rearrange("p (k t) -> p k t", k=4)

    count = [0, 0, 0]

    def take(groups, chunks):
        was = tuple(count)
        for n, more in enumerate((groups, groups * chunks, groups * (chunks - 1))):
            count[n] += more
        return was

    def take_mlp():
        return [(take(4, 2), take(2, 4)) for _ in range(2)]

    RET_QK, RET_V, RET_G, RET_OUT = take(4, 2), take(4, 2), take(4, 2), take(2, 4)
    MLP = [take_mlp()]
    GDN_K, GDN_V, GDN_Q, GDN_Z, GDN_OUT = (take(2, 2) for _ in range(5))
    MLP.append(take_mlp())
    CHUNKS = count[1]
    NEXT_GROUP = [0, MLP[0][0][0][0], GDN_K[0], MLP[1][0][0][0], count[0]]
    GAIN_ROWS = [(None, (0, 0)), ((0, 1), (0, 2)), ((0, 3), (1, 0)), ((1, 1), (1, 2)), ((1, 3), None)]
    GAINS_LANDED = [16, 48, 80, 112, 128]

    with ExitStack() as ctx:
        bank = [ctx.enter_context(nc.psum_tensor(f"bank{n}", [P, T], F32)) for n in range(8)]
        sems = {}

        def sem(name):
            if name not in sems:
                sems[name] = ctx.enter_context(nc.semaphore(name))
            return sems[name]

        def y_bank(n):
            return bank[n if n < 4 else 4 + n % 4]

        class Chain:

            def __init__(self, eng, name):
                self.eng, self.sem, self.n = eng, sem(name), 0

            def link(self, ins):
                self.n += 1
                ins.then_inc(self.sem, 1)
                self.eng.wait_ge(self.sem, self.n)

        w_landed = [sem("w_landed0"), sem("w_landed1")]
        w_high = sem("w_high")
        w_ready = sem("w_ready")
        chunk_used = sem("chunk_used")
        bank_full = sem("bank_full")
        emptied = sem("emptied")

        block = ctx.enter_context(nc.Block())

        @block.sync
        def _(sp):
            def stream(start, groups, w, chunks, col0=0):
                c0 = start[1]
                rows = w.rearrange("(k p) n -> p k n", p=P)

                def load(g, j, cols):
                    if c0 or not isinstance(g, int):
                        sp.wait_ge(w_ready, g * (2 * chunks) + 2 * (c0 + j - 1))
                    sp.dma_start(w_raw[:, j % 2, :, :], rows[:, j * CK:(j + 1) * CK, cols])\
                        .then_inc(w_landed[j % 2], 16)

                if c0 == 0:
                    for j in range(2):
                        for m in (2 * j, 2 * j + 1):
                            sp.dma_start(resid[:, m, :], x[0, m * P:(m + 1) * P, :]).then_inc(sem(f"x_landed{m}"), 16)
                        load(0, j, slice(col0, col0 + GC))
                with sp.Fori(0 if c0 else 1, groups) as g:
                    cols = bass.ds(sp.snap(g * GC + col0), GC)
                    for j in range(chunks):
                        load(g, j, cols)

            def stream_mlp(layer):
                for half, (up, down) in enumerate(MLP[layer]):
                    stream(up, 4, mlp_w_up[layer], 2, half * FF // 2)
                    stream(down, 2, mlp_w_down[layer, half * FF // 2:(half + 1) * FF // 2, :], 4)

            stream(RET_QK, 12, ret_w_in[0], 2)
            stream(RET_OUT, 2, ret_w_out[0], 4)
            sp.dma_start(ba_raw[:, :, :], gdn_w_in[0].rearrange("(k p) n -> p k n", p=P)[:, :, 4 * D:GDN_IN])\
                .then_inc(sem("ba_landed"), 16)
            stream_mlp(0)
            for start, first in ((GDN_K, D), (GDN_V, 2 * D), (GDN_Q, 0), (GDN_Z, 3 * D)):
                stream(start, 2, gdn_w_in[0], 2, first)
            stream(GDN_OUT, 2, gdn_w_out[0], 2)
            stream_mlp(1)
            for m in range(TT):
                sp.wait_ge(sem("residual_low"), 3 * TT + m + 1)
                sp.dma_start(out[0, m * P:(m + 1) * P, 0:GC], resid[:, m, 0:GC]).then_inc(sem("stored"), 16)
                sp.wait_ge(sem("residual_done"), 3 * TT + m + 1)
                sp.dma_start(out[0, m * P:(m + 1) * P, GC:D], resid[:, m, GC:D]).then_inc(sem("stored"), 16)
            sp.wait_ge(sem("stored"), 16 * 2 * TT)

        @block.gpsimd
        def _(pool):
            def low_part(s, before):
                for half in range(2):
                    pool.wait_ge(w_high, before + (half + 1))
                    kt = slice(half * CK // 2, (half + 1) * CK // 2)
                    nc.gpsimd.tensor_tensor(w_lo[:, s, kt, :], w_raw[:, s, kt, :], w_hi[:, s, kt, :].bitcast(F32),
                                            ALU.subtract).then_inc(w_ready, 1)

            def low_parts(first, last):
                with pool.Fori(first // 2, last // 2) as i:
                    for s in range(2):
                        low_part(s, i * 4 + 2 * s)

            def norm_share(b):
                for m in range(2):
                    if b:
                        pool.wait_ge(sem("residual_done"), TT * (b - 1) + m + 1)
                        pool.wait_ge(sem("acts_transposed"), TT * (b - 1) + m + 3)
                    else:
                        pool.wait_ge(sem(f"x_landed{m}"), 16)
                    pool.wait_ge(sem("gains_landed"), GAINS_LANDED[b])
                    share = normed[:, m, GC:2 * GC]
                    nc.gpsimd.tensor_tensor(share, resid[:, m, GC:2 * GC], gains[:, 1, GC:2 * GC], ALU.mult)\
                        .then_inc(sem("share_gained"), 1)

            norm_share(0)
            low_parts(0, MLP[0][0][0][1])
            norm_share(1)
            low_parts(MLP[0][0][0][1], GDN_K[1])
            norm_share(2)
            low_parts(GDN_K[1], GDN_K[1] + 2)
            pool.wait_ge(bank_full, 4 * GDN_K[0])
            pool.memset(ba_hi[:, :, :].bitcast(F32), 0.0)
            pool.memset(ba_lo[:, :, :].bitcast(F32), 0.0).then_inc(sem("ba_cleared"), 1)
            pool.wait_ge(sem("residual_done"), 2 * TT)
            pool.memset(pad[:, :, 0:CONV - 1], 0.0).then_inc(sem("pad_cleared"), 1)
            low_parts(GDN_K[1] + 2, GDN_OUT[1])
            def grow_q(first, last):
                for h in range(first, last):
                    pool.wait_ge(sem("row_exped"), h + 1)
                    pool.wait_ge(sem("unit_prods"), h + 1)
                    nc.gpsimd.tensor_tensor(gq[:, h, :], gq[:, h, :], tmp[:, 2 + h % 2, :], ALU.mult)\
                        .then_inc(sem("q_grown"), 1)

            grow_q(0, 4)
            pool.wait_ge(bank_full, 4 * GDN_OUT[0])
            pool.memset(inv_t[:, 0:UNITS // 2, :], 0.0).then_inc(sem("inv_cleared"), 1)
            grow_q(4, GH)
            low_part(0, 2 * GDN_OUT[1])
            for p in range(2):
                for m in range(TT):
                    z = gz[:, m, p * GC:(p + 1) * GC].rearrange("p (h e) -> p h e", h=4)
                    nc.gpsimd.tensor_tensor(z, z, z_gain[:, :].rearrange("p (o e) -> p o e", o=1)
                                            .broadcast_to([P, 4, P]), ALU.mult).then_inc(sem("z_gained"), 1)
            for h in range(GH):
                pool.wait_ge(sem("k_grown"), h + 1)
                k = gk[:, h, :].rearrange("p (n e) -> p n e", n=TT)
                nc.gpsimd.tensor_tensor(k, k, col[:, EXP_REST, h * TT:(h + 1) * TT]
                                        .rearrange("p (k o) -> p k o", o=1).broadcast_to([P, TT, P]), ALU.mult)\
                    .then_inc(sem("k_faded"), 1)
            low_part(1, 2 * GDN_OUT[1] + 2)
            pool.wait_ge(sem("z_gained"), 2 * TT)
            units = gv[:, :, :].rearrange("p h (n e) -> p h n e", n=TT)
            for n in range(TT):
                pool.wait_ge(sem("o_out"), 2 * n + 2)
                z = gz[:, n, :].rearrange("p (h e) -> p h e", h=GH)
                nc.gpsimd.tensor_tensor(z, z, units[:, :, n, :], ALU.mult).then_inc(sem("o_gated"), 1)
            low_parts(GDN_OUT[1] + 2, MLP[1][0][0][1])
            norm_share(3)
            low_parts(MLP[1][0][0][1], CHUNKS)

        @block.tensor
        def _(pe):
            def three(dst, sta_hi, sta_lo, mov_hi, mov_lo, first, last):
                pe.matmul(dst, sta_hi, mov_hi, start=first, stop=False)
                pe.matmul(dst, sta_hi, mov_lo, start=False, stop=False)
                return pe.matmul(dst, sta_lo, mov_hi, start=False, stop=last)

            def part(c, j, parity, chunks, m, features_out, a_hi, a_lo, tokens=slice(0, T), fresh=False):
                s = j % 2
                mm = slice(m * P, (m + 1) * P)
                dst = bank[4 * parity + m][:, tokens] if features_out else bank[4 * parity + m][:, :]
                for kt in range(CK):
                    if fresh and kt % (CK // 2) == 0:
                        pe.wait_ge(w_ready, c * 2 + (2 * j + 1 + kt // (CK // 2)))
                    k = j * CK + kt
                    ends = (k == 0, k == chunks * CK - 1)
                    if features_out:
                        done = three(dst, w_hi[:, s, kt, mm], w_lo[:, s, kt, mm], a_hi[:, k, tokens], a_lo[:, k, tokens],
                                     *ends)
                    else:
                        done = three(dst, a_hi[:, k, mm], a_lo[:, k, mm], w_hi[:, s, kt, :], w_lo[:, s, kt, :], *ends)
                return done

            def group(c, parity, chunks, features_out, a_hi, a_lo, aside={}, tiles=None):
                for j in range(chunks):
                    if tiles is not None:
                        pe.wait_ge(tiles[0], tiles[1] + CK * (j + 1))
                    for m in range(4):
                        done = part(c, j, parity, chunks, m, features_out, a_hi, a_lo, fresh=m == 0)
                        if j == chunks - 1:
                            done.then_inc(bank_full, 1)
                        elif m == 3:
                            done.then_inc(chunk_used, 1)
                        if (j, m) in aside:
                            aside[j, m]()

            def turn_tile(b, m):
                if b:
                    pe.wait_ge(emptied, 4 * (NEXT_GROUP[b] - 1) + (0, 0, 2, 4)[m])
                pe.wait_ge(sem("normed"), TT * b + m + 1)
                if m < 2:
                    pe.wait_ge(sem("normed_share"), 2 * b + m + 1)
                for k in range(KT):
                    done = pe.transpose(bank[2 * m + k // 4][:, k % 4 * P:(k % 4 + 1) * P],
                                        normed[:, m % 2, k * P:(k + 1) * P], ident)
                done.then_inc(sem("acts_transposed"), 1)

            def last_group(norm, start, chunks, a_hi, a_lo):
                g0, c0, _ = start
                c = c0 + chunks
                pe.wait_ge(emptied, 4 * g0)
                for j in range(chunks - 2):
                    for m in range(4):
                        done = part(c, j, 1, chunks, m, False, a_hi, a_lo, fresh=m == 0)
                    done.then_inc(chunk_used, 1)
                a, b = chunks - 2, chunks - 1
                for m, j in ((0, a), (1, a), (0, b), (1, b), (2, a), (3, a), (2, b), (3, b)):
                    if (m, j) == (3, b) and norm < 4:
                        turn_tile(norm, 0)
                    done = part(c, j, 1, chunks, m, False, a_hi, a_lo, fresh=m == 0)
                    if j == b:
                        done.then_inc(bank_full, 1)
                    elif m == 3:
                        done.then_inc(chunk_used, 1)

            def groups(start, n, chunks, features_out, a_hi, a_lo):
                g0, c0, _ = start
                if g0:
                    pe.wait_ge(emptied, 4 * (g0 - 1))

                def pair(i):
                    group(i * (2 * chunks) + c0, 0, chunks, features_out, a_hi, a_lo)
                    if g0 or i:
                        pe.wait_ge(emptied, i * 8 + 4 * g0)
                    group(i * (2 * chunks) + (c0 + chunks), 1, chunks, features_out, a_hi, a_lo)

                if n == 2 or not g0:
                    for i in range(n // 2):
                        if i:
                            pe.wait_ge(emptied, i * 8 + 4 * (g0 - 1))
                        pair(i)
                    return
                with pe.Fori(0, n // 2) as i:
                    pair(i)
                    pe.wait_ge(emptied, i * 8 + 4 * (g0 + 1))

            def begin(b, between=None):
                c = 0 if b == 0 else (MLP[0][0][0], GDN_K, MLP[1][0][0])[b - 1][1]

                if b == 0:
                    turn_tile(b, 0)
                turn_tile(b, 1)
                pe.wait_ge(sem("act_low"), 2 * (TT * b + 2))
                for j in range(2):
                    for m in range(4):
                        part(c, j, 0, 2, m, True, act_hi, act_lo, slice(0, 2 * P), fresh=m == 0)
                        if (j, m) == (1, 0):
                            turn_tile(b, 2)
                        if (j, m) == (1, 1):
                            turn_tile(b, 3)
                pe.wait_ge(sem("act_low"), 2 * TT * (b + 1))
                if between:
                    between()
                for j in range(2):
                    for m in range(4):
                        done = part(c, j, 0, 2, m, True, act_hi, act_lo, slice(2 * P, T))
                        if j:
                            done.then_inc(bank_full, 1)
                    if j == 0:
                        done.then_inc(chunk_used, 1)

            def rest(start, n):
                g0, c0, _ = start
                for i in range(1, n):
                    if g0 or i > 1:
                        pe.wait_ge(emptied, 4 * (g0 + i - 1))
                    group(c0 + 2 * i, i % 2, 2, True, act_hi, act_lo)

            def retention():
                pe.wait_ge(emptied, 4 * RET_OUT[0])
                pe.wait_ge(sem("roped"), KT)

                def scores(h):
                    if h:
                        pe.wait_ge(sem("decayed"), TT * h)
                    for i in range(TT):
                        for d in range(2):
                            done = pe.matmul(bank[i][:, 0:T - i * P], qk_t[:, KT + 2 * h + d, i * P:(i + 1) * P],
                                             qk_t[:, 2 * h + d, i * P:T], start=d == 0, stop=d == 1)
                        done.then_inc(sem("scored"), 1)

                scores(0)
                for h in range(RH):
                    if h + 1 < RH:
                        scores(h + 1)
                    else:
                        pe.wait_ge(sem("decayed"), TT * RH)
                    for j in range(TT):
                        if h:
                            pe.wait_ge(sem("y_gated"), TT * (h - 1) + j + 1)
                        for i in range(j + 1):
                            done = pe.matmul(bank[4 + j][:, :], score[:, h % 2, i, j * P:(j + 1) * P],
                                             v_tm[:, i, h * RV:(h + 1) * RV], start=i == 0, stop=i == j)
                        done.then_inc(sem("attended"), 1)
                turn_y(0, 8)

            def turn_y(first, last):
                for n in range(first, last):
                    h, m = n // TT, n % TT
                    pe.wait_ge(sem("y_scaled"), n + 1)
                    pe.wait_ge(sem("y_gated"), min(n + 9, RH * TT))
                    if n >= 8:
                        pe.wait_ge(sem("y_low"), n - 3)
                    for f in range(4):
                        done = pe.transpose(y_bank(n)[:, f * P:(f + 1) * P],
                                            gate[:, m, h * RV + f * P:h * RV + (f + 1) * P], ident)
                    done.then_inc(sem("y_transposed"), 1)

            def mlp(layer):
                for half, (up, down) in enumerate(MLP[layer]):
                    if half:
                        groups(up, 4, 2, True, act_hi, act_lo)
                    else:
                        begin(2 * layer + 1)
                        rest(up, 4)
                    g0, c0, _ = down
                    pe.wait_ge(emptied, 4 * (g0 - 1))
                    group(c0, 0, 4, False, hid_hi, hid_lo, tiles=(sem("hid_low"), HALF_TILES * (2 * layer + half)))
                    if half:
                        last_group(2 * layer + 2, down, 4, hid_hi, hid_lo)
                    else:
                        pe.wait_ge(emptied, 4 * g0)
                        group(c0 + 4, 1, 4, False, hid_hi, hid_lo)

            def unit(t, u):
                return t[:, u // TT, u % TT * P:(u % TT + 1) * P]

            def drained(gi):
                if gi == 1:
                    pe.wait_ge(sem("kq_squared"), GH)
                    pe.wait_ge(sem("g_sums_read"), 2)
                if gi in (2, 3):
                    pe.wait_ge(sem("triangled"), 4 * (gi - 1))
                if gi == 4:
                    pe.wait_ge(sem("v_turned_out"), GH)
                if gi == 5:
                    pe.wait_ge(sem("kq_squared"), 2 * GH)

            def turn(src, h, b, done):
                for n in range(TT):
                    last = pe.transpose(bank[b][:, n * P:(n + 1) * P], src[:, h, n * P:(n + 1) * P], ident)
                last.then_inc(sem(done), 1)

            def turn_k(first):
                pe.wait_ge(emptied, 4 * GDN_V[0])
                pe.wait_ge(sem("silued"), first + 4)
                for i in range(4):
                    if first:
                        pe.wait_ge(sem("kq_squared"), i + 1)
                        if i == 3:
                            pe.wait_ge(sem("g_sums_read"), 2)
                    turn(gk, first + i, 4 + i, "kq_turned")

            def turn_q(first):
                pe.wait_ge(emptied, 4 * GDN_Z[0])
                pe.wait_ge(sem("silued"), 2 * GH + first + 4)
                for i in range(4):
                    if first:
                        pe.wait_ge(sem("kq_squared"), GH + i + 1)
                    turn(gq, first + i, 4 + i, "kq_turned")

            def turn_v(first):
                pe.wait_ge(emptied, 4 * (GDN_Q[0] + 1))
                pe.wait_ge(sem("silued"), GH + first + 4)
                for i in range(4):
                    if first:
                        pe.wait_ge(sem("v_turned_out"), i + 1)
                    turn(gv, first + i, i, "v_turned")

            def sum_g():
                pe.wait_ge(sem("g_made"), 1)
                pe.wait_ge(sem("kq_squared"), 4)
                pe.matmul(bank[7][:, 0:UNITS], tri, col[:, G, :], start=True, stop=True)
                pe.matmul(bank[7][:, UNITS:2 * UNITS], ones, col[:, G, :], start=True, stop=True)\
                    .then_inc(sem("g_summed"), 1)

            def row_sums(h, b):
                for n in range(TT):
                    g = col[:, G, h * TT + n:h * TT + n + 1].broadcast_to([P, P])
                    done = pe.matmul(bank[b][:, n * P:(n + 1) * P], g, tri, start=True, stop=True)
                return done

            def products(h, b, other):
                for n in range(TT):
                    done = pe.matmul(bank[b][:, n * P:(n + 1) * P], gk[:, h, n * P:(n + 1) * P],
                                     other[:, h, n * P:(n + 1) * P], start=True, stop=True)
                return done

            def rows_and_products(first):
                pe.wait_ge(emptied, 4 * (GDN_Z[0] + 1))
                for h in (first, first + 1):
                    if h >= 2:
                        pe.wait_ge(sem("row_exped"), h - 1)
                        pe.wait_ge(sem("unit_scaled"), h - 1)
                    row_sums(h, h % 2).then_inc(sem("row_made"), 1)
                    products(h, 2 + h % 2, gq).then_inc(sem("unit_prods"), 1)

            def triangles(first):
                g = GDN_V[0] + 1 + first // 4
                pe.wait_ge(emptied, 4 * g)
                if first % 4:
                    pe.wait_ge(sem("triangled"), first)
                for i in range(2):
                    b = (0 if first < 4 else 4) + 2 * i
                    row_sums(first + i, b).then_inc(sem("tri_rows"), 1)
                    products(first + i, b + 1, gk).then_inc(sem("tri_prods"), 1)

            def delta_projections():
                g0, c0, _ = GDN_K

                def beta_a():
                    pe.wait_ge(sem("ba_low"), 1)
                    for k in range(KT):
                        done = three(bank[4][:, :], ba_hi[:, k, :], ba_lo[:, k, :], act_hi[:, k, :], act_lo[:, k, :],
                                     k == 0, k == KT - 1)
                    done.then_inc(sem("ba_full"), 1)

                begin(2, beta_a)
                pe.wait_ge(sem("ba_out"), 1)
                pe.wait_ge(sem("conv_rows_landed"), 16)
                for n in range(TT):
                    pe.transpose(bank[5][:, n * P:(n + 1) * P], ba_t[:, n * P:(n + 1) * P], ident)
                rows = CONV * 3 * KT
                pe.transpose(bank[6][:, 0:rows], conv_rows[:, :], ident[0:rows, 0:rows]).then_inc(sem("small_turned"), 1)
                pe.wait_ge(sem("small_out"), 2)
                group(c0 + 2, 1, 2, True, act_hi, act_lo)
                for gi, (start, features_out, aside) in enumerate((
                        (GDN_V, True, {(0, 1): lambda: turn_k(0), (0, 3): sum_g, (1, 1): lambda: turn_k(4)}),
                        (GDN_V, True, {(0, 1): lambda: triangles(0), (1, 1): lambda: triangles(2)}),
                        (GDN_Q, True, {(0, 1): lambda: triangles(4), (1, 1): lambda: triangles(6)}),
                        (GDN_Q, True, {(0, 1): lambda: turn_v(0), (1, 1): lambda: turn_v(4)}),
                        (GDN_Z, False, {(0, 1): lambda: turn_q(0), (1, 1): lambda: turn_q(4)}),
                        (GDN_Z, False, {(0, 2): lambda: rows_and_products(0), (1, 1): lambda: rows_and_products(2)}))):
                    p = gi % 2
                    pe.wait_ge(emptied, 4 * (start[0] + p - 1))
                    drained(gi)
                    group(start[1] + 2 * p, p, 2, features_out, act_hi, act_lo, aside)

            def turn_k_back(h):
                if h >= 2:
                    pe.wait_ge(sem("k_turned_out"), h - 1)
                turn(gk, h, 6 + h % 2, "k_turned")

            def delta_rule():
                pe.wait_ge(emptied, 4 * GDN_OUT[0])
                for h in range(4, 8):
                    if h >= 6:
                        pe.wait_ge(sem("row_exped"), h - 1)
                    row_sums(h, 4 + h % 2).then_inc(sem("row_made"), 1)
                    pe.wait_ge(sem("unit_scaled"), h - 1)
                    products(h, 2 + h % 2, gq).then_inc(sem("unit_prods"), 1)
                    turn_k_back(h - 4)
                for h in range(4, 8):
                    turn_k_back(h)
                pe.wait_ge(sem("row_exped"), GH)
                pe.wait_ge(sem("unit_scaled"), GH)
                pe.wait_ge(sem("k_turned_out"), GH)
                step = 0
                pe.wait_ge(sem("inv_seeded"), P // BLOCK)
                for batch in range(2):
                    heads = range(4 * batch, 4 * batch + 4)
                    for level in range(len(LEVELS)):
                        for r, h in enumerate(heads):
                            if level:
                                pe.wait_ge(sem("joined"), step - 4 + r + 1)
                            for n in range(TT):
                                done = pe.transpose(bank[r][:, n * P:(n + 1) * P], inv_t[:, h * TT + n, :], ident)
                            done.then_inc(sem("inv_turned"), 1)
                        for r, h in enumerate(heads):
                            pe.wait_ge(sem("inv_placed"), step + r + 1)
                            for n in range(TT):
                                u = h * TT + n
                                done = pe.matmul(bank[r][:, n * P:(n + 1) * P], neg_l_t[:, u, :],
                                                 inv[:, u - batch * UNITS // 2, :], start=True, stop=True)
                            done.then_inc(sem("prod_made"), 1)
                        for r, h in enumerate(heads):
                            pe.wait_ge(sem("prod_out"), step + r + 1)
                            if step >= 4:
                                pe.wait_ge(sem("joined"), step - 4 + r + 1)
                            for n in range(TT):
                                u = h * TT + n
                                done = pe.matmul(bank[4 + r][:, n * P:(n + 1) * P],
                                                 half_prod[:, u - batch * UNITS // 2, :], inv_t[:, u, :],
                                                 start=True, stop=True)
                            done.then_inc(sem("seconds_made"), 1)
                        step += 4
                    for r, h in enumerate(heads):
                        pe.wait_ge(sem("k_grown"), h + 1)
                        pe.wait_ge(sem("joined"), step - 4 + r + 1)
                        for n in range(TT):
                            u = h * TT + n
                            done = pe.matmul(bank[r][:, n * P:(n + 1) * P], k_grown[:, u - batch * UNITS // 2, :],
                                             inv_t[:, u, :], start=True, stop=True)
                        done.then_inc(sem("w_made"), 1)
                    for r, h in enumerate(heads):
                        pe.wait_ge(sem("w_out"), h + 1)
                for n in range(TT):
                    for q in range(2):
                        if n:
                            pe.wait_ge(sem("state_made"), 2 * (n - 1) + q + 1)
                            pe.wait_ge(sem("v_new_made"), 2 * (n - 1) + q + 1)
                        for r in range(4):
                            h = 4 * q + r
                            u = h * TT + n
                            cols = slice(r * P, (r + 1) * P)
                            done = pe.matmul(bank[q][:, cols], inv_t[:, u, :], unit(gv, u), start=True, stop=n == 0)
                            if n:
                                done = pe.matmul(bank[q][:, cols], w_t[:, u, :], states[(n - 1) % 2][:, h, :],
                                                 start=False, stop=True)
                        done.then_inc(sem("v_new_full"), 1)
                    if n >= 2:
                        turn_out(n - 2)
                    for q in range(2):
                        pe.wait_ge(sem("v_new_made"), 2 * n + q + 1)
                        if n < TT - 1:
                            if n:
                                pe.wait_ge(sem("state_made"), 2 * (n - 1) + q + 1)
                            pe.wait_ge(sem("k_faded"), 4 * q + 4)
                            for r in range(4):
                                h = 4 * q + r
                                done = pe.matmul(bank[4 + q][:, r * P:(r + 1) * P], unit(gk, h * TT + n),
                                                 v_new[:, h, :], start=True, stop=True)
                            done.then_inc(sem("state_full"), 1)
                        if n:
                            pe.wait_ge(sem("o_out"), 2 * (n - 1) + q + 1)
                        else:
                            pe.wait_ge(sem("q_grown"), GH)
                        for r in range(4):
                            h = 4 * q + r
                            u = h * TT + n
                            cols = slice(r * P, (r + 1) * P)
                            if n:
                                pe.matmul(bank[2 + q][:, cols], unit(gq, u), states[(n - 1) % 2][:, h, :],
                                          start=True, stop=False)
                            done = pe.matmul(bank[2 + q][:, cols], attn[:, u, :], v_new[:, h, :],
                                             start=n == 0, stop=True)
                        done.then_inc(sem("o_full"), 1)
                turn_out(TT - 2)

            def turn_out(n):
                pe.wait_ge(sem("o_scaled"), n + 1)
                if n:
                    pe.wait_ge(sem("o_low"), 2 * n)
                for h in range(GH):
                    done = pe.transpose(bank[6 + h // 4][:, h % 4 * P:(h % 4 + 1) * P],
                                        gz[:, n, h * P:(h + 1) * P], ident)
                done.then_inc(sem("o_turned"), 1)

            def first_gdn_out():
                c = GDN_OUT[1]
                pe.wait_ge(sem("o_out"), 2 * TT)
                for m, j in ((0, 0), (1, 0), (2, 0), (0, 1), (3, 0), (1, 1), (2, 1), (3, 1)):
                    pe.wait_ge(sem("o_low"), 2 * TT if m == 3 else 2 * (m + 1))
                    if (m, j) == (0, 1):
                        turn_out(TT - 1)
                    done = part(c, j, 0, 2, m, False, go_hi, go_lo, fresh=m == 0)
                    if j:
                        done.then_inc(bank_full, 1)
                    elif m == 3:
                        done.then_inc(chunk_used, 1)

            pe.wait_ge(sem("const_landed"), 16)
            begin(0)
            rest(RET_QK, 4)
            groups(RET_V, 8, 2, False, act_hi, act_lo)
            retention()
            group(RET_OUT[1], 0, 4, False, y_hi, y_lo, {(0, 1): lambda: turn_y(8, 12), (0, 3): lambda: turn_y(12, 16)},
                  tiles=(sem("y_low"), 0))
            last_group(1, RET_OUT, 4, y_hi, y_lo)
            mlp(0)
            delta_projections()
            delta_rule()
            first_gdn_out()
            last_group(3, GDN_OUT, 2, go_hi, go_lo)
            mlp(1)

        @block.scalar
        def _(act):
            chain = Chain(act, "act_step")

            def high(slot):
                for half in range(2):
                    kt = slice(half * CK // 2, (half + 1) * CK // 2)
                    act.activation(w_hi[:, slot, kt, :], w_raw[:, slot, kt, :], ACT.Copy).then_inc(w_high, 1)

            def splits(start, i, chunks, first=1, last=None):
                g0, c0, u0 = start
                for j in range(first, (last or chunks) + 1):
                    act.wait_ge(w_landed[j % 2], i * (8 * chunks) + 16 * ((c0 + j) // 2 + 1))
                    if j == 1:
                        if g0 or not isinstance(i, int) or i:
                            act.wait_ge(bank_full, i * 4 + 4 * g0)
                    else:
                        act.wait_ge(chunk_used, i * (chunks - 1) + (u0 + j - 1))
                    high(j % 2)

            def empty(start, i, p, m, dst, func=ACT.Copy):
                act.wait_ge(bank_full, i * 4 + (4 * start[0] + m + 1))
                act.activation(dst, bank[4 * p + m][:, :], func).then_inc(emptied, 1)

            def load_gains(b):
                for n, row in enumerate(GAIN_ROWS[b]):
                    if row is not None:
                        act.dma_start(gains[:, n, :], norm_gains[row[0], row[1], :].partition_broadcast(P))\
                            .then_inc(sem("gains_landed"), 16)

            def root(m, ss, to, bias, done):
                act.activation(stat[:, to, m:m + 1], stat[:, ss, m:m + 1], ACT.Sqrt, scale=1.0 / D, bias=bias)\
                    .then_inc(sem(done), 1)

            def sum_squares(src, m, where):
                chain.link(act.activation(dump[:, 0:src.shape[-1]], src, ACT.Square, accum_out=stat[:, where, m:m + 1]))

            def half_squares(b):
                for m in range(TT):
                    act.wait_ge(emptied, 4 * (NEXT_GROUP[b] - 2) + m + 1)
                    act.activation(dump[:, 0:GC], mix[:, m, 0:GC], ACT.Square, accum_out=stat[:, SS_HALF, m:m + 1])\
                        .then_inc(sem("half_squared"), 1)
                    act.wait_ge(sem("half_squared"), TT * (b - 1) + m + 1)

            def mix_root(b, m):
                if b == 0:
                    return
                act.wait_ge(emptied, 4 * (NEXT_GROUP[b] - 1) + m + 1)
                sum_squares(mix[:, m, GC:2 * GC], m, SS_MIX)
                act.wait_ge(sem("half_eps_made"), TT * b)
                root(m, SS_MIX, ROOT_MIX, stat[:, HALF_EPS, m:m + 1], "mix_rooted")

            def resid_root(b, m):
                if b:
                    act.wait_ge(sem("residual_done"), TT * (b - 1) + m + 1)
                else:
                    act.wait_ge(sem(f"x_landed{m}"), 16)
                sum_squares(resid[:, m, :], m, SS_RES)
                root(m, SS_RES, ROOT_RES, eps, "resid_rooted")

            def norm_share(b, m):
                act.wait_ge(sem("share_gained"), 2 * b + m + 1)
                act.wait_ge(sem("rstd_made"), TT * b + m + 1)
                share = normed[:, m, GC:2 * GC]
                act.activation(share, share, ACT.Copy, scale=stat[:, RSTD_RES, m:m + 1])\
                    .then_inc(sem("normed_share"), 1)

            def high_acts(b, m):
                act.wait_ge(sem("acts_transposed"), TT * b + m + 1)
                for half in range(2):
                    act.activation(act_hi[:, 4 * half:4 * half + 4, m * P:(m + 1) * P],
                                   tall(bank[2 * m + half]), ACT.Copy).then_inc(sem("act_high"), 1)

            def norms(b, before, after):
                mix_root(b, 0)
                mix_root(b, 1)
                resid_root(b, 0)
                if before:
                    splits(*before)
                if b:
                    norm_share(b, 0)
                    resid_root(b, 1)
                else:
                    resid_root(b, 1)
                    norm_share(b, 0)
                norm_share(b, 1)
                if not before:
                    act.wait_ge(w_landed[0], 16)
                    high(0)
                high_acts(b, 0)
                high_acts(b, 1)
                mix_root(b, 2)
                splits(after, 0, 2, 1, 1)
                mix_root(b, 3)
                resid_root(b, 2)
                resid_root(b, 3)
                high_acts(b, 2)
                high_acts(b, 3)

            load_gains(0)
            act.dma_start(square[:, :, :], square_c).then_inc(sem("const_landed"), 16)
            act.dma_start(rope[:, :, :], rope_c).then_inc(sem("rope_landed"), 16)
            act.wait_ge(sem("eps_set"), 1)
            chain.link(act.activation(stat[:, ROOT_MIX, 0:1], eps, ACT.Sqrt))

            norms(0, None, RET_QK)
            act.wait_ge(sem("normed"), TT)
            act.wait_ge(sem("normed_share"), 2)
            act.dma_start(gains[:, :, :].rearrange("p a n -> p (a n)"), ret_gn_gain[0].partition_broadcast(P))\
                .then_inc(sem("gn_gain_landed"), 16)

            for i in range(4):
                splits(RET_QK, i, 2, first=1 if i else 2)
                for m in range(4):
                    empty(RET_QK, i, i % 2, m, qk_t[:, 4 * i + m, :])
            with act.Fori(0, 2) as i2:
                for p in range(2):
                    i = i2 * 2 + p
                    splits(RET_V, i, 2)
                    for m in range(4):
                        empty(RET_V, i, p, m, v_tm[:, m, bass.ds(i * GC, GC)])
            act.wait_ge(sem("roped"), KT)
            with act.Fori(0, 2) as i2:
                for p in range(2):
                    i = i2 * 2 + p
                    splits(RET_G, i, 2)
                    for m in range(4):
                        empty(RET_G, i, p, m, gate[:, m, bass.ds(i * GC, GC)], ACT.Silu)
            act.dma_start(decay[:, :, :], decay_c).then_inc(sem("decay_landed"), 16)
            act.wait_ge(sem("gate_gained"), 4 * TT)
            load_gains(1)
            splits(RET_OUT, 0, 4, last=1)
            for n in range(RH * TT + 1):
                if n < RH * TT:
                    act.wait_ge(sem("varied"), n + 1)
                    act.activation(bn[:, n, BN_ROOT:BN_ROOT + 1], bn[:, n, BN_VAR:BN_VAR + 1], ACT.Sqrt, bias=eps)\
                        .then_inc(sem("gn_rooted"), 1)
                if n:
                    h, m = (n - 1) // TT, (n - 1) % TT
                    act.wait_ge(sem("gn_inverted"), n)
                    y = gate[:, m, h * RV:(h + 1) * RV]
                    act.activation(y, y, ACT.Copy, scale=bn[:, n - 1, BN_RSTD:BN_RSTD + 1])\
                        .then_inc(sem("y_scaled"), 1)
            for n in range(RH * TT):
                h, m = n // TT, n % TT
                act.wait_ge(sem("y_transposed"), n + 1)
                act.activation(y_hi[:, 4 * h:4 * h + 4, m * P:(m + 1) * P], tall(y_bank(n)), ACT.Copy)\
                    .then_inc(sem("y_high"), 1)
            splits(RET_OUT, 0, 4, first=2)
            splits(RET_OUT, 1, 4, last=1)
            half_squares(1)
            splits(RET_OUT, 1, 4, first=2, last=3)
            norms(1, (RET_OUT, 1, 4, 4, 4), MLP[0][0][0])

            def mlp(layer):
                def up_group(i, p, first=1):
                    splits(up, i, 2, first)
                    for m in range(4):
                        empty(up, i, p, m, relu[:, m, :], ACT.Relu)
                    act.wait_ge(sem("squared"), i * 4 + (HALF_TILES * (2 * layer + half) + 4))

                for half, (up, down) in enumerate(MLP[layer]):
                    if half:
                        with act.Fori(0, 2) as i2:
                            for p in range(2):
                                up_group(i2 * 2 + p, p)
                    else:
                        for i in range(4):
                            up_group(i, i % 2, first=1 if i else 2)
                    splits(down, 0, 4)
                    if half == 0:
                        for m in range(TT):
                            empty(down, 0, 0, m, mix[:, m, 0:GC])
                        splits(down, 1, 4)
                        for m in range(TT):
                            empty(down, 1, 1, m, mix[:, m, GC:2 * GC])
                splits(down, 1, 4, last=1)
                half_squares(2 * layer + 2)
                splits(down, 1, 4, first=2, last=3)
                if layer:
                    for m in range(TT):
                        mix_root(4, m)
                else:
                    norms(2, (down, 1, 4, 4, 4), GDN_K)

            act.wait_ge(sem("normed"), 2 * TT)
            act.wait_ge(sem("normed_share"), 4)
            load_gains(2)
            mlp(0)

            act.dma_start(conv_rows[:, :], gdn_conv_w[0].rearrange("j (k p) -> (j k) p", p=P))\
                .then_inc(sem("conv_rows_landed"), 16)
            act.dma_start(join_f[:, :, :], join_c).then_inc(sem("join_landed"), 16)
            act.dma_start(z_gain[:, :], gdn_norm_gain[0].partition_broadcast(P)).then_inc(sem("rows_landed"), 16)
            act.dma_start(head_rows[:, 0, :], gdn_dt_bias[0].partition_broadcast(P)).then_inc(sem("rows_landed"), 16)
            act.dma_start(head_rows[:, 1, :], gdn_a_log[0].partition_broadcast(P)).then_inc(sem("rows_landed"), 16)
            act.wait_ge(sem("ba_cleared"), 1)
            act.wait_ge(sem("ba_landed"), 16)
            act.activation(ba_hi[:, :, 0:2 * GH], ba_raw[:, :, :], ACT.Copy).then_inc(sem("ba_high"), 1)
            act.wait_ge(sem("ba_full"), 1)
            act.activation(ba_t[:, :], bank[4][:, :], ACT.Copy).then_inc(sem("ba_out"), 1)
            order = [(GDN_K, gk), (GDN_V, gv), (GDN_Q, gq)]

            def silu(gi):
                for m in range(4):
                    act.wait_ge(sem("convolved"), 4 * gi + m + 1)
                    t = order[gi // 2][1][:, gi % 2 * 4 + m, :]
                    act.activation(t, t, ACT.Silu).then_inc(sem("silued"), 1)

            def square_heads(first, last):
                for i in range(first, last):
                    act.wait_ge(sem("kq_turned"), i + 1)
                    for n in range(TT):
                        u = i % GH * TT + n
                        done = act.activation(squares[:, i % 2, n, :], bank[4 + i % 4][:, n * P:(n + 1) * P],
                                              ACT.Square, accum_out=col[:, (SS_K, SS_Q)[i // GH], u:u + 1])
                    done.then_inc(sem("kq_squared"), 1)
                    act.wait_ge(sem("kq_squared"), i + 1)

            def row_exps(h):
                act.wait_ge(sem("row_shifted"), h + 1)
                if h >= 2:
                    act.wait_ge(sem("q_grown"), h - 1)
                act.activation(tmp[:, 2 + h % 2, :], bank[(0 if h < 4 else 4) + h % 2][:, :], ACT.Exp)\
                    .then_inc(sem("row_exped"), 1)
                act.activation(tmp[:, h % 2, :], tmp[:, h % 2, :], ACT.Exp).then_inc(sem("decay_made"), 1)

            def tri_exps(first):
                for h in (first, first + 1):
                    act.wait_ge(sem("tri_shifted"), h + 1)
                    act.activation(tmp[:, h % 2, :], tmp[:, h % 2, :], ACT.Exp).then_inc(sem("tri_exped"), 1)

            def v_out(first):
                for h in range(first, first + 4):
                    act.wait_ge(sem("v_turned"), h + 1)
                    act.wait_ge(sem("cols_k"), 1)
                    for n in range(TT):
                        u = h * TT + n
                        done = act.activation(gv[:, h, n * P:(n + 1) * P], bank[h % 4][:, n * P:(n + 1) * P],
                                              ACT.Copy, scale=col[:, N_K, u:u + 1])
                    done.then_inc(sem("v_turned_out"), 1)

            for gi in range(8):
                start, p = (order + [(GDN_Z, None)])[gi // 2][0], gi % 2
                if gi:
                    splits(start, p, 2, last=1)
                else:
                    splits(start, p, 2, first=2)
                    act.wait_ge(sem("small_turned"), 1)
                    act.activation(ba_cols[:, :, :], tall(bank[5])[:, :, 0:2 * GH], ACT.Copy)\
                        .then_inc(sem("small_out"), 1)
                    rows = CONV * 3 * KT
                    act.activation(conv_w[:, :, :].rearrange("p j k -> p (j k)"), bank[6][:, 0:rows], ACT.Copy)\
                        .then_inc(sem("small_out"), 1)
                if gi == 1:
                    act.wait_ge(sem("cols_a"), 1)
                    act.activation(ct[:, 2:4, :], ct[:, 0:2, :], ACT.Exp).then_inc(sem("cols_b"), 1)
                    act.wait_ge(sem("rows_landed"), 48)
                    act.activation(head_rows[:, 2, :], head_rows[:, 1, :], ACT.Exp).then_inc(sem("cols_b"), 1)
                    act.wait_ge(sem("cols_c"), 1)
                    act.activation(ct[:, 6, :], ct[:, 5, :], ACT.Ln).then_inc(sem("cols_d"), 1)
                if gi == 2:
                    square_heads(0, 4)
                if gi == 5:
                    v_out(0)
                if gi == 6:
                    square_heads(GH, GH + 4)
                    silu(5)
                if gi == 7:
                    act.wait_ge(sem("kq_x_made"), 2)
                    act.activation(ct[:, 3, :], ct[:, 1, :], ACT.Sqrt).then_inc(sem("kq_rooted"), 1)
                if gi:
                    splits(start, p, 2, first=2)
                if gi == 2:
                    act.wait_ge(sem("g_summed"), 1)
                    act.activation(col[:, EXP_G, :], bank[7][:, 0:UNITS], ACT.Exp)
                    act.activation(col[:, EXP_TOT, :], bank[7][:, UNITS:2 * UNITS], ACT.Exp)\
                        .then_inc(sem("g_sums_read"), 1)
                    act.wait_ge(sem("rest_made"), 1)
                    act.activation(ct[:, 8, :], ct[:, 7, :], ACT.Exp).then_inc(sem("rest_exped"), 1)
                if gi in (3, 4):
                    tri_exps(4 * (gi - 3))
                if 1 <= gi < 6:
                    silu(gi - 1)
                if gi == 2:
                    square_heads(4, GH)
                    act.wait_ge(sem("kq_x_made"), 1)
                    act.activation(ct[:, 2, :], ct[:, 0, :], ACT.Sqrt).then_inc(sem("kq_rooted"), 1)
                if gi in (3, 4):
                    tri_exps(4 * (gi - 3) + 2)
                if gi == 5:
                    v_out(4)
                if gi == 6:
                    square_heads(GH + 4, 2 * GH)
                if gi == 7:
                    act.wait_ge(sem("blocks_done"), 1)
                    for h in range(4):
                        row_exps(h)
                for m in range(4):
                    if gi < 6:
                        if gi:
                            act.wait_ge(sem("convolved"), 4 * (gi - 1) + m + 1)
                        else:
                            act.wait_ge(sem("pad_cleared"), 1)
                        empty(start, p, p, m, pad[:, m, CONV - 1:CONV - 1 + T])
                    else:
                        empty(start, p, p, m, gz[:, m, p * GC:(p + 1) * GC], ACT.Silu)

            def k_back(h):
                act.wait_ge(sem("k_turned"), h + 1)
                act.activation(gk[:, h, :], bank[6 + h % 2][:, :], ACT.Copy).then_inc(sem("k_turned_out"), 1)

            for h in range(4, GH):
                row_exps(h)
                k_back(h - 4)
            for h in range(4, GH):
                k_back(h)
            act.wait_ge(sem("q_grown"), GH)
            act.wait_ge(sem("unit_scaled"), GH)
            load_gains(3)
            splits(GDN_OUT, 0, 2, last=1)
            step = 0
            for batch in range(2):
                heads = range(4 * batch, 4 * batch + 4)
                for level in range(len(LEVELS)):
                    for r in range(4):
                        act.wait_ge(sem("inv_turned"), step + r + 1)
                        act.activation(inv[:, 4 * r:4 * r + 4, :], tall(bank[r]), ACT.Copy)\
                            .then_inc(sem("inv_placed"), 1)
                    for r in range(4):
                        act.wait_ge(sem("prod_made"), step + r + 1)
                        act.activation(half_prod[:, 4 * r:4 * r + 4, :], tall(bank[r]), ACT.Copy)\
                            .then_inc(sem("prod_out"), 1)
                    step += 4
                for r, h in enumerate(heads):
                    act.wait_ge(sem("w_made"), h + 1)
                    act.activation(w_t[:, h * TT:(h + 1) * TT, :], tall(bank[r]), ACT.Copy, scale=-1.0)\
                        .then_inc(sem("w_out"), 1)
            outs = gv[:, :, :].rearrange("p h (n e) -> p h n e", n=TT)

            def high_out(n):
                act.wait_ge(sem("o_turned"), n + 1)
                for half in range(2):
                    act.activation(go_hi[:, 4 * half:4 * half + 4, n * P:(n + 1) * P], tall(bank[6 + half]),
                                   ACT.Copy).then_inc(sem("o_high"), 1)

            def root_out(n):
                act.wait_ge(sem("o_summed"), n + 1)
                act.activation(on[:, n, 1, :], on[:, n, 0, :], ACT.Sqrt, scale=1.0 / P, bias=eps)\
                    .then_inc(sem("o_rooted"), 1)

            for n in range(TT):
                if n >= 2:
                    high_out(n - 2)
                if n:
                    root_out(n - 1)
                act.wait_ge(sem("o_out"), 2 * n + 2)
                if n:
                    act.wait_ge(sem("o_summed"), n)
                act.activation(o_sq[:, :, :], outs[:, :, n, :], ACT.Square).then_inc(sem("o_squared"), 1)
            high_out(TT - 2)
            root_out(TT - 1)
            high_out(TT - 1)
            splits(GDN_OUT, 0, 2, first=2)
            splits(GDN_OUT, 1, 2, last=1)
            half_squares(3)
            norms(3, (GDN_OUT, 1, 2, 2, 2), MLP[1][0][0])
            act.wait_ge(sem("normed"), 4 * TT)
            act.wait_ge(sem("normed_share"), 8)
            load_gains(4)
            mlp(1)

        @block.vector
        def _(dve):
            chain = Chain(dve, "dve_step")
            link = chain.link

            def inv_root(x, root, temp, out_, scale=1.0, add=EPS):
                t = [temp(n) for n in range(3)]
                dve.tensor_scalar(t[0], x, scale, add, ALU.mult, ALU.add)
                link(dve.reciprocal(t[1], root))
                link(dve.tensor_tensor(t[2], t[0], t[1], ALU.mult))
                link(dve.tensor_tensor(t[2], t[2], t[1], ALU.mult))
                link(dve.tensor_scalar(t[2], t[2], -0.5, 1.5, ALU.mult, ALU.add))
                return dve.tensor_tensor(out_, t[1], t[2], ALU.mult)

            def col_of(n, m):
                return stat[:, n, m:m + 1]

            def first_half(b, more):
                g0 = NEXT_GROUP[b] - 2
                dve.wait_ge(sem("gains_landed"), GAINS_LANDED[b])
                dve.wait_ge(emptied, 4 * g0)
                for m in range(TT):
                    take_out(b, 0, m, more)
                for m in range(TT):
                    dve.wait_ge(sem("half_squared"), TT * (b - 1) + m + 1)
                    dve.tensor_scalar(col_of(HALF_EPS, m), col_of(SS_HALF, m), 1.0 / D, EPS, ALU.mult, ALU.add)\
                        .then_inc(sem("half_eps_made"), 1)
                    dve.tensor_tensor(mix[:, m, 0:GC], mix[:, m, 0:GC], gains[:, 0, 0:GC], ALU.mult)\
                        .then_inc(sem("half_gained"), 1)

            def take_out(b, p, m, more):
                dve.wait_ge(bank_full, 4 * (NEXT_GROUP[b] - 2 + p) + m + 1)
                dst = mix[:, m, p * GC:(p + 1) * GC]
                if more:
                    dve.tensor_tensor(dst, dst, bank[4 * p + m][:, :], ALU.add).then_inc(emptied, 1)
                else:
                    dve.tensor_copy(dst, bank[4 * p + m][:, :]).then_inc(emptied, 1)

            def mix_rstd(b, m):
                dve.wait_ge(sem("mix_rooted"), TT * (b - 1) + m + 1)
                link(inv_root(col_of(SS_MIX, m), col_of(ROOT_MIX, m), lambda n: col_of(NEWTON + n, m),
                              col_of(RSTD_MIX, m), 1.0 / D, col_of(HALF_EPS, m)))

            def add_mix(b, m):
                dve.wait_ge(sem("half_gained"), TT * b)
                low, high = slice(0, GC), slice(GC, 2 * GC)
                dve.scalar_tensor_tensor(resid[:, m, low], mix[:, m, low], col_of(RSTD_MIX, m), resid[:, m, low],
                                         ALU.mult, ALU.add).then_inc(sem("residual_low"), 1)
                link(dve.scalar_tensor_tensor(mix[:, m, high], mix[:, m, high], col_of(RSTD_MIX, m), gains[:, 0, high],
                                              ALU.mult, ALU.mult))
                dve.tensor_tensor(resid[:, m, high], resid[:, m, high], mix[:, m, high], ALU.add)\
                    .then_inc(sem("residual_done"), 1)

            def norm_tile(b, m):
                if b:
                    dve.wait_ge(sem("residual_done"), TT * (b - 1) + m + 1)
                dve.wait_ge(sem("resid_rooted"), TT * b + m + 1)
                inv_root(col_of(SS_RES, m), col_of(ROOT_RES, m), lambda n: col_of(NEWTON + n, m),
                         col_of(RSTD_RES, m), 1.0 / D).then_inc(sem("rstd_made"), 1)
                dve.wait_ge(sem("rstd_made"), TT * b + m + 1)
                if m >= 2:
                    dve.wait_ge(sem("acts_transposed"), TT * b + m - 1)
                elif b:
                    dve.wait_ge(sem("acts_transposed"), TT * (b - 1) + m + 3)
                cols = slice(0, GC if m < 2 else D)
                dve.scalar_tensor_tensor(normed[:, m % 2, cols], resid[:, m, cols], col_of(RSTD_RES, m),
                                         gains[:, 1, cols], ALU.mult, ALU.mult).then_inc(sem("normed"), 1)

            def low_acts(b, m):
                for half in range(2):
                    dve.wait_ge(sem("act_high"), 2 * (TT * b + m) + half + 1)
                    where = (slice(None), slice(4 * half, 4 * half + 4), slice(m * P, (m + 1) * P))
                    dve.tensor_tensor(act_lo[where], tall(bank[2 * m + half]), act_hi[where].bitcast(F32),
                                      ALU.subtract).then_inc(sem("act_low"), 1)

            def norms(b, more=False):
                if b == 0:
                    dve.wait_ge(sem("gains_landed"), GAINS_LANDED[0])
                else:
                    take_out(b, 1, 0, more)
                    mix_rstd(b, 0)
                    take_out(b, 1, 1, more)
                    add_mix(b, 0)
                    mix_rstd(b, 1)
                    add_mix(b, 1)
                if b < 4:
                    norm_tile(b, 0)
                    norm_tile(b, 1)
                if b:
                    take_out(b, 1, 2, more)
                if b < 4:
                    low_acts(b, 0)
                    low_acts(b, 1)
                if b:
                    take_out(b, 1, 3, more)
                    for m in (2, 3):
                        mix_rstd(b, m)
                        add_mix(b, m)
                if b < 4:
                    norm_tile(b, 2)
                    norm_tile(b, 3)
                    low_acts(b, 2)
                    low_acts(b, 3)

            dve.memset(stat[:, :, :], EPS).then_inc(sem("eps_set"), 1)
            dve.wait_ge(sem("eps_set"), 1)
            norms(0)

            dve.wait_ge(sem("rope_landed"), 16)
            cos, sin = rope[:, 0, :], rope[:, 1, :]
            for n in range(KT):
                dve.wait_ge(emptied, 2 * n + 2)
                x1, x2 = qk_t[:, 2 * n, :], qk_t[:, 2 * n + 1, :]
                dve.tensor_tensor(rope_tmp[:, 0, :], x1, cos, ALU.mult)
                dve.tensor_tensor(rope_tmp[:, 1, :], x2, sin, ALU.mult)
                dve.tensor_tensor(rope_tmp[:, 2, :], x1, sin, ALU.mult)
                link(dve.tensor_tensor(rope_tmp[:, 3, :], x2, cos, ALU.mult))
                dve.tensor_tensor(x1, rope_tmp[:, 0, :], rope_tmp[:, 1, :], ALU.subtract)
                dve.tensor_tensor(x2, rope_tmp[:, 2, :], rope_tmp[:, 3, :], ALU.add).then_inc(sem("roped"), 1)
                dve.wait_ge(sem("roped"), n + 1)
            dve.wait_ge(sem("gn_gain_landed"), 16)
            with dve.Fori(0, 4) as i:
                for m in range(TT):
                    dve.wait_ge(emptied, i * 4 + (4 * RET_G[0] + m + 1))
                    g = gate[:, m, bass.ds(i * GC, GC)]
                    dve.tensor_tensor(g, g, gains[:, :, :].rearrange("p a n -> p (a n)")[:, bass.ds(i * GC, GC)],
                                      ALU.mult).then_inc(sem("gate_gained"), 1)
            dve.wait_ge(sem("gate_gained"), 4 * TT)
            dve.wait_ge(sem("decay_landed"), 16)

            def decayed(h):
                for i in range(TT):
                    dve.wait_ge(sem("scored"), TT * h + i + 1)
                    if h >= 2:
                        dve.wait_ge(sem("attended"), TT * (h - 1))
                    dve.tensor_tensor(score[:, h % 2, i, i * P:T], bank[i][:, 0:T - i * P],
                                      decay[:, h, 0:T - i * P], ALU.mult).then_inc(sem("decayed"), 1)

            def inverted(n):
                dve.wait_ge(sem("gn_rooted"), n + 1)
                inv_root(bn[:, n, BN_VAR:BN_VAR + 1], bn[:, n, BN_ROOT:BN_ROOT + 1],
                         lambda t: bn[:, n, BN_NEWTON + t:BN_NEWTON + t + 1], bn[:, n, BN_RSTD:BN_RSTD + 1])\
                    .then_inc(sem("gn_inverted"), 1)

            decayed(0)
            for h in range(RH):
                if h + 1 < RH:
                    decayed(h + 1)
                for m in range(TT):
                    n = TT * h + m
                    dve.wait_ge(sem("attended"), n + 1)
                    link(dve.bn_stats(bn[:, n, 0:6], bank[4 + m][:, :]))
                    dve.bn_aggr(bn[:, n, BN_MEAN:BN_VAR + 1], bn[:, n, 0:6]).then_inc(sem("varied"), 1)
                    dve.wait_ge(sem("varied"), n + 1)
                    y = gate[:, m, h * RV:(h + 1) * RV]
                    dve.scalar_tensor_tensor(y, bank[4 + m][:, :], bn[:, n, BN_MEAN:BN_MEAN + 1], y,
                                             ALU.subtract, ALU.mult).then_inc(sem("y_gated"), 1)
                    inverted(n)
            for n in range(RH * TT):
                h, m = n // TT, n % TT
                dve.wait_ge(sem("y_high"), n + 1)
                where = (slice(None), slice(4 * h, 4 * h + 4), slice(m * P, (m + 1) * P))
                dve.tensor_tensor(y_lo[where], tall(y_bank(n)), y_hi[where].bitcast(F32), ALU.subtract)\
                    .then_inc(sem("y_low"), 1)
            first_half(1, False)
            norms(1)

            def mlp(layer):
                for half, (up, down) in enumerate(MLP[layer]):
                    base = HALF_TILES * (2 * layer + half)
                    with dve.Fori(0, 4) as i:
                        for m in range(4):
                            dve.wait_ge(emptied, i * 4 + (4 * up[0] + m + 1))
                            dve.tensor_tensor(relu_sq[:, m, :], relu[:, m, :], relu[:, m, :], ALU.mult)\
                                .then_inc(sem("squared"), 1)
                            dve.wait_ge(sem("squared"), i * 4 + (base + m + 1))
                            dve.tensor_copy(hid_hi[:, bass.ds(i * 4 + m, 1), :], relu_sq[:, m:m + 1, :])\
                                .then_inc(sem("hid_high"), 1)
                            dve.wait_ge(sem("hid_high"), i * 4 + (base + m + 1))
                            dve.tensor_tensor(hid_lo[:, bass.ds(i * 4 + m, 1), :], relu_sq[:, m:m + 1, :],
                                              hid_hi[:, bass.ds(i * 4 + m, 1), :].bitcast(F32), ALU.subtract)\
                                .then_inc(sem("hid_low"), 1)

                first_half(2 * layer + 2, True)
                norms(2 * layer + 2, True)

            mlp(0)

            dve.wait_ge(sem("ba_high"), 1)
            dve.tensor_tensor(ba_lo[:, :, 0:2 * GH], ba_raw[:, :, :], ba_hi[:, :, 0:2 * GH].bitcast(F32), ALU.subtract)\
                .then_inc(sem("ba_low"), 1)
            dve.wait_ge(sem("join_landed"), 16)
            dve.tensor_copy(join[:, :, :], join_f[:, :, :]).then_inc(sem("join_cast"), 1)

            def by_unit(t, first):
                return t[:, :, first:first + GH].rearrange("p n h -> p h n")

            def units_of(c):
                return c.rearrange("p (h n) -> p h n", n=TT)

            def spread(row):
                return row.rearrange("p (h o) -> p h o", o=1).broadcast_to([P, GH, TT])

            def columns_before():
                dve.wait_ge(sem("small_out"), 1)
                dve.wait_ge(sem("rows_landed"), 48)
                link(dve.tensor_scalar(units_of(ct[:, 0, :]), by_unit(ba_cols, 0), -1.0, None, ALU.mult))
                link(dve.tensor_tensor(units_of(ct[:, 4, :]), by_unit(ba_cols, GH), spread(head_rows[:, 0, :]), ALU.add))
                link(dve.tensor_scalar(ct[:, 9, :], ct[:, 4, :], -1.0, None, ALU.mult))
                dve.tensor_tensor(ct[:, 1, :], ct[:, 9, :], ct[:, 4, :], ALU.min).then_inc(sem("cols_a"), 1)
                dve.wait_ge(sem("cols_b"), 2)
                dve.tensor_scalar(ct[:, 5, :], ct[:, 3, :], 1.0, None, ALU.add).then_inc(sem("cols_c"), 1)
                dve.wait_ge(sem("cols_c"), 1)

            def columns_after():
                link(dve.tensor_scalar(ct[:, 10, :], ct[:, 2, :], 1.0, None, ALU.add))
                link(dve.reciprocal(col[:, BETA, :], ct[:, 10, :]))
                link(dve.tensor_scalar(ct[:, 11, :], ct[:, 5, :], -1.0, 1e-30, ALU.add, ALU.max))
                link(dve.reciprocal(ct[:, 12, :], ct[:, 11, :]))
                dve.wait_ge(sem("cols_d"), 1)
                link(dve.tensor_tensor(ct[:, 13, :], ct[:, 6, :], ct[:, 3, :], ALU.mult))
                link(dve.tensor_tensor(ct[:, 13, :], ct[:, 13, :], ct[:, 12, :], ALU.mult))
                link(dve.scalar_tensor_tensor(ct[:, 14, :], ct[:, 5, :], 1.0, ct[:, 3, :], ALU.is_equal, ALU.mult))
                link(dve.scalar_tensor_tensor(ct[:, 13, :], ct[:, 4, :], 0.0, ct[:, 13, :], ALU.max, ALU.add))
                link(dve.tensor_tensor(ct[:, 13, :], ct[:, 13, :], ct[:, 14, :], ALU.add))
                dve.scalar_tensor_tensor(units_of(col[:, G, :]), units_of(ct[:, 13, :]), -1.0,
                                         spread(head_rows[:, 2, :]), ALU.mult, ALU.mult).then_inc(sem("g_made"), 1)

            order = [(GDN_K, gk, KT), (GDN_V, gv, 2 * KT), (GDN_Q, gq, 0)]
            dve.wait_ge(sem("pad_cleared"), 1)
            columns_before()
            dve.wait_ge(sem("small_out"), 2)
            def over(c, n=P):
                return c.rearrange("p (k o) -> p k o", o=1).broadcast_to([P, c.shape[-1], n])

            def column(c, u):
                return col[:, c, u:u + 1]

            def convolve(gi):
                start, dest, tile0 = order[gi // 2]
                p = gi % 2
                for m in range(4):
                    dve.wait_ge(emptied, 4 * (start[0] + p) + m + 1)
                    t = dest[:, 4 * p + m, :]
                    w = [conv_w[:, j, tile0 + 4 * p + m:tile0 + 4 * p + m + 1] for j in range(CONV)]
                    link(dve.tensor_scalar(t, pad[:, m, 0:T], w[0], None, ALU.mult))
                    for j in range(1, CONV):
                        step = dve.scalar_tensor_tensor(t, pad[:, m, j:j + T], w[j], t, ALU.mult, ALU.add)
                        if j < CONV - 1:
                            link(step)
                    step.then_inc(sem("convolved"), 1)

            def g_sums():
                dve.wait_ge(sem("g_sums_read"), 1)
                link(dve.tensor_copy(col[:, GCUM, :], bank[7][:, 0:UNITS]))
                link(dve.tensor_tensor(ct[:, 7, :], bank[7][:, UNITS:2 * UNITS], col[:, GCUM, :], ALU.subtract))
                dve.sem_inc(sem("rest_made"), 1)
                dve.sem_inc(sem("g_sums_read"), 1)

            def k_columns():
                dve.wait_ge(sem("kq_squared"), GH)
                link(dve.tensor_scalar(ct[:, 0, :], col[:, SS_K, :], EPS, None, ALU.add))
                dve.sem_inc(sem("kq_x_made"), 1)
                dve.wait_ge(sem("kq_rooted"), 1)
                link(inv_root(col[:, SS_K, :], ct[:, 2, :], lambda n: ct[:, 9 + n, :], col[:, R_K, :]))
                rk = col[:, R_K, :]
                link(dve.tensor_tensor(col[:, S_V, :], col[:, BETA, :], rk, ALU.mult))
                link(dve.scalar_tensor_tensor(col[:, S_U, :], rk, -1.0, col[:, S_V, :], ALU.mult, ALU.mult))
                dve.wait_ge(sem("rest_exped"), 1)
                link(dve.tensor_tensor(col[:, EXP_REST, :], ct[:, 8, :], rk, ALU.mult))
                dve.tensor_tensor(col[:, N_K, :], ct[:, 0, :], rk, ALU.mult).then_inc(sem("cols_k"), 1)

            def q_columns():
                dve.wait_ge(sem("kq_squared"), 2 * GH)
                link(dve.tensor_scalar(ct[:, 1, :], col[:, SS_Q, :], EPS, None, ALU.add))
                dve.sem_inc(sem("kq_x_made"), 1)
                dve.wait_ge(sem("kq_rooted"), 2)
                link(inv_root(col[:, SS_Q, :], ct[:, 3, :], lambda n: ct[:, 9 + n, :], ct[:, 12, :]))
                link(dve.tensor_scalar(col[:, R_Q, :], ct[:, 12, :], float(P) ** -0.5, None, ALU.mult))

            def shifted(h, b):
                for n in range(TT):
                    cols = slice(n * P, (n + 1) * P)
                    step = dve.scalar_tensor_tensor(tmp[:, h % 2, cols], bank[b][:, cols], column(GCUM, h * TT + n),
                                                    neg, ALU.subtract, ALU.add)
                return step

            def triangle(h):
                b = (0 if h < 4 else 4) + 2 * (h % 2)
                dve.wait_ge(sem("tri_prods"), h + 1)
                dve.wait_ge(sem("tri_exped"), h + 1)
                for n in range(TT):
                    u = h * TT + n
                    cols = slice(n * P, (n + 1) * P)
                    step = dve.scalar_tensor_tensor(neg_l_t[:, u, :], bank[b + 1][:, cols], column(S_U, u),
                                                    tmp[:, h % 2, cols], ALU.mult, ALU.mult)
                step.then_inc(sem("triangled"), 1)

            def triangles(first):
                for h0 in (first, first + 2):
                    for h in (h0, h0 + 1):
                        b = (0 if h < 4 else 4) + 2 * (h % 2)
                        dve.wait_ge(sem("tri_rows"), h + 1)
                        shifted(h, b).then_inc(sem("tri_shifted"), 1)
                    for h in (h0, h0 + 1):
                        triangle(h)

            def shift_row(h):
                dve.wait_ge(sem("row_made"), h + 1)
                if h >= 2:
                    dve.wait_ge(sem("unit_scaled"), h - 1)
                shifted(h, (0 if h < 4 else 4) + h % 2).then_inc(sem("row_shifted"), 1)

            def scale_products(first, last):
                shift_row(first)
                for h in range(first, last):
                    if h + 1 < last:
                        shift_row(h + 1)
                    dve.wait_ge(sem("unit_prods"), h + 1)
                    dve.wait_ge(sem("decay_made"), h + 1)
                    for n in range(TT):
                        u = h * TT + n
                        cols = slice(n * P, (n + 1) * P)
                        step = dve.scalar_tensor_tensor(attn[:, u, :], bank[2 + h % 2][:, cols], column(R_K, u),
                                                        tmp[:, h % 2, cols], ALU.mult, ALU.mult)
                    step.then_inc(sem("unit_scaled"), 1)

            def quarter(i):
                return slice(i * BLOCK, (i + 1) * BLOCK)

            def take_blocks():
                dve.wait_ge(sem("triangled"), GH)
                dve.memset(block_x[:, :, :], 0.0)
                for i in range(P // BLOCK):
                    step = dve.transpose(block_l[quarter(i), :, :],
                                         neg_l_t[quarter(i), :, quarter(i)].rearrange("s u c -> s c u"))
                link(step)
                flat = block_x[:, :, :].rearrange("p r c -> p (r c)")
                link(dve.memset(flat[:, 0:BLOCK * BLOCK:BLOCK + 1], 1.0))

            def block_rows(first, last):
                for r in range(first, last):
                    prod = tmp[:, 2:4, :].rearrange("p a n -> p (a n)")[:, 0:r * r].rearrange("p (c s) -> p c s", c=r)
                    link(dve.tensor_tensor(prod, block_x[:, 0:r, 0:r].rearrange("p s c -> p c s"),
                                           block_l[:, r:r + 1, 0:r].broadcast_to([P, r, r]), ALU.mult))
                    link(dve.tensor_reduce(block_x[:, r, 0:r], prod, AX.X, ALU.add))

            dve.wait_ge(sem("small_out"), 2)
            convolve(0)
            columns_after()
            convolve(1)
            g_sums()
            k_columns()
            convolve(2)
            triangles(0)
            convolve(3)
            triangles(4)
            convolve(4)
            take_blocks()
            block_rows(1, 14)
            convolve(5)
            block_rows(14, BLOCK)
            dve.sem_inc(sem("blocks_done"), 1)
            q_columns()
            scale_products(0, 4)
            dve.wait_ge(bank_full, 4 * GDN_OUT[0])
            dve.memset(inv_t[:, UNITS // 2:UNITS, :], 0.0).then_inc(sem("inv_cleared"), 1)
            dve.wait_ge(sem("inv_cleared"), 2)
            for i in range(P // BLOCK):
                dve.transpose(inv_t[quarter(i), :, quarter(i)].rearrange("b u c -> b c u"), block_x[quarter(i), :, :])\
                    .then_inc(sem("inv_seeded"), 1)
            dve.wait_ge(sem("inv_seeded"), P // BLOCK)

            scale_products(4, GH)
            dve.wait_ge(sem("join_cast"), 1)

            n_joined = 0
            for batch in range(2):
                heads = range(4 * batch, 4 * batch + 4)
                for level in range(len(LEVELS)):
                    for r, h in enumerate(heads):
                        n_joined += 1
                        dve.wait_ge(sem("seconds_made"), n_joined)
                        dve.copy_predicated(inv_t[:, h * TT:(h + 1) * TT, :],
                                            join[:, level:level + 1, :].broadcast_to([P, TT, P]),
                                            tall(bank[4 + r])).then_inc(sem("joined"), 1)
                        if level == len(LEVELS) - 1:
                            k = gk[:, h, :].rearrange("p (n e) -> p n e", n=TT)
                            cs = slice(h * TT, (h + 1) * TT)
                            dve.wait_ge(sem("k_turned_out"), GH)
                            dve.tensor_tensor(k_grown[:, 4 * r:4 * r + 4, :], k, over(col[:, EXP_G, cs]), ALU.mult)\
                                .then_inc(sem("k_grown"), 1)
            outs = gv[:, :, :].rearrange("p h (n e) -> p h n e", n=TT)
            per_unit = [col[:, c, :].rearrange("p (h n) -> p h n", n=TT) for c in range(13)]

            def some(c, q, n):
                return per_unit[c][:, 4 * q:4 * q + 4, n:n + 1].broadcast_to([P, 4, P])

            def sum_outputs(n):
                dve.wait_ge(sem("o_squared"), n + 1)
                dve.tensor_reduce(on[:, n, 0, :], o_sq[:, :, :], AX.X, ALU.add).then_inc(sem("o_summed"), 1)

            def outputs(n):
                dve.wait_ge(sem("o_rooted"), n + 1)
                link(inv_root(on[:, n, 0, :], on[:, n, 1, :], lambda t: on[:, n, 2 + t, :], on[:, n, 5, :], 1.0 / P))
                dve.wait_ge(sem("o_gated"), n + 1)
                z = gz[:, n, :].rearrange("p (h e) -> p h e", h=GH)
                dve.tensor_tensor(z, z, over(on[:, n, 5, :]), ALU.mult).then_inc(sem("o_scaled"), 1)

            def low_out(n):
                for half in range(2):
                    dve.wait_ge(sem("o_high"), 2 * n + half + 1)
                    where = (slice(None), slice(4 * half, 4 * half + 4), slice(n * P, (n + 1) * P))
                    dve.tensor_tensor(go_lo[where], tall(bank[6 + half]), go_hi[where].bitcast(F32), ALU.subtract)\
                        .then_inc(sem("o_low"), 1)

            for n in range(TT):
                for q in range(2):
                    hs = slice(4 * q, 4 * q + 4)
                    dve.wait_ge(sem("v_new_full"), 2 * n + q + 1)
                    if n:
                        dve.wait_ge(sem("state_full"), 2 * (n - 1) + q + 1)
                        dve.wait_ge(sem("o_full"), 2 * (n - 1) + q + 1)
                    dve.tensor_tensor(v_new[:, hs, :], tall(bank[q]), some(S_V, q, n), ALU.mult)\
                        .then_inc(sem("v_new_made"), 1)
                if n:
                    sum_outputs(n - 1)
                if n == TT - 1:
                    low_out(n - 2)
                    outputs(n - 1)
                for q in range(2):
                    hs = slice(4 * q, 4 * q + 4)
                    if n < TT - 1:
                        dve.wait_ge(sem("state_full"), 2 * n + q + 1)
                        if n == 0:
                            dve.tensor_copy(states[0][:, hs, :], tall(bank[4 + q])).then_inc(sem("state_made"), 1)
                        else:
                            dve.wait_ge(sem("o_full"), 2 * (n - 1) + q + 1)
                            dve.wait_ge(sem("state_made"), 2 * (n - 1) + q + 1)
                            for r in range(4):
                                h = 4 * q + r
                                step = dve.scalar_tensor_tensor(states[n % 2][:, h, :], states[(n - 1) % 2][:, h, :],
                                                                column(EXP_TOT, h * TT + n),
                                                                bank[4 + q][:, r * P:(r + 1) * P], ALU.mult, ALU.add)
                            step.then_inc(sem("state_made"), 1)
                    dve.wait_ge(sem("o_full"), 2 * n + q + 1)
                    dve.tensor_tensor(outs[:, hs, n, :], tall(bank[2 + q]), some(R_Q, q, n), ALU.mult)\
                        .then_inc(sem("o_out"), 1)
                if 0 < n < TT - 1:
                    outputs(n - 1)
                if n == TT - 2:
                    low_out(n - 2)
            sum_outputs(TT - 1)
            outputs(TT - 1)
            low_out(TT - 2)
            low_out(TT - 1)
            first_half(3, False)
            norms(3)
            mlp(1)


_INS = ["x", "norm_gains", "ret_w_in", "ret_gn_gain", "ret_w_out", "gdn_w_in", "gdn_conv_w", "gdn_a_log",
        "gdn_dt_bias", "gdn_norm_gain", "gdn_w_out", "mlp_w_up", "mlp_w_down"]


def kernel(**inputs):
    import concourse.bacc as bacc
    from concourse.bass_utils import run_bass_kernel_spmd

    nc = bacc.Bacc("TRN2", target_bir_lowering=False, num_devices=1)
    arrays, args = {}, []
    given = {name: np.ascontiguousarray(inputs[name]) for name in _INS}
    for name, a in {**given, **shape_constants()}.items():
        arrays[f"in_{name}_dram"] = a
        args.append(nc.dram_tensor(f"in_{name}_dram", a.shape, mybir.dt.from_np(a.dtype), kind="ExternalInput").ap())
    out = nc.dram_tensor("out_dram", (1, T, D), F32, kind="ExternalOutput").ap()
    hybrid_trunk(nc, *args, out)
    result = run_bass_kernel_spmd(nc, [arrays], core_ids=[0])
    return result.results[0]["out_dram"]
```
